# Optimizing a Trainium2 kernel written in Bass

```python
import math
import jax, jax.numpy as jnp
from jax import lax
import numpy as np

D_MODEL = 1024
BATCH = 1
SEQ = 512
DEPTH = 2

ATT_HEADS = 8
ATT_KV_GROUPS = 2
ATT_HPG = ATT_HEADS // ATT_KV_GROUPS
HEAD_DIM = 64
D_ATT = ATT_HEADS * HEAD_DIM
D_KV = ATT_KV_GROUPS * HEAD_DIM
N_BRANCH = 3
CMP_LEN = 32
CMP_STRIDE = 16
CMP_HIDDEN = 256
SLC_BLOCK = 64
SLC_TOPN = 16
WINDOW = 512
Q_BLOCK = 128
SEL_FORCE = 1.0e4
REL_BUCKETS = 32
REL_MAX_DIST = 128
GMLP_GROUPS = 4
GMLP_GROUP_DIM = 64
D_GMLP = GMLP_GROUPS * GMLP_GROUP_DIM
GMLP_CHUNK = 128
SSM_HEADS = 4
SSM_HEAD_DIM = 64
D_SSM = SSM_HEADS * SSM_HEAD_DIM
SSM_GROUPS = 2
SSM_STATE = 128
SSM_CONV = 4
SSM_CHUNK = 256
D_XBC = D_SSM + 2 * SSM_GROUPS * SSM_STATE
D_MIX = D_ATT + D_GMLP + D_SSM
D_ATT_IN = D_ATT + 6 * D_KV + ATT_HEADS * N_BRANCH
D_GMLP_IN = 2 * D_GMLP
D_SSM_IN = D_SSM + D_XBC + SSM_HEADS
D_IN = D_ATT_IN + D_GMLP_IN + D_SSM_IN
D_FF = 2816
N_SUB = 3
ALPHA = (2 * DEPTH) ** 0.25
BETA = (8 * DEPTH) ** -0.25
LN_EPS = 1e-5


def layer_norm(x, g, b):
    xf = x.astype(jnp.float32)
    mu = xf.mean(-1, keepdims=True)
    var = jnp.square(xf - mu).mean(-1, keepdims=True)
    return ((xf - mu) * lax.rsqrt(var + LN_EPS)).astype(x.dtype) * g + b

def swiglu(h, w1, w3, w2):
    return (jax.nn.silu(h @ w1) * (h @ w3)) @ w2

def masked_softmax(s, mask):
    s = jnp.where(mask, s.astype(jnp.float32), -jnp.inf)
    m = jnp.max(s, axis=-1, keepdims=True)
    m = jnp.where(jnp.isfinite(m), m, 0.0)
    p = jnp.exp(s - m)
    return p / jnp.maximum(p.sum(-1, keepdims=True), 1e-30)

def rel_bucket(dist):
    n = jnp.maximum(dist, 0)
    max_exact = REL_BUCKETS // 2
    nf = jnp.maximum(n, 1).astype(jnp.float32)
    large = max_exact + (jnp.log(nf / max_exact) / math.log(REL_MAX_DIST / max_exact)
                         * (REL_BUCKETS - max_exact)).astype(jnp.int32)
    large = jnp.minimum(large, REL_BUCKETS - 1)
    return jnp.where(n < max_exact, n, large)

def nsa_attention(q, k_cmp, v_cmp, k_slc, v_slc, k_win, v_win, gates, rel_bias,
                  cmp_pe, cmp_w1, cmp_b1, cmp_w2):
    Bn, T = q.shape[:2]
    G, I, Dh = ATT_KV_GROUPS, ATT_HPG, HEAD_DIM
    n_cmp = (T - CMP_LEN) // CMP_STRIDE + 1
    n_slc = T // SLC_BLOCK
    n_qb = T // Q_BLOCK
    top_n = min(SLC_TOPN, n_slc)
    kw_len = Q_BLOCK + WINDOW

    cmp_start = np.arange(n_cmp) * CMP_STRIDE
    blk_idx = cmp_start[:, None] + np.arange(CMP_LEN)[None, :]

    def compress(kv, j):
        blocks = kv[:, blk_idx] + cmp_pe[j][None, None, :, None, :]
        blocks = blocks.transpose(0, 3, 1, 2, 4).reshape(Bn, G, n_cmp, CMP_LEN * Dh)
        return jax.nn.gelu(blocks @ cmp_w1[j] + cmp_b1[j]) @ cmp_w2[j]

    kc, vc = compress(k_cmp, 0), compress(v_cmp, 1)
    cmp_end = jnp.asarray(cmp_start + CMP_LEN - 1, jnp.int32)
    slc_start = np.arange(n_slc) * SLC_BLOCK
    overlap = np.clip(np.minimum(cmp_start[:, None] + CMP_LEN, slc_start[None, :] + SLC_BLOCK)
                      - np.maximum(cmp_start[:, None], slc_start[None, :]), 0, None)
    overlap = jnp.asarray(overlap / CMP_LEN, jnp.float32)

    ks = k_slc.transpose(0, 2, 1, 3).reshape(Bn, G, n_slc, SLC_BLOCK, Dh)
    vs = v_slc.transpose(0, 2, 1, 3).reshape(Bn, G, n_slc, SLC_BLOCK, Dh)
    pad_w = ((0, 0), (0, 0), (WINDOW, 0), (0, 0))
    kw = jnp.pad(k_win.transpose(0, 2, 1, 3), pad_w)
    vw = jnp.pad(v_win.transpose(0, 2, 1, 3), pad_w)

    win_dist = np.arange(Q_BLOCK)[:, None] + WINDOW - np.arange(kw_len)[None, :]
    win_mask = jnp.asarray((win_dist >= 0) & (win_dist < WINDOW))
    win_bias = rel_bias[rel_bucket(jnp.asarray(win_dist, jnp.int32))]
    win_bias = win_bias.reshape(Q_BLOCK, kw_len, G, I).transpose(2, 3, 0, 1)
    rb = rel_bias.reshape(REL_BUCKETS, G, I)
    gather_blocks = jax.vmap(jax.vmap(lambda kb, s: kb[s]))
    bias_by_group = jax.vmap(lambda tb, bk: tb[bk], in_axes=(1, 1), out_axes=1)

    qb_all = q.reshape(Bn, n_qb, Q_BLOCK, G, I, Dh).transpose(1, 0, 3, 4, 2, 5) * (Dh ** -0.5)
    gb_all = gates.reshape(Bn, n_qb, Q_BLOCK, G, I, N_BRANCH).transpose(1, 0, 3, 4, 2, 5)

    def block(args):
        b_idx, qb, gb = args
        start = b_idx * Q_BLOCK
        t = start + jnp.arange(Q_BLOCK, dtype=jnp.int32)
        dist_c = t[:, None] - cmp_end[None, :]
        bias_c = rel_bias[rel_bucket(dist_c)].reshape(Q_BLOCK, n_cmp, G, I).transpose(2, 3, 0, 1)
        p_c = masked_softmax(jnp.einsum('bgiqd,bgkd->bgiqk', qb, kc) + bias_c, dist_c >= 0)
        o_c = jnp.einsum('bgiqk,bgkd->bgiqd', p_c.astype(vc.dtype), vc)
        imp = jnp.einsum('bgiqk,kn->bgqn', p_c, overlap)
        cur = (t // SLC_BLOCK)[:, None]
        blk = jnp.arange(n_slc, dtype=jnp.int32)[None, :]
        forced = (blk == 0) | (blk == cur) | (blk == cur - 1)
        imp = jnp.where(forced, SEL_FORCE, jnp.where(blk <= cur, imp, -SEL_FORCE))
        _, sel = lax.top_k(imp, top_n)
        k_sel = gather_blocks(ks, sel).reshape(Bn, G, Q_BLOCK, top_n * SLC_BLOCK, Dh)
        v_sel = gather_blocks(vs, sel).reshape(Bn, G, Q_BLOCK, top_n * SLC_BLOCK, Dh)
        pos_sel = (sel[..., None] * SLC_BLOCK + jnp.arange(SLC_BLOCK, dtype=jnp.int32)
                   ).reshape(Bn, G, Q_BLOCK, top_n * SLC_BLOCK)
        dist_s = t[None, None, :, None] - pos_sel
        bias_s = bias_by_group(rb, rel_bucket(dist_s)).transpose(0, 1, 4, 2, 3)
        p_s = masked_softmax(jnp.einsum('bgiqd,bgqkd->bgiqk', qb, k_sel) + bias_s,
                             (dist_s >= 0)[:, :, None])
        o_s = jnp.einsum('bgiqk,bgqkd->bgiqd', p_s.astype(v_sel.dtype), v_sel)
        kb = lax.dynamic_slice_in_dim(kw, start, kw_len, axis=2)
        vb = lax.dynamic_slice_in_dim(vw, start, kw_len, axis=2)
        pos_w = start - WINDOW + jnp.arange(kw_len, dtype=jnp.int32)
        p_w = masked_softmax(jnp.einsum('bgiqd,bgkd->bgiqk', qb, kb) + win_bias,
                             win_mask & (pos_w >= 0)[None, :])
        o_w = jnp.einsum('bgiqk,bgkd->bgiqd', p_w.astype(vb.dtype), vb)
        return gb[..., 0:1] * o_c + gb[..., 1:2] * o_s + gb[..., 2:3] * o_w

    o = lax.map(block, (jnp.arange(n_qb, dtype=jnp.int32), qb_all, gb_all))
    return o.transpose(1, 0, 4, 2, 3, 5).reshape(Bn, T, ATT_HEADS * Dh)

def gmlp_spatial_gating(uv, ln_g, ln_b, ws, bs):
    Bn, T, _ = uv.shape
    u, v = jnp.split(jax.nn.gelu(uv), 2, axis=-1)
    v = layer_norm(v, ln_g, ln_b)
    v = v.reshape(Bn, T // GMLP_CHUNK, GMLP_CHUNK, GMLP_GROUPS, GMLP_GROUP_DIM)
    causal = jnp.tril(jnp.ones((GMLP_CHUNK, GMLP_CHUNK), dtype=bool))
    w = jnp.where(causal[None], ws, 0.0)
    sv = jnp.einsum('gts,bcsgd->bctgd', w, v) + bs.T[None, None, :, :, None]
    return u * sv.reshape(Bn, T, D_GMLP)

def segsum(a):
    L = a.shape[-1]
    cs = jnp.cumsum(a, axis=-1)
    mask = jnp.tril(jnp.ones((L, L), dtype=bool))
    return jnp.where(mask, cs[..., :, None] - cs[..., None, :], -jnp.inf)

def ssd_chunked(X, A, Bh, Ch):
    Bn, T, H, P = X.shape
    nc = -(-T // SSM_CHUNK)
    pad = nc * SSM_CHUNK - T
    def chunk(a):
        a = jnp.pad(a, [(0, 0), (0, pad)] + [(0, 0)] * (a.ndim - 2))
        return a.reshape(Bn, nc, SSM_CHUNK, *a.shape[2:])
    X, A, Bh, Ch = chunk(X), chunk(A), chunk(Bh), chunk(Ch)
    A = A.transpose(0, 3, 1, 2)
    A_cs = jnp.cumsum(A, axis=-1)
    Lmat = jnp.exp(segsum(A))
    scores = jnp.einsum('bclhn,bcshn->bhcls', Ch, Bh) * Lmat
    y_diag = jnp.einsum('bhcls,bcshp->bclhp', scores, X)
    decay = jnp.exp(A_cs[..., -1:] - A_cs)
    states = jnp.einsum('bclhn,bhcl,bclhp->bchpn', Bh, decay, X)
    chunk_decay = jnp.exp(A_cs[..., -1])

    def step(h, inp):
        s_c, dec = inp
        return dec[:, :, None, None] * h + s_c, h

    h0 = jnp.zeros((Bn, H, P, Bh.shape[-1]), X.dtype)
    _, prev = lax.scan(step, h0, (states.transpose(1, 0, 2, 3, 4), chunk_decay.transpose(2, 0, 1)))
    prev = prev.transpose(1, 0, 2, 3, 4)
    y_off = jnp.einsum('bclhn,bchpn,bhcl->bclhp', Ch, prev, jnp.exp(A_cs))
    return (y_diag + y_off).reshape(Bn, nc * SSM_CHUNK, H, P)[:, :T]

def mamba2_ssd(zxbcdt, conv_w, conv_b, dt_bias, a_log, d_skip, norm_g):
    Bn, T, _ = zxbcdt.shape
    z, xbc, dt = jnp.split(zxbcdt, [D_SSM, D_SSM + D_XBC], axis=-1)
    xbc = lax.conv_general_dilated(xbc, conv_w[:, None, :], window_strides=(1,),
                                   padding=[(SSM_CONV - 1, 0)],
                                   dimension_numbers=('NWC', 'WIO', 'NWC'),
                                   feature_group_count=D_XBC) + conv_b
    xbc = jax.nn.silu(xbc)
    xs, Bm, Cm = jnp.split(xbc, [D_SSM, D_SSM + SSM_GROUPS * SSM_STATE], axis=-1)
    dt = jax.nn.softplus((dt + dt_bias).astype(jnp.float32))
    A = -jnp.exp(a_log.astype(jnp.float32))
    X = xs.reshape(Bn, T, SSM_HEADS, SSM_HEAD_DIM)
    rep = SSM_HEADS // SSM_GROUPS
    Bh = jnp.repeat(Bm.reshape(Bn, T, SSM_GROUPS, SSM_STATE), rep, axis=2).astype(jnp.float32)
    Ch = jnp.repeat(Cm.reshape(Bn, T, SSM_GROUPS, SSM_STATE), rep, axis=2).astype(jnp.float32)
    y = ssd_chunked(X.astype(jnp.float32) * dt[..., None], A * dt, Bh, Ch)
    y = y + X.astype(jnp.float32) * d_skip.astype(jnp.float32)[:, None]
    g = (y.reshape(Bn, T, D_SSM) * jax.nn.silu(z.astype(jnp.float32))).reshape(Bn, T, SSM_GROUPS, -1)
    g = g * lax.rsqrt(jnp.mean(jnp.square(g), axis=-1, keepdims=True) + LN_EPS)
    return g.reshape(Bn, T, D_SSM).astype(zxbcdt.dtype) * norm_g

def hybrid_mixer(h, rel_bias, w_in, w_out, cmp_pe, cmp_w1, cmp_b1, cmp_w2,
                 gmlp_ln_g, gmlp_ln_b, gmlp_ws, gmlp_bs,
                 conv_w, conv_b, dt_bias, a_log, d_skip, norm_g):
    Bn, T, _ = h.shape
    proj = h @ w_in
    att_in, gmlp_in, ssm_in = jnp.split(proj, [D_ATT_IN, D_ATT_IN + D_GMLP_IN], axis=-1)
    cuts = [D_ATT + i * D_KV for i in range(7)]
    q, kc, vc, ks, vs, kw, vw, g = jnp.split(att_in, cuts, axis=-1)
    kvr = lambda a: a.reshape(Bn, T, ATT_KV_GROUPS, HEAD_DIM)
    gates = jax.nn.sigmoid(g).reshape(Bn, T, ATT_HEADS, N_BRANCH)
    o_att = nsa_attention(q.reshape(Bn, T, ATT_HEADS, HEAD_DIM), kvr(kc), kvr(vc), kvr(ks), kvr(vs),
                          kvr(kw), kvr(vw), gates, rel_bias, cmp_pe, cmp_w1, cmp_b1, cmp_w2)
    o_gmlp = gmlp_spatial_gating(gmlp_in, gmlp_ln_g, gmlp_ln_b, gmlp_ws, gmlp_bs)
    o_ssm = mamba2_ssd(ssm_in, conv_w, conv_b, dt_bias, a_log, d_skip, norm_g)
    return jnp.concatenate([o_att, o_gmlp, o_ssm], axis=-1) @ w_out

def post_norm_residual(x, y, gate, weight, g, b):
    return layer_norm(ALPHA * x + weight * (1.0 + gate) * y, g, b)

def first_inputs(seed: int = 0) -> dict:
    key = jax.random.key(seed)
    k = jax.random.split(key, 30)
    nrm = lambda kk, shape, s: jax.random.normal(kk, shape, jnp.float32) * s
    L = DEPTH
    dt_init = jnp.exp(jax.random.uniform(k[25], (L, SSM_HEADS), jnp.float32,
                                         math.log(1e-3), math.log(1e-1)))
    return {
        "x": nrm(k[0], (BATCH, SEQ, D_MODEL), 1.0),
        "c": nrm(k[1], (BATCH, D_MODEL), 1.0),
        "rel_bias": nrm(k[2], (REL_BUCKETS, ATT_HEADS), 0.5),
        "ada_w": nrm(k[3], (L, D_MODEL, N_SUB * 3 * D_MODEL), 0.5 * D_MODEL ** -0.5),
        "ada_b": nrm(k[4], (L, N_SUB * 3 * D_MODEL), 0.02),
        "ln_g": 1.0 + nrm(k[5], (L, N_SUB, D_MODEL), 0.02),
        "ln_b": nrm(k[6], (L, N_SUB, D_MODEL), 0.02),
        "ffn_w1": nrm(k[7], (L, 2, D_MODEL, D_FF), BETA * D_MODEL ** -0.5),
        "ffn_w3": nrm(k[8], (L, 2, D_MODEL, D_FF), BETA * D_MODEL ** -0.5),
        "ffn_w2": nrm(k[9], (L, 2, D_FF, D_MODEL), BETA * D_FF ** -0.5),
        "w_in": nrm(k[10], (L, D_MODEL, D_IN), D_MODEL ** -0.5),
        "w_out": nrm(k[11], (L, D_MIX, D_MODEL), BETA * D_MIX ** -0.5),
        "cmp_pe": nrm(k[12], (L, 2, CMP_LEN, HEAD_DIM), 0.1),
        "cmp_w1": nrm(k[13], (L, 2, CMP_LEN * HEAD_DIM, CMP_HIDDEN), (CMP_LEN * HEAD_DIM) ** -0.5),
        "cmp_b1": nrm(k[14], (L, 2, CMP_HIDDEN), 0.02),
        "cmp_w2": nrm(k[15], (L, 2, CMP_HIDDEN, HEAD_DIM), 1.5 * CMP_HIDDEN ** -0.5),
        "gmlp_ln_g": 1.0 + nrm(k[16], (L, D_GMLP), 0.02),
        "gmlp_ln_b": nrm(k[17], (L, D_GMLP), 0.02),
        "gmlp_ws": nrm(k[18], (L, GMLP_GROUPS, GMLP_CHUNK, GMLP_CHUNK), GMLP_CHUNK ** -0.5),
        "gmlp_bs": 1.0 + nrm(k[19], (L, GMLP_GROUPS, GMLP_CHUNK), 0.02),
        "ssm_conv_w": nrm(k[20], (L, SSM_CONV, D_XBC), SSM_CONV ** -0.5),
        "ssm_conv_b": nrm(k[21], (L, D_XBC), 0.02),
        "ssm_dt_bias": dt_init + jnp.log(-jnp.expm1(-dt_init)),
        "ssm_a_log": jnp.log(jax.random.uniform(k[22], (L, SSM_HEADS), jnp.float32, 1.0, 16.0)),
        "ssm_d": 1.0 + nrm(k[23], (L, SSM_HEADS), 0.02),
        "ssm_norm_g": 1.0 + nrm(k[24], (L, D_SSM), 0.02),
    }

def first_block(x, c, rel_bias, ada_w, ada_b, ln_g, ln_b, ffn_w1, ffn_w3, ffn_w2, w_in, w_out,
              cmp_pe, cmp_w1, cmp_b1, cmp_w2, gmlp_ln_g, gmlp_ln_b, gmlp_ws, gmlp_bs,
              ssm_conv_w, ssm_conv_b, ssm_dt_bias, ssm_a_log, ssm_d, ssm_norm_g):
    Bn = x.shape[0]
    for l in range(DEPTH):
        mod = (jax.nn.silu(c) @ ada_w[l] + ada_b[l]).reshape(Bn, N_SUB, 3, D_MODEL)
        shift, scale, gate = mod[:, :, 0, None], mod[:, :, 1, None], mod[:, :, 2, None]
        h = x * (1.0 + scale[:, 0]) + shift[:, 0]
        y = swiglu(h, ffn_w1[l, 0], ffn_w3[l, 0], ffn_w2[l, 0])
        x = post_norm_residual(x, y, gate[:, 0], 0.5, ln_g[l, 0], ln_b[l, 0])
        h = x * (1.0 + scale[:, 1]) + shift[:, 1]
        y = hybrid_mixer(h, rel_bias, w_in[l], w_out[l], cmp_pe[l], cmp_w1[l], cmp_b1[l], cmp_w2[l],
                         gmlp_ln_g[l], gmlp_ln_b[l], gmlp_ws[l], gmlp_bs[l],
                         ssm_conv_w[l], ssm_conv_b[l], ssm_dt_bias[l], ssm_a_log[l], ssm_d[l],
                         ssm_norm_g[l])
        x = post_norm_residual(x, y, gate[:, 1], 1.0, ln_g[l, 1], ln_b[l, 1])
        h = x * (1.0 + scale[:, 2]) + shift[:, 2]
        y = swiglu(h, ffn_w1[l, 1], ffn_w3[l, 1], ffn_w2[l, 1])
        x = post_norm_residual(x, y, gate[:, 2], 0.5, ln_g[l, 2], ln_b[l, 2])
    return x


_first_inputs = first_inputs


def first_inputs(seed=0):
    import zlib

    import numpy as np

    out = dict(_first_inputs(seed))
    spreads = {}
    factors = {'ada_b': 3.363,
     'cmp_pe': 3.236,
     'cmp_b1': 8.0,
     'gmlp_ln_g': 8.0,
     'gmlp_ln_b': 8.0,
     'gmlp_bs': 8.0,
     'ssm_conv_b': 7.623,
     'ssm_d': 8.0,
     'ssm_norm_g': 8.0}
    for name, (base, spread) in spreads.items():
        noise = np.random.default_rng([zlib.crc32(name.encode()), seed]).standard_normal(out[name].shape)
        drawn = base * np.exp(spread * noise) if base else spread * noise
        out[name] = __import__('jax').numpy.asarray(drawn.astype(out[name].dtype))
    for name, factor in factors.items():
        out[name] = (out[name] * factor).astype(out[name].dtype)
    return out


_narrow_inputs = first_inputs


def first_inputs(seed=0):
    out = dict(_narrow_inputs(seed))
    wider = {'rel_bias': 3.89,
     'cmp_b1': 4.15,
     'gmlp_ln_g': 5.78,
     'gmlp_ln_b': 6.32,
     'gmlp_bs': 4.23,
     'ssm_d': 3.42,
     'ssm_norm_g': 3.37}
    for name, times in wider.items():
        mean = out[name].mean()
        out[name] = (mean + times * (out[name] - mean)).astype(out[name].dtype)
    return out


D_MIX_2 = D_MODEL
DN_HEADS = 4
DN_HEAD_DIM = 128
DN_WIDTH = DN_HEADS * DN_HEAD_DIM
DN_CONV = 4
CHUNK = 64
SC_WIDTH = D_MIX_2 - DN_WIDTH
SC_GROUPS = 4
SC_GROUP_DIM = SC_WIDTH // SC_GROUPS
SC_CONV = 3
D_FF_2 = ((8 * D_MODEL + 3 * 256 - 1) // (3 * 256)) * 256
W_IN_COLS = 4 * DN_WIDTH + 2 * DN_HEADS + 3 * SC_WIDTH
EPS = 1e-6


def rms_norm(x, gain):
    xf = x.astype(jnp.float32)
    y = xf * lax.rsqrt(jnp.mean(xf * xf, axis=-1, keepdims=True) + EPS)
    return (y * gain.astype(jnp.float32)).astype(x.dtype)

def l2_normalize(x):
    return x * lax.rsqrt(jnp.sum(x * x, axis=-1, keepdims=True) + EPS)

def causal_depthwise_conv(x, w):
    K = w.shape[0]
    T = x.shape[1]
    xp = jnp.pad(x, ((0, 0), (K - 1, 0), (0, 0)))
    y = xp[:, 0:T, :] * w[0]
    for j in range(1, K):
        y = y + xp[:, j:j + T, :] * w[j]
    return y

def chunk_gated_delta_rule(q, k, v, g, beta):
    Bsz, T, H, DK = q.shape
    DV = v.shape[-1]
    C = CHUNK
    N = T // C
    q = q * (DK ** -0.5)

    def to_chunks(t):
        return t.reshape(Bsz, N, C, H, t.shape[-1]).transpose(0, 3, 1, 2, 4)

    q, k, v = to_chunks(q), to_chunks(k), to_chunks(v)
    g = jnp.cumsum(g.reshape(Bsz, N, C, H).transpose(0, 3, 1, 2), axis=-1)
    beta = beta.reshape(Bsz, N, C, H).transpose(0, 3, 1, 2)

    causal = jnp.tril(jnp.ones((C, C), dtype=bool))
    strict = jnp.tril(jnp.ones((C, C), dtype=bool), -1)
    decay = jnp.exp(jnp.where(causal, g[..., :, None] - g[..., None, :], -jnp.inf))

    k_beta = k * beta[..., None]
    v_beta = v * beta[..., None]
    lower = jnp.where(strict, jnp.einsum('bhncd,bhnmd->bhncm', k_beta, k) * decay, 0.0)
    a_mat = lower + jnp.eye(C, dtype=jnp.float32)
    rhs = jnp.concatenate([v_beta, k_beta * jnp.exp(g)[..., None]], axis=-1)
    sol = lax.linalg.triangular_solve(a_mat, rhs, left_side=True, lower=True, unit_diagonal=True)
    u, w = sol[..., :DV], sol[..., DV:]

    qk = jnp.einsum('bhncd,bhnmd->bhncm', q, k) * decay
    q_dec = q * jnp.exp(g)[..., None]
    k_dec = k * jnp.exp(g[..., -1:] - g)[..., None]
    g_last = jnp.exp(g[..., -1])

    def step(S, xs):
        qk_i, q_dec_i, k_dec_i, u_i, w_i, gl_i = xs
        v_new = u_i - jnp.einsum('bhck,bhkv->bhcv', w_i, S)
        o_i = jnp.einsum('bhck,bhkv->bhcv', q_dec_i, S) + jnp.einsum('bhcm,bhmv->bhcv', qk_i, v_new)
        S = S * gl_i[..., None, None] + jnp.einsum('bhck,bhcv->bhkv', k_dec_i, v_new)
        return S, o_i

    xs = (jnp.moveaxis(qk, 2, 0), jnp.moveaxis(q_dec, 2, 0), jnp.moveaxis(k_dec, 2, 0),
          jnp.moveaxis(u, 2, 0), jnp.moveaxis(w, 2, 0), jnp.moveaxis(g_last, 2, 0))
    S0 = jnp.zeros((Bsz, H, DK, DV), dtype=jnp.float32)
    _, o = lax.scan(step, S0, xs)
    return o.transpose(1, 0, 3, 2, 4).reshape(Bsz, T, H, DV)

def hybrid_layer(x, norm1_g, w_in, dn_conv_w, dn_a_log, dn_dt_bias, dn_norm_g,
                 sc_conv_w, sc_norm_g, w_out, norm2_g, ffn_w_gate, ffn_w_up, ffn_w_down):
    Bsz, T, _ = x.shape
    h = rms_norm(x, norm1_g)
    proj = h @ w_in
    o1 = 3 * DN_WIDTH
    o2 = o1 + DN_WIDTH
    o3 = o2 + DN_HEADS
    o4 = o3 + DN_HEADS
    qkv, z, b_in, a_in, sc_in = proj[..., :o1], proj[..., o1:o2], proj[..., o2:o3], proj[..., o3:o4], proj[..., o4:]

    qkv = jax.nn.silu(causal_depthwise_conv(qkv, dn_conv_w)).astype(jnp.float32)
    q = l2_normalize(qkv[..., :DN_WIDTH].reshape(Bsz, T, DN_HEADS, DN_HEAD_DIM))
    k = l2_normalize(qkv[..., DN_WIDTH:2 * DN_WIDTH].reshape(Bsz, T, DN_HEADS, DN_HEAD_DIM))
    v = qkv[..., 2 * DN_WIDTH:].reshape(Bsz, T, DN_HEADS, DN_HEAD_DIM)
    beta = jax.nn.sigmoid(b_in.astype(jnp.float32))
    g = -jnp.exp(dn_a_log.astype(jnp.float32)) * jax.nn.softplus(
        a_in.astype(jnp.float32) + dn_dt_bias.astype(jnp.float32))
    o_dn = chunk_gated_delta_rule(q, k, v, g, beta)
    zf = z.astype(jnp.float32).reshape(Bsz, T, DN_HEADS, DN_HEAD_DIM)
    o_dn = (o_dn * lax.rsqrt(jnp.mean(o_dn * o_dn, axis=-1, keepdims=True) + EPS)
            * dn_norm_g.astype(jnp.float32) * jax.nn.silu(zf))
    o_dn = o_dn.reshape(Bsz, T, DN_WIDTH).astype(x.dtype)

    gate_b, gate_c, hv = sc_in[..., :SC_WIDTH], sc_in[..., SC_WIDTH:2 * SC_WIDTH], sc_in[..., 2 * SC_WIDTH:]
    y = gate_b * causal_depthwise_conv(gate_c * hv, sc_conv_w)
    yf = y.astype(jnp.float32).reshape(Bsz, T, SC_GROUPS, SC_GROUP_DIM)
    yf = yf * lax.rsqrt(jnp.mean(yf * yf, axis=-1, keepdims=True) + EPS)
    o_sc = (yf * sc_norm_g.astype(jnp.float32).reshape(SC_GROUPS, SC_GROUP_DIM)).reshape(Bsz, T, SC_WIDTH).astype(x.dtype)

    x = x + jnp.concatenate([o_dn, o_sc], axis=-1) @ w_out

    h2 = rms_norm(x, norm2_g)
    x = x + (jax.nn.silu(h2 @ ffn_w_gate) * (h2 @ ffn_w_up)) @ ffn_w_down
    return x

def second_inputs(seed: int = 0) -> dict:
    key = jax.random.key(seed)
    ks = jax.random.split(key, 16)
    f32 = jnp.float32

    def nrm(k, shape, scale):
        return jax.random.normal(k, shape, f32) * scale

    def gain(k, shape):
        return 1.0 + 0.02 * jax.random.normal(k, shape, f32)

    x = nrm(ks[0], (BATCH, SEQ, D_MODEL), 1.0)
    norm1_g = gain(ks[1], (DEPTH, D_MODEL))
    w_in = nrm(ks[2], (DEPTH, D_MODEL, W_IN_COLS), D_MODEL ** -0.5)
    dn_conv_w = nrm(ks[3], (DEPTH, DN_CONV, 3 * DN_WIDTH), DN_CONV ** -0.5)
    dn_a_log = jnp.log(jax.random.uniform(ks[4], (DEPTH, DN_HEADS), f32, 1.0, 16.0))
    dt = jnp.exp(jax.random.uniform(ks[5], (DEPTH, DN_HEADS), f32, math.log(1e-3), math.log(1e-1)))
    dn_dt_bias = dt + jnp.log(-jnp.expm1(-dt))
    dn_norm_g = gain(ks[6], (DEPTH, DN_HEAD_DIM))
    sc_conv_w = nrm(ks[7], (DEPTH, SC_CONV, SC_WIDTH), SC_CONV ** -0.5)
    sc_norm_g = gain(ks[8], (DEPTH, SC_WIDTH))
    w_out = nrm(ks[9], (DEPTH, D_MIX_2, D_MODEL), D_MIX_2 ** -0.5)
    norm2_g = gain(ks[10], (DEPTH, D_MODEL))
    ffn_w_gate = nrm(ks[11], (DEPTH, D_MODEL, D_FF_2), D_MODEL ** -0.5)
    ffn_w_up = nrm(ks[12], (DEPTH, D_MODEL, D_FF_2), D_MODEL ** -0.5)
    ffn_w_down = nrm(ks[13], (DEPTH, D_FF_2, D_MODEL), D_FF_2 ** -0.5)
    final_norm_g = gain(ks[14], (D_MODEL,))
    return {'x': x, 'norm1_g': norm1_g, 'w_in': w_in, 'dn_conv_w': dn_conv_w,
            'dn_a_log': dn_a_log, 'dn_dt_bias': dn_dt_bias, 'dn_norm_g': dn_norm_g,
            'sc_conv_w': sc_conv_w, 'sc_norm_g': sc_norm_g, 'w_out': w_out,
            'norm2_g': norm2_g, 'ffn_w_gate': ffn_w_gate, 'ffn_w_up': ffn_w_up,
            'ffn_w_down': ffn_w_down, 'final_norm_g': final_norm_g}

def second_block(x, norm1_g, w_in, dn_conv_w, dn_a_log, dn_dt_bias, dn_norm_g, sc_conv_w,
              sc_norm_g, w_out, norm2_g, ffn_w_gate, ffn_w_up, ffn_w_down, final_norm_g):
    for l in range(DEPTH):
        x = hybrid_layer(x, norm1_g[l], w_in[l], dn_conv_w[l], dn_a_log[l], dn_dt_bias[l],
                         dn_norm_g[l], sc_conv_w[l], sc_norm_g[l], w_out[l], norm2_g[l],
                         ffn_w_gate[l], ffn_w_up[l], ffn_w_down[l])
    return rms_norm(x, final_norm_g)


def setup_inputs(seed=0):
    out = dict(first_inputs(seed))
    for name, value in second_inputs(seed + 1).items():
        if name != "x":
            out[name + "_2"] = value
    return out


def reference(
    x, c, rel_bias, ada_w, ada_b, ln_g, ln_b, ffn_w1, ffn_w3, ffn_w2, w_in, w_out, cmp_pe,
    cmp_w1, cmp_b1, cmp_w2, gmlp_ln_g, gmlp_ln_b, gmlp_ws, gmlp_bs, ssm_conv_w, ssm_conv_b,
    ssm_dt_bias, ssm_a_log, ssm_d, ssm_norm_g, norm1_g_2, w_in_2, dn_conv_w_2, dn_a_log_2,
    dn_dt_bias_2, dn_norm_g_2, sc_conv_w_2, sc_norm_g_2, w_out_2, norm2_g_2, ffn_w_gate_2,
    ffn_w_up_2, ffn_w_down_2, final_norm_g_2,
):
    x = first_block(
        x, c, rel_bias, ada_w, ada_b, ln_g, ln_b, ffn_w1, ffn_w3, ffn_w2, w_in, w_out, cmp_pe,
        cmp_w1, cmp_b1, cmp_w2, gmlp_ln_g, gmlp_ln_b, gmlp_ws, gmlp_bs, ssm_conv_w, ssm_conv_b,
        ssm_dt_bias, ssm_a_log, ssm_d, ssm_norm_g,
    )
    return second_block(
        x, norm1_g_2, w_in_2, dn_conv_w_2, dn_a_log_2, dn_dt_bias_2, dn_norm_g_2, sc_conv_w_2,
        sc_norm_g_2, w_out_2, norm2_g_2, ffn_w_gate_2, ffn_w_up_2, ffn_w_down_2, final_norm_g_2,
    )


_drawn_inputs = setup_inputs


def setup_inputs(seed=0):
    import zlib

    import numpy as np

    out = dict(_drawn_inputs(seed))
    spreads = {}
    factors = {'dn_norm_g_2': 5.558, 'sc_norm_g_2': 3.063, 'norm2_g_2': 2.956, 'final_norm_g_2': 2.863}
    for name, (base, spread) in spreads.items():
        noise = np.random.default_rng([zlib.crc32(name.encode()), seed]).standard_normal(out[name].shape)
        drawn = base * np.exp(spread * noise) if base else spread * noise
        out[name] = __import__('jax').numpy.asarray(drawn.astype(out[name].dtype))
    for name, factor in factors.items():
        out[name] = (out[name] * factor).astype(out[name].dtype)
    return out
```

```python
import math
from collections import namedtuple
from contextlib import ExitStack, contextmanager

import numpy as np
import concourse.bass as bass
from concourse import mybir

F32 = mybir.dt.float32
ALU = mybir.AluOpType
ACT = mybir.ActivationFunctionType
AX = mybir.AxisListType

P = 128
T = 512
TT = T // P
D = 1024
DT = D // P
F = 2816
FT = F // P
DEPTH = 2
ALPHA = (2 * DEPTH) ** 0.25
LN_EPS = 1e-5
RMS_EPS = 1e-6

HEADS, GROUPS, HD = 8, 2, 64
HPG = HEADS // GROUPS
KV = GROUPS * HD
N_BRANCH = 3
CMP_LEN, CMP_STRIDE, CMP_HID = 32, 16, 256
N_CMP = (T - CMP_LEN) // CMP_STRIDE + 1
BUCKETS, MAX_DIST = 32, 128
Q_OFF = 0
KC_OFF = HEADS * HD
VW_OFF = KC_OFF + 5 * KV
GATE_OFF = KC_OFF + 6 * KV
GMLP_OFF = GATE_OFF + HEADS * N_BRANCH
D_GMLP, GG, GGD = 256, 4, 64
Z_OFF = GMLP_OFF + 2 * D_GMLP
D_SSM, SH, SG, NSTATE, SCONV = 256, 4, 2, 128, 4
XBC_OFF = Z_OFF + D_SSM
D_XBC = D_SSM + 2 * SG * NSTATE
XT = D_XBC // P
DT_OFF = XBC_OFF + D_XBC
D_IN = DT_OFF + SH
MASKED = -1.0e30
FLOOR = -1.0e29

DH, DHD, DCONV = 4, 128, 4
DW = DH * DHD
SCW, SCCONV = 512, 3
SCT = SCW // P
W2_COLS = 4 * DW + 2 * DH + 3 * SCW
LEVELS = 7


def rel_bucket_onehot():
    dist = T - 1 - np.arange(T + P)
    n = np.maximum(dist, 0)
    exact = BUCKETS // 2
    nf = np.maximum(n, 1).astype(np.float32)
    large = exact + (np.log(nf / exact) / math.log(MAX_DIST / exact) * (BUCKETS - exact)).astype(np.int32)
    bucket = np.where(n < exact, n, np.minimum(large, BUCKETS - 1))
    out = np.zeros((BUCKETS + 1, T + P), np.float32)
    seen = dist >= 0
    out[bucket[seen], np.nonzero(seen)[0]] = 1
    out[BUCKETS, ~seen] = 1
    return out


def triangle():
    return (np.arange(T + P * 3)[None, :] - P * 3 >= np.arange(P)[:, None]).astype(np.float32)


def level_masks():
    i = np.arange(P)
    out = np.zeros((P, LEVELS, P), np.float32)
    for n in range(LEVELS):
        m = 1 << n
        out[:, n, :] = ((i[:, None] // (2 * m) == i[None, :] // (2 * m))
                        & ((i // m) % 2 == 0)[:, None] & ((i // m) % 2 == 1)[None, :])
    return out


class Memory:
    pass


@contextmanager
def stage(nc, name, signals):
    names = signals.split()
    sems = [nc.alloc_semaphore(f"{name}_{s}") for s in names]
    with nc.Block(name) as block:
        yield block, namedtuple("Signals", names)(*sems)
    nc.clear_and_free_semaphores(sems)
    nc.all_engine_barrier()


def tensors(nc, memory, prefix):
    return lambda name, *shape: memory.enter_context(nc.sbuf_tensor(prefix + name, [P, *shape], F32))


def chain(engine, sem):
    done = [0]

    def link(instruction):
        done[0] += 1
        instruction.then_inc(sem, 1)
        engine.wait_ge(sem, done[0])
        return instruction
    return link


def setup(nc, M, I):
    with stage(nc, "setup", "consts onehot x_landed rel_landed mask_row turned copied tape_ready "
               "tape_copied tape_stored bias_landed bias_turned") as (block, S):
        x_rows = M.hT[:].rearrange("p d t -> p (d t)").rearrange("p (i n) -> p i n", i=TT)

        @block.sync
        def _(sp):
            sp.dma_start(M.ident[:], nc.inline_tensor(np.eye(P, dtype=np.float32), name="c_ident").ap()).then_inc(S.consts, 16)
            sp.dma_start(M.tri[:], nc.inline_tensor(triangle(), name="c_tri").ap()).then_inc(S.consts, 16)
            sp.dma_start(M.ones[:], nc.inline_tensor(np.ones((P, P), np.float32), name="c_ones").ap()).then_inc(S.consts, 16)
            sp.dma_start(M.mean_d[:], nc.inline_tensor(np.full((P, P), 1 / D, np.float32), name="c_mean").ap()).then_inc(S.consts, 16)
            sp.dma_start(x_rows, I.x[0].rearrange("(i p) n -> p i n", p=P)).then_inc(S.x_landed, 16)
            sp.dma_start(M.onehot[0:BUCKETS + 1, :],
                         nc.inline_tensor(rel_bucket_onehot(), name="c_bucket").ap()).then_inc(S.onehot, 16)
            sp.dma_start(M.relx[0:BUCKETS, :], I.rel_bias).then_inc(S.rel_landed, 16)
            sp.dma_start(M.flip, nc.inline_tensor(np.eye(P, dtype=np.float32)[::-1].copy(), name="c_flip").ap()).then_inc(S.consts, 16)
            sp.wait_ge(S.tape_copied, 2)
            sp.dma_start(M.tape_dram, M.tape[0:HEADS, :]).then_inc(S.tape_stored, 16)
            sp.wait_ge(S.tape_stored, 16)
            for h in range(HEADS):
                rows = bass.AP(tensor=M.tape_dram.tensor, offset=h * (T + P), ap=[[1, P], [1, T]])
                sp.dma_start(M.flipped[:, h, :], rows).then_inc(S.bias_landed, 16)

        @block.tensor
        def _(pe):
            pe.wait_ge(S.consts, 80)
            pe.wait_ge(S.x_landed, 16)
            for d in range(DT):
                for i in range(TT):
                    mm = pe.transpose(M.ps[:, d, i * P:(i + 1) * P], x_rows[:, i, d * P:(d + 1) * P], M.ident[:])
                mm.then_inc(S.turned, 1)
            pe.wait_ge(S.onehot, 16)
            pe.wait_ge(S.rel_landed, 16)
            pe.wait_ge(S.mask_row, 1)
            pe.wait_ge(S.copied, 2)
            pe.matmul(M.ps[0:HEADS, 0, :], M.relx[0:BUCKETS + 1, :], M.onehot[0:BUCKETS + 1, 0:T],
                      start=True, stop=True).then_inc(S.tape_ready, 1)
            pe.matmul(M.ps[0:HEADS, 1, 0:P], M.relx[0:BUCKETS + 1, :], M.onehot[0:BUCKETS + 1, T:T + P],
                      start=True, stop=True).then_inc(S.tape_ready, 1)
            pe.wait_ge(S.bias_landed, 16 * HEADS)
            pe.wait_ge(S.copied, DT)
            for h in range(HEADS):
                pe.matmul(M.ps[:, h, :], M.flip, M.flipped[:, h, :], start=True, stop=True).then_inc(S.bias_turned, 1)

        @block.vector
        def _(dve):
            dve.memset(M.relx[BUCKETS:BUCKETS + 1, :], MASKED).then_inc(S.mask_row, 1)
            for d in range(DT):
                dve.wait_ge(S.turned, d + 1)
                dve.tensor_copy(M.x[:, d, :], M.ps[:, d, :]).then_inc(S.copied, 1)
            dve.wait_ge(S.tape_ready, 2)
            dve.tensor_copy(M.tape[0:HEADS, 0:T], M.ps[0:HEADS, 0, :]).then_inc(S.tape_copied, 1)
            dve.tensor_copy(M.tape[0:HEADS, T:T + P], M.ps[0:HEADS, 1, 0:P]).then_inc(S.tape_copied, 1)
            for h in range(HEADS):
                dve.wait_ge(S.bias_turned, h + 1)
                dve.tensor_copy(M.bias[:, h, :], M.ps[:, h, :])


def modulation(nc, M, I, l):
    chunks = 9 * D // 512
    slots = [M.wide[:, s].rearrange("p a k n -> p (a k n)").rearrange("p (k n) -> p k n", k=DT) for s in range(2)]
    w = I.ada_w[l].rearrange("(k p) n -> p k n", p=P)
    with stage(nc, "ada", "c_landed rows_landed w0_landed w1_landed c_ready mac partial column "
               "rows_turned dve") as (block, S):
        landed = [S.w0_landed, S.w1_landed]

        @block.sync
        def _(sp):
            with nc.allow_non_contiguous_dma(reason="one vector as columns"):
                sp.dma_start(M.ccol[:], I.c[0].rearrange("(k p) -> p k", p=P)).then_inc(S.c_landed, 16)
            sp.dma_start(M.prow[0:72, :], I.ada_b[l].rearrange("(r n) -> r n", n=P)).then_inc(S.rows_landed, 16)
            sp.dma_start(M.prow[72:96, :], I.ln_g[l].rearrange("s (d n) -> (s d) n", n=P)).then_inc(S.rows_landed, 16)
            sp.dma_start(M.prow[96:120, :], I.ln_b[l].rearrange("s (d n) -> (s d) n", n=P)).then_inc(S.rows_landed, 16)
            for s in range(2):
                sp.dma_start(slots[s], w[:, :, s * 512:(s + 1) * 512]).then_inc(landed[s], 16)
            with sp.Fori(0, chunks // 2 - 1) as i:
                for s in range(2):
                    sp.wait_ge(S.partial, 2 * i + s + 1)
                    sp.dma_start(slots[s], w[:, :, bass.ds((2 * i + s + 2) * 512, 512)]).then_inc(landed[s], 16)

        @block.scalar
        def _(act):
            act.wait_ge(S.c_landed, 16)
            act.activation(M.ccol[:], M.ccol[:], ACT.Silu).then_inc(S.c_ready, 1)

        @block.vector
        def _(dve):
            dve.wait_ge(S.c_ready, 1)

            def chunk(s, first, i):
                n = 2 * i + s
                dve.wait_ge(landed[s], 16 * (i + 1))
                if not first:
                    dve.wait_ge(S.column, n - 1)
                dve.tensor_scalar(M.part[:, s, :], slots[s][:, 0, :], M.ccol[:, 0:1], None,
                                  ALU.mult).then_inc(S.mac, 1)
                for k in range(1, DT):
                    dve.wait_ge(S.mac, n * (DT - 1) + k)
                    ins = dve.scalar_tensor_tensor(out=M.part[:, s, :], in0=slots[s][:, k, :],
                                                   scalar=M.ccol[:, k:k + 1], in1=M.part[:, s, :],
                                                   op0=ALU.mult, op1=ALU.add)
                    ins.then_inc(S.mac if k < DT - 1 else S.partial, 1)

            chunk(0, True, 0)
            chunk(1, True, 0)
            with dve.Fori(1, chunks // 2) as i:
                chunk(0, False, i)
                chunk(1, False, i)
            link = chain(dve, S.dve)
            dve.wait_ge(S.rows_turned, 1)
            link(dve.tensor_copy(M.pcol[:], M.ps[:, 1, 0:120]))
            dve.wait_ge(S.column, chunks)
            link(dve.tensor_tensor(M.mod[:], M.ps[:, 0, 0:72], M.pcol[:, 0:72], ALU.add))
            for sub in range(3):
                weight = 1.0 if sub == 1 else 0.5
                scale, gate = (M.mod[:, sub * 24 + w * DT:sub * 24 + (w + 1) * DT] for w in (1, 2))
                link(dve.tensor_scalar(scale, scale, 1.0, None, ALU.add))
                link(dve.tensor_scalar(gate, gate, 1.0, weight / ALPHA, ALU.add, ALU.mult))

        @block.tensor
        def _(pe):
            pe.wait_ge(S.rows_landed, 48)
            pe.transpose(M.ps[:, 1, 0:120], M.prow[0:120, :], M.ident[0:120, 0:120]).then_inc(S.rows_turned, 1)
            with pe.Fori(0, chunks // 2) as i:
                for s in range(2):
                    pe.wait_ge(S.partial, 2 * i + s + 1)
                    for q in range(4):
                        mm = pe.matmul(M.ps[:, 0, bass.ds((2 * i + s) * 4 + q, 1)], M.part[:, s, q * P:(q + 1) * P],
                                       M.ones[:, 0:1], start=True, stop=True)
                    mm.then_inc(S.column, 1)


NORM_SIGNALS = " z_ready mean_ready centered square_ready square_used var_ready root_ready rstd_ready xhat_ready"


def post_norm_pe(pe, M, S):
    for d in range(DT):
        pe.wait_ge(S.z_ready, d + 1)
        mm = pe.matmul(M.ps[:, 0, :], M.mean_d[:], M.x[:, d, :], start=(d == 0), stop=(d == DT - 1))
    mm.then_inc(S.mean_ready, 1)
    for d in range(DT):
        pe.wait_ge(S.square_ready, d + 1)
        pe.matmul(M.ps[:, 1, :], M.mean_d[:], M.sq[:, d % 2, :], start=(d == 0),
                  stop=(d == DT - 1)).then_inc(S.square_used, 1)


def post_norm_act(act, M, S):
    for d in range(DT):
        act.wait_ge(S.centered, d + 1)
        if d >= 2:
            act.wait_ge(S.square_used, d - 1)
        act.activation(M.sq[:, d % 2, :], M.x[:, d, :], ACT.Square).then_inc(S.square_ready, 1)
    act.wait_ge(S.var_ready, 1)
    act.activation(M.rstd[:], M.rstd[:], ACT.Sqrt).then_inc(S.root_ready, 1)


def post_norm_dve(dve, M, S, sub):
    gate = M.mod[:, sub * 24 + 2 * DT:sub * 24 + 3 * DT]
    g = M.pcol[:, 72 + sub * DT:72 + (sub + 1) * DT]
    b = M.pcol[:, 96 + sub * DT:96 + (sub + 1) * DT]
    for d in range(DT):
        dve.wait_ge(S.y_ready, d + 1)
        dve.scalar_tensor_tensor(out=M.x[:, d, :], in0=M.ps[:, d, :], scalar=gate[:, d:d + 1],
                                 in1=M.x[:, d, :], op0=ALU.mult, op1=ALU.add).then_inc(S.z_ready, 1)
    dve.wait_ge(S.z_ready, DT)
    dve.wait_ge(S.mean_ready, 1)
    for d in range(DT):
        dve.tensor_tensor(M.x[:, d, :], M.x[:, d, :], M.ps[:, 0, :], ALU.subtract).then_inc(S.centered, 1)
    dve.wait_ge(S.square_used, DT)
    dve.tensor_scalar(M.rstd[:], M.ps[:, 1, :], LN_EPS / ALPHA ** 2, None, ALU.add).then_inc(S.var_ready, 1)
    dve.wait_ge(S.root_ready, 1)
    dve.reciprocal(M.rstd[:], M.rstd[:]).then_inc(S.rstd_ready, 1)
    dve.wait_ge(S.rstd_ready, 1)
    for d in range(DT):
        dve.tensor_tensor(M.x[:, d, :], M.x[:, d, :], M.rstd[:], ALU.mult).then_inc(S.xhat_ready, 1)
    for d in range(DT):
        dve.wait_ge(S.xhat_ready, d + 1)
        dve.tensor_scalar(M.x[:, d, :], M.x[:, d, :], g[:, d:d + 1], b[:, d:d + 1], ALU.mult, ALU.add)


def modulate_act(act, M, S, sub):
    for d in range(DT):
        act.activation(M.hT[:, d, :], M.x[:, d, :], ACT.Identity, scale=M.mod[:, sub * 24 + DT + d:sub * 24 + DT + d + 1],
                       bias=M.mod[:, sub * 24 + d:sub * 24 + d + 1]).then_inc(S.h_ready, 1)


def ffn(nc, M, tag, w_gate, w_up, w_down, sub):
    slices = F // 256
    pairs = FT // 2
    gate_v = w_gate.rearrange("(k p) f -> p k f", p=P)
    up_v = w_up.rearrange("(k p) f -> p k f", p=P)
    down_v = w_down.rearrange("(f p) n -> p f n", p=P)
    signals = ("h_ready wide0_landed wide1_landed rows0_landed rows1_landed projected silu_done hidden_done "
               "pair_used y_ready x_done")
    with ExitStack() as memory, stage(nc, tag, signals + NORM_SIGNALS) as (block, S):
        hid = memory.enter_context(nc.sbuf_tensor(f"{tag}_hid", [P, FT, T], F32))
        sil = memory.enter_context(nc.sbuf_tensor(f"{tag}_sil", [P, 2, T], F32))
        wide_landed = [S.wide0_landed, S.wide1_landed]
        rows_landed = [S.rows0_landed, S.rows1_landed]

        @block.sync
        def _(sp):
            def load_slice(s, n):
                sp.dma_start(M.wide[:, s, 0], gate_v[:, :, bass.ds(n * 256, 256)]).then_inc(wide_landed[s], 16)
                sp.dma_start(M.wide[:, s, 1], up_v[:, :, bass.ds(n * 256, 256)]).then_inc(wide_landed[s], 16)

            def load_pair(s, n):
                sp.dma_start(M.rows[:, s], down_v[:, bass.ds(n * 2, 2), :]).then_inc(rows_landed[s], 16)

            load_slice(0, 0)
            load_slice(1, 1)
            load_pair(0, 0)
            load_pair(1, 1)
            with sp.Fori(1, slices // 2) as i:
                for s in range(2):
                    sp.wait_ge(S.projected, 4 * i + 2 * s - 2)
                    load_slice(s, 2 * i + s)
            sp.wait_ge(S.projected, 2 * slices - 4)
            load_slice(0, slices - 1)
            with sp.Fori(1, pairs // 2) as i:
                for s in range(2):
                    sp.wait_ge(S.pair_used, 2 * i + s - 1)
                    load_pair(s, 2 * i + s)
            sp.wait_ge(S.pair_used, pairs - 2)
            load_pair(0, pairs - 1)

        @block.tensor
        def _(pe):
            def project(s, half, f, landings, wait_banks):
                if wait_banks:
                    pe.wait_ge(S.hidden_done, f - 1)
                if half == 0:
                    pe.wait_ge(wide_landed[s], landings)
                for which in range(2):
                    for k in range(DT):
                        mm = pe.matmul(M.ps[:, 2 * half + which, :], M.wide[:, s, which, k, half * P:(half + 1) * P],
                                       M.hT[:, k, :], start=(k == 0), stop=(k == DT - 1))
                mm.then_inc(S.projected, 1)

            if sub is not None:
                pe.wait_ge(S.h_ready, DT)
            for s in range(2):
                for half in range(2):
                    project(s, half, 2 * s + half, 32, s > 0)
            with pe.Fori(1, slices // 2) as i:
                for s in range(2):
                    for half in range(2):
                        project(s, half, 4 * i + 2 * s + half, 32 * i + 32, True)
            for half in range(2):
                project(0, half, FT - 2 + half, 32 * (slices // 2 + 1), True)

            def down(s, n, landings, first):
                pe.wait_ge(rows_landed[s], landings)
                for e in range(2):
                    for d in range(DT):
                        mm = pe.matmul(M.ps[:, d, :], M.rows[:, s, e, d * P:(d + 1) * P], hid[:, bass.ds(2 * n + e, 1), :]
                                       .rearrange("p a t -> p (a t)"),
                                       start=(first and e == 0), stop=False, skip_group_check=True)
                mm.then_inc(S.pair_used, 1)

            pe.wait_ge(S.hidden_done, FT)
            down(0, 0, 16, True)
            down(1, 1, 16, False)
            with pe.Fori(1, pairs // 2) as i:
                for s in range(2):
                    down(s, 2 * i + s, 16 * i + 16, False)
            pe.wait_ge(rows_landed[0], 16 * (pairs // 2 + 1))
            for d in range(DT):
                for e in range(2):
                    mm = pe.matmul(M.ps[:, d, :], M.rows[:, 0, e, d * P:(d + 1) * P], hid[:, FT - 2 + e, :],
                                   start=False, stop=(e == 1), skip_group_check=True)
                mm.then_inc(S.y_ready, 1)
            if sub is not None:
                post_norm_pe(pe, M, S)

        @block.scalar
        def _(act):
            if sub is not None:
                modulate_act(act, M, S, sub)

            def tile(f, half, wait_buffer):
                act.wait_ge(S.projected, f + 1)
                if wait_buffer:
                    act.wait_ge(S.hidden_done, f - 1)
                act.activation(sil[:, half, :], M.ps[:, 2 * half, :], ACT.Silu).then_inc(S.silu_done, 1)

            tile(0, 0, False)
            tile(1, 1, False)
            with act.Fori(1, FT // 2) as i:
                tile(2 * i, 0, True)
                tile(2 * i + 1, 1, True)
            if sub is not None:
                post_norm_act(act, M, S)

        @block.vector
        def _(dve):
            with dve.Fori(0, FT // 2) as i:
                for half in range(2):
                    dve.wait_ge(S.silu_done, 2 * i + half + 1)
                    dve.tensor_tensor(hid[:, bass.ds(2 * i + half, 1), :].rearrange("p a t -> p (a t)"), sil[:, half, :],
                                      M.ps[:, 2 * half + 1, :], ALU.mult).then_inc(S.hidden_done, 1)
            if sub is not None:
                post_norm_dve(dve, M, S, sub)
            else:
                for d in range(DT):
                    dve.wait_ge(S.y_ready, d + 1)
                    dve.tensor_tensor(M.x[:, d, :], M.x[:, d, :], M.ps[:, d, :], ALU.add)


def project(nc, M, tag, chunks, tiles, sub):
    slots = [M.wide[:, s].rearrange("p a k n -> p (a k n)").rearrange("p (k n) -> p k n", k=DT) for s in range(2)]
    last_tile = [max(n for n, t in enumerate(tiles) if t[0] == c) for c in range(len(chunks))]
    engine_of = [t[3] for t in tiles]

    def evacuated(n):
        return engine_of[:n + 1].count(engine_of[n])

    with stage(nc, tag, "h_ready w0_landed w1_landed product act_evacuated dve_evacuated") as (block, S):
        landed = [S.w0_landed, S.w1_landed]
        done = {"act": S.act_evacuated, "dve": S.dve_evacuated}
        landings = [16 * sum(len(chunks[j]) for j in range(c % 2, c + 1, 2)) for c in range(len(chunks))]

        @block.sync
        def _(sp):
            for c, pieces in enumerate(chunks):
                if c >= 2:
                    sp.wait_ge(S.product, last_tile[c - 2] + 1)
                for cols, src in pieces:
                    sp.dma_start(slots[c % 2][:, :, cols], src).then_inc(landed[c % 2], 16)

        @block.tensor
        def _(pe):
            if sub is not None:
                pe.wait_ge(S.h_ready, DT)
            for n, (c, cols, i, _, _) in enumerate(tiles):
                if n == 0 or tiles[n - 1][0] != c:
                    pe.wait_ge(landed[c % 2], landings[c])
                if n >= 8:
                    pe.wait_ge(done[engine_of[n - 8]], evacuated(n - 8))
                w = slots[c % 2][:, :, cols]
                for k in range(DT):
                    if i is None:
                        mm = pe.matmul(M.ps[:, n % 8, :], w[:, k, :], M.hT[:, k, :], start=(k == 0), stop=(k == DT - 1))
                    else:
                        mm = pe.matmul(M.ps[:, n % 8, 0:w.shape[2]], M.hT[:, k, i * P:(i + 1) * P], w[:, k, :],
                                       start=(k == 0), stop=(k == DT - 1))
                mm.then_inc(S.product, 1)

        @block.scalar
        def _(act):
            if sub is not None:
                modulate_act(act, M, S, sub)
            for n, (_, _, i, engine, evacuate) in enumerate(tiles):
                if engine == "act":
                    act.wait_ge(S.product, n + 1)
                    evacuate(act, M.ps[:, n % 8, :], i).then_inc(S.act_evacuated, 1)

        @block.vector
        def _(dve):
            for n, (_, _, i, engine, evacuate) in enumerate(tiles):
                if engine == "dve":
                    dve.wait_ge(S.product, n + 1)
                    evacuate(dve, M.ps[:, n % 8, :], i).then_inc(S.dve_evacuated, 1)


def mixer1_project(nc, M, A, I, l):
    w = I.w_in[l].rearrange("(k p) n -> p k n", p=P)
    q_pieces = [(slice(P * a + HD * g, P * a + HD * (g + 1)), w[:, :, (a + HPG * g) * HD:(a + HPG * g + 1) * HD])
                for a in range(HPG) for g in range(GROUPS)]
    bounds = [KC_OFF, KC_OFF + 4 * KV, GMLP_OFF, Z_OFF, XBC_OFF, XBC_OFF + 4 * P, D_IN]
    chunks = [q_pieces] + [[(slice(0, b - a), w[:, :, a:b])] for a, b in zip(bounds, bounds[1:])]
    cols = lambda a, n: slice(a, a + n)

    def q_tile(a):
        return lambda act, ps, i: act.activation(A.qT[:, a, :], ps, ACT.Copy, scale=HD ** -0.5)

    def blocks(j):
        return lambda dve, ps, i: dve.tensor_copy(
            A.blk[:, j, :, 0:N_CMP], bass.AP(tensor=ps.tensor, offset=ps.offset,
                                             ap=[list(ps.ap[0]), [1, CMP_LEN], [CMP_STRIDE, N_CMP]]))

    def copy_to(dst):
        return lambda dve, ps, i: dve.tensor_copy(dst, ps[:, 0:dst.shape[-1]])

    def vs_tile(dve, ps, i):
        return dve.tensor_copy(A.vs[:, i, :], ps[:, 0:KV])

    def vw_gate_tile(act, ps, i):
        act.copy(A.vw[:, i, :], ps[:, 0:KV])
        return act.activation(A.gates[:, i, :], ps[:, KV:KV + HEADS * N_BRANCH], ACT.Sigmoid)

    tiles = [(0, cols(P * a, P), None, "act", q_tile(a)) for a in range(HPG)]
    tiles += [(1, cols(0, P), None, "dve", blocks(0)), (1, cols(P, P), None, "dve", blocks(1)),
              (1, cols(2 * P, P), None, "dve", copy_to(A.ksT[:]))]
    tiles += [(1, cols(3 * P, KV), i, "dve", vs_tile) for i in range(TT)]
    tiles += [(2, cols(0, P), None, "dve", copy_to(A.kwT[:]))]
    tiles += [(2, cols(P, KV + HEADS * N_BRANCH), i, "act", vw_gate_tile) for i in range(TT)]
    tiles += [(3, cols(0, 2 * D_GMLP), i, "act",
               lambda act, ps, i: act.activation(A.uv[:, i, :], ps, ACT.Gelu_apprx_tanh)) for i in range(TT)]
    tiles += [(4, cols(0, D_SSM), i, "act",
               lambda act, ps, i: act.activation(A.silz[:, i, :], ps[:, 0:D_SSM], ACT.Silu)) for i in range(TT)]
    tiles += [(5 + c // 4, cols(P * (c % 4), P), None, "dve", copy_to(A.raw[:, c, SCONV - 1:])) for c in range(XT)]
    tiles += [(6, cols(2 * P, SH), i, "dve", lambda dve, ps, i: dve.tensor_copy(A.dt[:, i, :], ps[:, 0:SH]))
              for i in range(TT)]
    project(nc, M, "proj1", chunks, tiles, 1)


def mixer1_local(nc, M, A, I, l):
    with stage(nc, "local", "w0_landed w1_landed w_half_used pe_landed small_landed ws_landed cmp_sum bias_col "
               "hidden keys_ready taps_padded conv_acc conv_done ws_turned ws_copied "
               "v_normed spatial act_chain dve_chain var_ready root_ready exp_ready one_plus ln_ready") as (block, S):
        w_landed = [S.w0_landed, S.w1_landed]
        slots = [M.wide[:, s].rearrange("p a k n -> p (a k n)").rearrange("p (l n) -> p l n", l=16) for s in range(2)]

        @block.sync
        def _(sp):
            with nc.allow_non_contiguous_dma(reason="small vectors as columns"):
                for j in range(2):
                    for g in range(GROUPS):
                        sp.dma_start(A.blk[HD * g:HD * (g + 1), j, :, N_CMP], I.cmp_pe[l, j].rearrange("l d -> d l")
                                     ).then_inc(S.pe_landed, 16)
            for n in range(4):
                if n >= 2:
                    sp.wait_ge(S.w_half_used, n - 1)
                src = I.cmp_w1[l, n // 2].rearrange("(l d) n -> d l n", d=HD)[:, 16 * (n % 2):16 * (n % 2) + 16, :]
                for g in range(GROUPS):
                    sp.dma_start(slots[n % 2][HD * g:HD * (g + 1)], src).then_inc(w_landed[n % 2], 16)
            with nc.allow_non_contiguous_dma(reason="small vectors as columns"):
                sp.dma_start(A.cmp_b[:], I.cmp_b1[l].rearrange("j (m p) -> p (j m)", p=P)).then_inc(S.small_landed, 16)
                sp.dma_start(A.conv_w[:], I.ssm_conv_w[l].rearrange("j (c p) -> p j c", p=P)).then_inc(S.small_landed, 16)
                sp.dma_start(A.conv_b[:], I.ssm_conv_b[l].rearrange("(c p) -> p c", p=P)).then_inc(S.small_landed, 16)
                sp.dma_start(A.ws_b[:], I.gmlp_bs[l].rearrange("g p -> p g")).then_inc(S.small_landed, 16)
            for j in range(2):
                for g in range(GROUPS):
                    sp.dma_start(A.cmp_w2[:, j, :, g, :], I.cmp_w2[l, j].rearrange("(m p) d -> p m d", p=P)
                                 ).then_inc(S.small_landed, 16)
            for dst, vector in ((A.dt_bias, I.ssm_dt_bias), (A.a_log, I.ssm_a_log), (A.d_skip, I.ssm_d),
                                (A.norm_g, I.ssm_norm_g), (A.ln_g, I.gmlp_ln_g), (A.ln_b, I.gmlp_ln_b)):
                sp.dma_start(dst[:], vector[l].partition_broadcast(P)).then_inc(S.small_landed, 16)
            sp.dma_start(A.ws[:], I.gmlp_ws[l].rearrange("g t s -> t g s")).then_inc(S.ws_landed, 16)

        small = 16 * 14

        @block.tensor
        def _(pe):
            pe.wait_ge(S.pe_landed, 64)
            for n in range(4):
                j, half = n // 2, n % 2
                pe.wait_ge(w_landed[n % 2], 32 * (n // 2 + 1))
                for m in range(2):
                    for g in range(GROUPS):
                        rows = slice(HD * g, HD * (g + 1))
                        for q in range(16):
                            mm = pe.matmul(M.ps[:, 4 * j + 2 * m + g, 0:N_CMP + 1],
                                           slots[n % 2][rows, q, m * P:(m + 1) * P], A.blk[rows, j, 16 * half + q, :],
                                           start=(half == 0 and q == 0), stop=(half == 1 and q == 15))
                mm.then_inc(S.w_half_used, 1)
            pe.wait_ge(S.hidden, 4)
            pe.wait_ge(S.small_landed, small)
            for g in range(GROUPS):
                for m in range(2):
                    mm = pe.matmul(M.ps[:, g, 0:N_CMP], A.cmp_w2[:, 0, m].rearrange("p g d -> p (g d)"),
                                   A.cmp_h[:, 0, m, g, :], start=(m == 0), stop=(m == 1))
            pe.wait_ge(S.hidden, 8)
            for g in range(GROUPS):
                for m in range(2):
                    mm = pe.matmul(M.ps[0:N_CMP, 2 + g, 0:HD], A.cmp_h[:, 1, m, g, :], A.cmp_w2[:, 1, m, 0, :],
                                   start=(m == 0), stop=(m == 1))
            mm.then_inc(S.keys_ready, 1)
            pe.wait_ge(S.ws_landed, 16)
            for g in range(GG):
                mm = pe.transpose(M.ps[:, 4, g * P:(g + 1) * P], A.ws[:, g, :], M.ident[:])
            mm.then_inc(S.ws_turned, 1)
            pe.wait_ge(S.ws_copied, 1)
            pe.wait_ge(S.v_normed, 1)
            for g in range(GG):
                rhs = A.uv[:, :, D_GMLP + GGD * g:D_GMLP + GGD * (g + 1)]
                out = M.ps[:, 5 + g // 2, (g % 2) * 256:(g % 2) * 256 + 256].rearrange("p (c d) -> p c d", c=TT)
                mm = pe.matmul(out, A.wsT[:, g, :], rhs, start=True, stop=True)
            mm.then_inc(S.spatial, 1)

        @block.scalar
        def _(act):
            link = chain(act, S.act_chain)
            act.wait_ge(S.small_landed, small)
            link(act.activation(A.a_neg[:], A.a_log[:], ACT.Exp))
            act.wait_ge(S.one_plus, 1)
            act.activation(A.dt_e[:], A.dt_e[:], ACT.Exp, scale=-1.0).then_inc(S.exp_ready, 1)
            act.wait_ge(S.one_plus, 2)
            act.activation(A.dt_ln[:], A.dt_u[:], ACT.Ln).then_inc(S.ln_ready, 1)
            for c in range(XT):
                act.wait_ge(S.conv_acc, SCONV * (c + 1))
                act.activation(A.xbc[:, c, :], A.xbc[:, c, :], ACT.Silu, bias=A.conv_b[:, c:c + 1]).then_inc(S.conv_done, 1)
            for j in range(2):
                act.wait_ge(S.bias_col, j + 1)
                for m in range(2):
                    for g in range(GROUPS):
                        act.activation(A.cmp_h[:, j, m, g, :], M.ps[:, 4 * j + 2 * m + g, 0:N_CMP], ACT.Gelu_apprx_tanh,
                                       bias=A.cmp_b[:, 2 * j + m:2 * j + m + 1]).then_inc(S.hidden, 1)
            act.wait_ge(S.var_ready, 1)
            act.activation(A.root[:, 0:TT], A.root[:, 0:TT], ACT.Sqrt).then_inc(S.root_ready, 1)

        @block.vector
        def _(dve):
            dve.memset(A.raw[:, :, 0:SCONV - 1], 0.0).then_inc(S.taps_padded, 1)
            dve.wait_ge(S.taps_padded, 1)
            dve.wait_ge(S.small_landed, small)
            link = chain(dve, S.dve_chain)
            link(dve.tensor_tensor(A.dt[:], A.dt[:], A.dt_bias[:].unsqueeze(1).to_broadcast([P, TT, SH]), ALU.add))
            dve.scalar_tensor_tensor(out=A.dt_e[:], in0=A.dt[:], scalar=-1.0, in1=A.dt[:], op0=ALU.mult,
                                     op1=ALU.max).then_inc(S.one_plus, 1)
            dve.wait_ge(S.exp_ready, 1)
            dve.tensor_scalar(A.dt_u[:], A.dt_e[:], 1.0, None, ALU.add).then_inc(S.one_plus, 1)
            dve.wait_ge(S.one_plus, 2)
            link(dve.scalar_tensor_tensor(out=A.dt_r[:], in0=A.dt_u[:], scalar=-1.0, in1=A.dt_e[:], op0=ALU.add,
                                          op1=ALU.subtract))
            link(dve.tensor_scalar(A.dt[:], A.dt[:], 0.0, None, ALU.max))
            link(dve.tensor_tensor(A.dt[:], A.dt[:], A.dt_r[:], ALU.subtract))
            dve.wait_ge(S.ln_ready, 1)
            link(dve.tensor_tensor(A.dt[:], A.dt[:], A.dt_ln[:], ALU.add))
            dve.wait_ge(S.act_chain, 1)
            link(dve.scalar_tensor_tensor(out=A.a[:], in0=A.dt[:], scalar=-1.0,
                                          in1=A.a_neg[:].unsqueeze(1).to_broadcast([P, TT, SH]),
                                          op0=ALU.mult, op1=ALU.mult))
            for c in range(XT):
                dve.tensor_scalar(A.xbc[:, c, :], A.raw[:, c, 0:T], A.conv_w[:, 0, c:c + 1], None,
                                  ALU.mult).then_inc(S.conv_acc, 1)
                for j in range(1, SCONV):
                    dve.wait_ge(S.conv_acc, SCONV * c + j)
                    dve.scalar_tensor_tensor(out=A.xbc[:, c, :], in0=A.raw[:, c, j:j + T],
                                             scalar=A.conv_w[:, j, c:c + 1], in1=A.xbc[:, c, :],
                                             op0=ALU.mult, op1=ALU.add).then_inc(S.conv_acc, 1)
            for i in range(TT):
                link(dve.bn_stats(A.stats[:, i, :], A.uv[:, i, D_GMLP:]))
            for i in range(TT):
                link(dve.bn_aggr(A.mv[:, i, :], A.stats[:, i, :]))
            dve.tensor_scalar(A.root[:, 0:TT], A.mv[:, :, 1], LN_EPS, None, ALU.add).then_inc(S.var_ready, 1)
            for j in range(2):
                dve.wait_ge(S.w_half_used, 2 * j + 2)
                for m in range(2):
                    link(dve.tensor_tensor(A.cmp_b[:, 2 * j + m:2 * j + m + 1], A.cmp_b[:, 2 * j + m:2 * j + m + 1],
                                           M.ps[:, 4 * j + 2 * m, N_CMP:N_CMP + 1], ALU.add))
                dve.sem_inc(S.bias_col, 1)
            dve.wait_ge(S.root_ready, 1)
            link(dve.reciprocal(A.root[:, 0:TT], A.root[:, 0:TT]))
            for i in range(TT):
                v = A.uv[:, i, D_GMLP:]
                link(dve.tensor_scalar(v, v, A.mv[:, i, 0:1], A.root[:, i:i + 1], ALU.subtract, ALU.mult))
                link(dve.tensor_tensor(v, v, A.ln_g[:], ALU.mult))
                ins = dve.tensor_tensor(v, v, A.ln_b[:], ALU.add)
            ins.then_inc(S.v_normed, 1)
            dve.wait_ge(S.keys_ready, 1)
            for g in range(GROUPS):
                dve.tensor_copy(A.kcT[HD * g:HD * (g + 1), :], M.ps[HD * g:HD * (g + 1), g, 0:N_CMP])
                dve.tensor_copy(A.vc[0:N_CMP, g, :], M.ps[0:N_CMP, 2 + g, 0:HD])
            dve.wait_ge(S.ws_turned, 1)
            dve.tensor_tensor(A.wsT[:], M.ps[:, 4, :].rearrange("p (g t) -> p g t", g=GG),
                              M.tri[:, 3 * P:4 * P].unsqueeze(1).to_broadcast([P, GG, P]),
                              ALU.mult).then_inc(S.ws_copied, 1)
            dve.wait_ge(S.spatial, 1)
            for g in range(GG):
                ps = M.ps[:, 5 + g // 2, (g % 2) * 256:(g % 2) * 256 + 256].rearrange("p (c d) -> p c d", c=TT)
                dve.scalar_tensor_tensor(out=A.mix[:, :, HEADS * HD + GGD * g:HEADS * HD + GGD * (g + 1)], in0=ps,
                                         scalar=A.ws_b[:, g:g + 1], in1=A.uv[:, :, GGD * g:GGD * (g + 1)],
                                         op0=ALU.add, op1=ALU.mult)


def mixer1_compressed(nc, M, A):
    with stage(nc, "cmp", "bias_init bias_c scores chain shifted probs normed turned turned_copied pv mixed") as (block, S):

        @block.tensor
        def _(pe):
            def outputs(i):
                pe.wait_ge(S.normed, i + 1)
                if i >= 2:
                    pe.wait_ge(S.turned_copied, i - 1)
                for h in range(HEADS):
                    mm = pe.transpose(M.ps[0:N_CMP, 4 * (i % 2) + 1 + h // 4, (h % 4) * P:(h % 4 + 1) * P], A.score_c[:, i, h, :],
                                      M.ident[:])
                mm.then_inc(S.turned, 1)
                pe.wait_ge(S.turned_copied, i + 1)
                for h in range(HEADS):
                    mm = pe.matmul(M.ps[:, 4 * (i % 2) + 3, HD * h:HD * (h + 1)], A.turned_c[0:N_CMP, i % 2, h * P:(h + 1) * P],
                                   A.vc[0:N_CMP, h // HPG, :], start=True, stop=True)
                mm.then_inc(S.pv, 1)

            for i in range(TT):
                if i >= 2:
                    pe.wait_ge(S.mixed, i - 1)
                for h in range(HEADS):
                    rows = slice(HD * (h // HPG), HD * (h // HPG + 1))
                    mm = pe.matmul(M.ps[:, 4 * (i % 2) + 3 * (h // HPG), N_CMP * (h % HPG):N_CMP * (h % HPG + 1)], A.qT[rows, h % HPG, i * P:(i + 1) * P],
                                   A.kcT[rows, :], start=True, stop=True)
                mm.then_inc(S.scores, 1)
                if i >= 1:
                    outputs(i - 1)
            outputs(TT - 1)

        @block.scalar
        def _(act):
            for i in range(TT):
                act.wait_ge(S.shifted, i + 1)
                act.activation(A.score_c[:, i], A.score_c[:, i], ACT.Exp).then_inc(S.probs, 1)

        @block.vector
        def _(dve):
            dve.memset(A.bias_c[:], MASKED).then_inc(S.bias_init, 1)
            dve.wait_ge(S.bias_init, 1)
            for i in range(TT):
                start = (TT - 1 - i) * P + CMP_LEN - 1
                n = min(N_CMP, -(-(T - start) // CMP_STRIDE))
                ins = dve.tensor_copy(A.bias_c[:, i, :, 0:n], A.bias_all[:, :, start:start + CMP_STRIDE * (n - 1) + 1:CMP_STRIDE])
            ins.then_inc(S.bias_c, 1)
            dve.wait_ge(S.bias_c, 1)
            link = chain(dve, S.chain)
            spread = lambda ap: ap.unsqueeze(2).to_broadcast([P, HEADS, N_CMP])

            def probabilities(i):
                s, d = A.score_c[:, i], A.denom_c[:, i, :]
                dve.wait_ge(S.scores, i + 1)
                for g in range(GROUPS):
                    heads = slice(HPG * g, HPG * (g + 1))
                    link(dve.tensor_tensor(s[:, heads], M.ps[:, 4 * (i % 2) + 3 * g, 0:HPG * N_CMP]
                                           .rearrange("p (h n) -> p h n", h=HPG), A.bias_c[:, i, heads], ALU.add))
                link(dve.tensor_reduce(d, s, AX.X, ALU.max))
                link(dve.tensor_scalar(d, d, FLOOR, None, ALU.max))
                dve.tensor_tensor(s, s, spread(d), ALU.subtract).then_inc(S.shifted, 1)

            def normalise(i):
                s, d = A.score_c[:, i], A.denom_c[:, i, :]
                dve.wait_ge(S.probs, i + 1)
                link(dve.tensor_reduce(d, s, AX.X, ALU.add))
                link(dve.tensor_scalar(d, d, 1e-30, None, ALU.max))
                link(dve.reciprocal(d, d))
                gates = A.gates[:, i, :].rearrange("p (h b) -> p h b", b=N_BRANCH)[:, :, 0]
                link(dve.tensor_tensor(d, d, gates, ALU.mult))
                dve.tensor_tensor(s, s, spread(d), ALU.mult).then_inc(S.normed, 1)

            def outputs(i):
                if i >= 2:
                    dve.wait_ge(S.pv, i - 1)
                dve.wait_ge(S.turned, i + 1)
                dve.tensor_copy(A.turned_c[0:N_CMP, i % 2, 0:4 * P], M.ps[0:N_CMP, 4 * (i % 2) + 1, :])
                dve.tensor_copy(A.turned_c[0:N_CMP, i % 2, 4 * P:], M.ps[0:N_CMP, 4 * (i % 2) + 2, :]).then_inc(S.turned_copied, 1)
                dve.wait_ge(S.pv, i + 1)
                dve.tensor_copy(A.mix[:, i, 0:HEADS * HD], M.ps[:, 4 * (i % 2) + 3, :]).then_inc(S.mixed, 1)

            probabilities(0)
            for i in range(TT):
                normalise(i)
                if i + 1 < TT:
                    probabilities(i + 1)
                outputs(i)


def mixer1_attention(nc, M, A):
    units = [(i, h) for i in range(TT) for h in range(HEADS)]
    N = len(units)
    with stage(nc, "attn", "scores score_biased row_max shifted probs turned slc_copied "
               "win_copied pv mixed denominators norm_chain") as (block, S):

        def branch_bias(i, h):
            start = (TT - 1 - i) * P
            return A.bias_all[:, h, start:start + (i + 1) * P]

        @block.tensor
        def _(pe):
            def scores(u):
                i, h = units[u]
                g, a = h // HPG, h % HPG
                rows, keys = slice(HD * g, HD * (g + 1)), (i + 1) * P
                q = A.qT[rows, a, i * P:(i + 1) * P]
                if u >= 2:
                    pe.wait_ge(S.score_biased, u - 1)
                pe.matmul(M.ps[:, 2 * (u % 2), 0:keys], q, A.ksT[rows, 0:keys], start=True, stop=True)
                pe.matmul(M.ps[:, 2 * (u % 2) + 1, 0:keys], q, A.kwT[rows, 0:keys], start=True, stop=True
                          ).then_inc(S.scores, 1)

            def turn(u):
                i, h = units[u]
                pe.wait_ge(S.probs, u + 1)
                if u >= 1:
                    pe.wait_ge(S.slc_copied, u)
                    pe.wait_ge(S.win_copied, u)
                for j in range(i + 1):
                    pe.transpose(M.ps[:, 6, j * P:(j + 1) * P], A.probs[:, u % 2, 0, j * P:(j + 1) * P], M.ident[:])
                for j in range(i + 1):
                    mm = pe.transpose(M.ps[:, 7, j * P:(j + 1) * P], A.probs[:, u % 2, 1, j * P:(j + 1) * P], M.ident[:])
                mm.then_inc(S.turned, 1)

            def values(u):
                i, h = units[u]
                cols = slice(HD * (h // HPG), HD * (h // HPG + 1))
                bank = M.ps[:, 4 + u % 2, :]
                pe.wait_ge(S.slc_copied, u + 1)
                pe.wait_ge(S.win_copied, u + 1)
                if u >= 2:
                    pe.wait_ge(S.mixed, u - 1)
                for j in range(i + 1):
                    pe.matmul(bank[:, 0:HD], A.turned[:, u % 2, 0, j * P:(j + 1) * P], A.vs[:, j, cols],
                              start=(j == 0), stop=(j == i))
                for j in range(i + 1):
                    mm = pe.matmul(bank[:, HD:2 * HD], A.turned[:, u % 2, 1, j * P:(j + 1) * P], A.vw[:, j, cols],
                                   start=(j == 0), stop=(j == i))
                mm.then_inc(S.pv, 1)

            for step in range(N + 2):
                if step < N:
                    scores(step)
                if step >= 2:
                    values(step - 2)
                if 1 <= step <= N:
                    turn(step - 1)

        @block.scalar
        def _(act):
            def exps(u):
                i, h = units[u]
                keys = (i + 1) * P
                act.wait_ge(S.shifted, u + 1)
                if u >= 2:
                    act.wait_ge(S.turned, u - 1)
                for b in range(2):
                    ins = act.activation(A.probs[:, u % 2, b, 0:keys], A.score[:, u % 2, b, 0:keys], ACT.Exp,
                                         bias=A.shift[:, u % 2, b:b + 1], accum_out=A.sums[:, u % 2, b:b + 1])
                ins.then_inc(S.probs, 1)

            def copy(u):
                i, h = units[u]
                act.wait_ge(S.turned, u + 1)
                if u >= 2:
                    act.wait_ge(S.pv, u - 1)
                act.copy(A.turned[:, u % 2, 0, 0:(i + 1) * P], M.ps[:, 6, 0:(i + 1) * P]).then_inc(S.slc_copied, 1)

            for step in range(N + 1):
                if step < N:
                    exps(step)
                if step >= 1:
                    copy(step - 1)

        @block.vector
        def _(dve):
            def biased(u):
                i, h = units[u]
                keys = (i + 1) * P
                dve.wait_ge(S.scores, u + 1)
                if u >= 2:
                    dve.wait_ge(S.probs, u - 1)
                for b in range(2):
                    ins = dve.tensor_tensor_reduce(A.score[:, u % 2, b, 0:keys], M.ps[:, 2 * (u % 2) + b, 0:keys],
                                                   branch_bias(i, h), 1.0, FLOOR, ALU.add, ALU.max,
                                                   A.top[:, u % 2, b:b + 1])
                ins.then_inc(S.score_biased, 1)
                dve.wait_ge(S.score_biased, u + 1)
                dve.tensor_scalar(A.shift[:, u % 2, :], A.top[:, u % 2, :], FLOOR, -1.0, ALU.max, ALU.mult
                                  ).then_inc(S.shifted, 1)

            def copy(u):
                i, h = units[u]
                dve.wait_ge(S.turned, u + 1)
                if u >= 2:
                    dve.wait_ge(S.pv, u - 1)
                dve.tensor_copy(A.turned[:, u % 2, 1, 0:(i + 1) * P], M.ps[:, 7, 0:(i + 1) * P]).then_inc(S.win_copied, 1)

            def combine(u):
                i, h = units[u]
                n = 4 * u
                d, out = A.denom[:, u % 2, :], A.mix[:, i, HD * h:HD * (h + 1)]
                dve.tensor_scalar(d, A.sums[:, u % 2, :], 1e-30, None, ALU.max).then_inc(S.norm_chain, 1)
                dve.wait_ge(S.norm_chain, n + 1)
                dve.reciprocal(d, d).then_inc(S.norm_chain, 1)
                dve.wait_ge(S.norm_chain, n + 2)
                dve.tensor_tensor(d, d, A.gates[:, i, N_BRANCH * h + 1:N_BRANCH * (h + 1)],
                                  ALU.mult).then_inc(S.norm_chain, 1)
                dve.wait_ge(S.norm_chain, n + 3)
                dve.wait_ge(S.pv, u + 1)
                bank = M.ps[:, 4 + u % 2, :]
                dve.scalar_tensor_tensor(out=out, in0=bank[:, 0:HD], scalar=d[:, 0:1], in1=out, op0=ALU.mult,
                                         op1=ALU.add).then_inc(S.norm_chain, 1)
                dve.wait_ge(S.norm_chain, n + 4)
                dve.scalar_tensor_tensor(out=out, in0=bank[:, HD:2 * HD], scalar=d[:, 1:2], in1=out, op0=ALU.mult,
                                         op1=ALU.add).then_inc(S.mixed, 1)

            for step in range(N + 2):
                if step >= 2:
                    combine(step - 2)
                if step < N:
                    biased(step)
                if 1 <= step <= N:
                    copy(step - 1)


def mixer1_ssd(nc, M, A):
    hpg = SH // SG
    with stage(nc, "ssd", "x_turned x_copied sums_col col_copied sums_row cb diff decay kept weighted "
               "y_ready chain squares_done root_ready gated") as (block, S):
        tri = lambda k, n0, n1: M.tri[:, 3 * P - k * P + n0:3 * P - k * P + n1]
        steps = [(g, k) for g in range(SG) for k in range(TT)]

        @block.tensor
        def _(pe):
            for c in range(2):
                for i in range(TT):
                    mm = pe.transpose(M.ps[:, c, i * P:(i + 1) * P], A.xbc[:, c, i * P:(i + 1) * P], M.ident[:])
                mm.then_inc(S.x_turned, 1)
            for k in range(TT):
                for j in range(k + 1):
                    mm = pe.matmul(M.ps[:, 2, SH * k:SH * (k + 1)], tri(j, k * P, (k + 1) * P), A.a[:, j, :],
                                   start=(j == 0), stop=(j == k))
            mm.then_inc(S.sums_col, 1)
            for h in range(SH):
                for j in range(TT):
                    mm = pe.matmul(M.ps[:, 4 + h, :], A.a[:, j, h:h + 1].to_broadcast([P, P]), tri(j, 0, T),
                                   start=(j == 0), stop=(j == TT - 1))
                mm.then_inc(S.sums_row, 1)
            pe.wait_ge(S.x_copied, 2)
            for n, (g, k) in enumerate(steps):
                if n >= 2:
                    pe.wait_ge(S.weighted, hpg * (n - 1))
                if n < 2:
                    pe.wait_ge(S.col_copied, 1)
                pe.matmul(M.ps[:, n % 2, k * P:T], A.xbc[:, 2 + g, k * P:(k + 1) * P], A.xbc[:, 2 + SG + g, k * P:T],
                          start=True, stop=True).then_inc(S.cb, 1)
            pe.wait_ge(S.weighted, hpg * len(steps))
            for i in range(TT):
                for h in range(SH):
                    for k in range(i + 1):
                        mm = pe.matmul(M.ps[:, 2 + i // 2, (i % 2) * 256 + HD * h:(i % 2) * 256 + HD * (h + 1)],
                                       A.decay[:, h, k, i * P:(i + 1) * P], A.xdt[:, k, h * HD:(h + 1) * HD],
                                       start=(k == 0), stop=(k == i))
            mm.then_inc(S.y_ready, 1)

        @block.scalar
        def _(act):
            n = 0
            for g, k in steps:
                for h in range(hpg * g, hpg * (g + 1)):
                    n += 1
                    act.wait_ge(S.diff, n)
                    act.activation(A.decay[:, h, k, k * P:T], A.decay[:, h, k, k * P:T], ACT.Exp).then_inc(S.decay, 1)
            act.wait_ge(S.squares_done, 1)
            act.activation(A.root[:], A.root[:], ACT.Sqrt).then_inc(S.root_ready, 1)

        @block.vector
        def _(dve):
            link = chain(dve, S.chain)
            for c in range(2):
                dve.wait_ge(S.x_turned, c + 1)
                dve.tensor_copy(A.xs[:, :, c * P:(c + 1) * P], M.ps[:, c, :].rearrange("p (i d) -> p i d", i=TT)
                                ).then_inc(S.x_copied, 1)
            dve.wait_ge(S.x_copied, 2)
            link(dve.tensor_tensor(A.xdt[:].rearrange("p i (h d) -> p (i h) d", h=SH),
                                   A.xs[:].rearrange("p i (h d) -> p (i h) d", h=SH),
                                   A.dt[:].rearrange("p i h -> p (i h)").unsqueeze(2).to_broadcast([P, TT * SH, HD]), ALU.mult))
            dve.wait_ge(S.sums_col, 1)
            dve.tensor_copy(A.cs[:], M.ps[:, 2, 0:SH * TT]).then_inc(S.col_copied, 1)
            dve.wait_ge(S.col_copied, 1)
            units = [(g, k, h) for g, k in steps for h in range(hpg * g, hpg * (g + 1))]

            def difference(n):
                g, k, h = units[n]
                dve.wait_ge(S.sums_row, h + 1)
                dve.tensor_scalar(A.decay[:, h, k, k * P:T], M.ps[:, 4 + h, k * P:T], A.cs[:, SH * k + h:SH * k + h + 1],
                                  0.0, ALU.subtract, ALU.min).then_inc(S.diff, 1)

            def weigh(n):
                g, k, h = units[n]
                dve.wait_ge(S.decay, n + 1)
                dve.wait_ge(S.cb, n // hpg + 1)
                link(dve.tensor_tensor(A.decay[:, h, k, k * P:T], A.decay[:, h, k, k * P:T], tri(0, 0, T - k * P), ALU.mult))
                dve.tensor_tensor(A.decay[:, h, k, k * P:T], A.decay[:, h, k, k * P:T], M.ps[:, (n // hpg) % 2, k * P:T],
                                  ALU.mult).then_inc(S.weighted, 1)

            difference(0)
            difference(1)
            for n in range(len(units)):
                if n + 2 < len(units):
                    difference(n + 2)
                weigh(n)
            out = A.mix[:, :, HEADS * HD + D_GMLP:]
            heads = lambda ap: ap.rearrange("p i (h d) -> p i h d", h=SH)
            for i in range(TT):
                link(dve.tensor_tensor(out[:, i, :].rearrange("p (h d) -> p h d", h=SH),
                                       A.xs[:, i, :].rearrange("p (h d) -> p h d", h=SH),
                                       A.d_skip[:].unsqueeze(2).to_broadcast([P, SH, HD]), ALU.mult))
            dve.wait_ge(S.y_ready, 1)
            for i in range(2):
                pair = out[:, 2 * i:2 * i + 2, :]
                link(dve.tensor_tensor(pair, pair, M.ps[:, 2 + i, :].rearrange("p (i d) -> p i d", i=2), ALU.add))
            link(dve.tensor_tensor(out, out, A.silz[:], ALU.mult))
            link(dve.tensor_tensor(A.xdt[:], out, out, ALU.mult))
            link(dve.tensor_reduce(A.root[:], A.xdt[:].rearrange("p i (g d) -> p (i g) d", g=SG), AX.X, ALU.add))
            dve.tensor_scalar(A.root[:], A.root[:], SG / D_SSM, LN_EPS, ALU.mult, ALU.add).then_inc(S.squares_done, 1)
            dve.wait_ge(S.root_ready, 1)
            link(dve.reciprocal(A.root[:], A.root[:]))
            for i in range(TT):
                o = out[:, i, :]
                og = o.rearrange("p (g d) -> p g d", g=SG)
                link(dve.tensor_tensor(og, og, A.root[:, SG * i:SG * (i + 1)].unsqueeze(2).to_broadcast([P, SG, D_SSM // SG]),
                                       ALU.mult))
                link(dve.tensor_tensor(o, o, A.norm_g[:], ALU.mult))


def mix_out(nc, M, tag, mix, turned, w_out, sub):
    w = w_out.rearrange("(k p) n -> p k n", p=P)
    wide = M.wide[:].rearrange("p s a k n -> p (s a k n)").rearrange("p (k n) -> p k n", k=DT)
    with stage(nc, tag, "w0_landed w1_landed mix_turned mix_copied y_ready" + NORM_SIGNALS) as (block, S):
        landed = [S.w0_landed, S.w1_landed]
        tiles = [k for k in range(DT) if k not in turned]

        @block.sync
        def _(sp):
            for s in range(2):
                sp.dma_start(wide[:, 4 * s:4 * s + 4, :], w[:, 4 * s:4 * s + 4, :]).then_inc(landed[s], 16)

        @block.tensor
        def _(pe):
            for n, k in enumerate(tiles):
                for i in range(TT):
                    mm = pe.transpose(M.ps[:, n, i * P:(i + 1) * P], mix[:, i, k * P:(k + 1) * P], M.ident[:])
                mm.then_inc(S.mix_turned, 1)
            pe.wait_ge(S.mix_copied, len(tiles))
            pe.wait_ge(landed[0], 16)
            pe.wait_ge(landed[1], 16)
            for d in range(DT):
                for k in range(DT):
                    mm = pe.matmul(M.ps[:, d, :], wide[:, k, d * P:(d + 1) * P], M.hT[:, k, :], start=(k == 0),
                                   stop=(k == DT - 1))
                mm.then_inc(S.y_ready, 1)
            if sub is not None:
                post_norm_pe(pe, M, S)

        @block.scalar
        def _(act):
            for n, k in enumerate(tiles):
                if n % 2:
                    act.wait_ge(S.mix_turned, n + 1)
                    act.copy(M.hT[:, k, :], M.ps[:, n, :]).then_inc(S.mix_copied, 1)
            if sub is not None:
                post_norm_act(act, M, S)

        @block.vector
        def _(dve):
            for n, k in enumerate(tiles):
                if n % 2 == 0:
                    dve.wait_ge(S.mix_turned, n + 1)
                    dve.tensor_copy(M.hT[:, k, :], M.ps[:, n, :]).then_inc(S.mix_copied, 1)
            if sub is not None:
                post_norm_dve(dve, M, S, sub)
            else:
                for d in range(DT):
                    dve.wait_ge(S.y_ready, d + 1)
                    dve.tensor_tensor(M.x[:, d, :], M.x[:, d, :], M.ps[:, d, :], ALU.add)


def mixer1(nc, M, I, l):
    with ExitStack() as memory:
        sb = tensors(nc, memory, "a_")
        A = Memory()
        A.bias_all = M.bias
        A.mix = sb("mix", TT, D)
        A.qT = sb("qT", HPG, T)
        A.ksT, A.kwT = sb("ksT", T), sb("kwT", T)
        A.vs, A.vw = sb("vs", TT, KV), sb("vw", TT, KV)
        A.gates = sb("gates", TT, HEADS * N_BRANCH)
        A.kcT, A.vc = sb("kcT", N_CMP), sb("vc", GROUPS, HD)
        A.silz, A.dt, A.a = sb("silz", TT, D_SSM), sb("dt", TT, SH), sb("a", TT, SH)
        A.xbc = sb("xbc", XT, T)
        A.d_skip, A.norm_g = sb("d_skip", SH), sb("norm_g", D_SSM)
        A.root = sb("root", TT * SG)
        with ExitStack() as inner:
            sb = tensors(nc, inner, "a_")
            A.uv = sb("uv", TT, 2 * D_GMLP)
            A.raw = sb("raw", XT, T + SCONV - 1)
            A.blk = sb("blk", 2, CMP_LEN, N_CMP + 1)
            A.cmp_b, A.cmp_w2 = sb("cmp_b", 4), sb("cmp_w2", 2, 2, GROUPS, HD)
            A.cmp_h = sb("cmp_h", 2, 2, GROUPS, N_CMP)
            A.conv_w, A.conv_b = sb("conv_w", SCONV, XT), sb("conv_b", XT)
            A.ws, A.wsT, A.ws_b = sb("ws", GG, P), sb("wsT", GG, P), sb("ws_b", GG)
            A.ln_g, A.ln_b = sb("ln_g", D_GMLP), sb("ln_b", D_GMLP)
            A.dt_bias, A.a_log, A.a_neg = sb("dt_bias", SH), sb("a_log", SH), sb("a_neg", SH)
            A.dt_e, A.dt_u, A.dt_r, A.dt_ln = (sb(f"dt_{x}", TT, SH) for x in "eurl")
            A.stats, A.mv = sb("stats", TT, 6), sb("mv", TT, 2)
            mixer1_project(nc, M, A, I, l)
            mixer1_local(nc, M, A, I, l)
        with ExitStack() as inner:
            sb = tensors(nc, inner, "a_")
            A.bias_c, A.score_c = sb("bias_c", TT, HEADS, N_CMP), sb("score_c", TT, HEADS, N_CMP)
            A.turned_c, A.denom_c = sb("turned_c", 2, HEADS * P), sb("denom_c", TT, HEADS)
            mixer1_compressed(nc, M, A)
        with ExitStack() as inner:
            sb = tensors(nc, inner, "a_")
            A.score, A.probs, A.turned = sb("score", 2, 2, T), sb("probs", 2, 2, T), sb("turned", 2, 2, T)
            A.top, A.shift, A.sums, A.denom = (sb(x, 2, 2) for x in ("top", "shift", "sums", "denom"))
            mixer1_attention(nc, M, A)
        with ExitStack() as inner:
            sb = tensors(nc, inner, "a_")
            A.xs, A.xdt = sb("xs", TT, D_SSM), sb("xdt", TT, D_SSM)
            A.cs = sb("cs", TT * SH)
            A.decay = sb("decay", SH, TT, T)
            mixer1_ssd(nc, M, A)
        mix_out(nc, M, "out1", A.mix, (), I.w_out[l], 1)


def sum_selectors():
    out = np.zeros((P, 7 * 32), np.float32)
    out[:, 96:128] = 1
    return out


def spread_selectors():
    out = np.zeros((P, 4, P), np.float32)
    for u in range(4):
        out[32 * u, u] = 1
    return out


def rms(nc, M, tag, gain):
    with stage(nc, tag, "gain_landed square_ready square_used mean_copied root_ready rstd_ready") as (block, S):

        @block.sync
        def _(sp):
            with nc.allow_non_contiguous_dma(reason="one vector as columns"):
                sp.dma_start(M.gain[:], gain.rearrange("(d p) -> p d", p=P)).then_inc(S.gain_landed, 16)

        @block.scalar
        def _(act):
            for d in range(DT):
                if d >= 2:
                    act.wait_ge(S.square_used, d - 1)
                act.activation(M.sq[:, d % 2, :], M.x[:, d, :], ACT.Square).then_inc(S.square_ready, 1)
            act.wait_ge(S.mean_copied, 1)
            act.activation(M.rstd[:], M.rstd[:], ACT.Sqrt).then_inc(S.root_ready, 1)

        @block.tensor
        def _(pe):
            for d in range(DT):
                pe.wait_ge(S.square_ready, d + 1)
                pe.matmul(M.ps[:, 0, :], M.mean_d[:], M.sq[:, d % 2, :], start=(d == 0),
                          stop=(d == DT - 1)).then_inc(S.square_used, 1)

        @block.vector
        def _(dve):
            dve.wait_ge(S.square_used, DT)
            dve.tensor_scalar(M.rstd[:], M.ps[:, 0, :], RMS_EPS, None, ALU.add).then_inc(S.mean_copied, 1)
            dve.wait_ge(S.root_ready, 1)
            dve.reciprocal(M.rstd[:], M.rstd[:]).then_inc(S.rstd_ready, 1)
            dve.wait_ge(S.rstd_ready, 1)
            dve.wait_ge(S.gain_landed, 16)
            for d in range(DT):
                dve.scalar_tensor_tensor(out=M.hT[:, d, :], in0=M.x[:, d, :], scalar=M.gain[:, d:d + 1], in1=M.rstd[:],
                                         op0=ALU.mult, op1=ALU.mult)


def mixer2_project(nc, M, A, I, l):
    w = I.w_in_2[l].rearrange("(k p) n -> p k n", p=P)
    z, ba = 3 * DW, 4 * DW
    sc = ba + 2 * DH
    bounds = [0, DW, 2 * DW, z, ba, sc, sc + SCW, sc + 2 * SCW, W2_COLS]
    chunks = [[(slice(0, b - a), w[:, :, a:b])] for a, b in zip(bounds, bounds[1:])]
    cols = lambda a, n: slice(a, a + n)

    def act_copy(dst):
        return lambda act, ps, i: act.copy(dst, ps)

    def dve_copy(dst):
        return lambda dve, ps, i: dve.tensor_copy(dst, ps)

    tiles = []
    for c in range(3):
        for h in range(DH):
            dst = A.raw[:, DH * c + h, DCONV - 1:]
            tiles.append((c, cols(P * h, P), None, "dve" if h % 2 else "act", (dve_copy if h % 2 else act_copy)(dst)))
    tiles += [(3, cols(0, DW), i, "act", lambda act, ps, i: act.activation(A.silz[:, i, :], ps, ACT.Silu)) for i in range(TT)]
    tiles += [(4, cols(0, 2 * DH), i, "dve", lambda dve, ps, i: dve.tensor_copy(A.ba[:, i, :], ps[:, 0:2 * DH]))
              for i in range(TT)]
    tiles += [(5, cols(P * c, P), None, "dve", dve_copy(A.gate_b[:, c, :])) for c in range(SCT)]
    tiles += [(6, cols(P * c, P), None, "act", act_copy(A.gate_c[:, c, :])) for c in range(SCT)]
    tiles += [(7, cols(P * c, P), None, "dve", dve_copy(A.prod[:, c, SCCONV - 1:])) for c in range(SCT)]
    project(nc, M, "proj2", chunks, tiles, None)


def mixer2_conv(nc, M, A, I, l):
    with stage(nc, "conv2", "small_landed padded conv conv_y gated silu_done square_ready square_used summed root_ready "
               "inverse_ready spread scaled act_chain dve_chain exp_ready one_plus ln_ready") as (block, S):

        @block.sync
        def _(sp):
            with nc.allow_non_contiguous_dma(reason="small vectors as columns"):
                for j in range(DCONV):
                    sp.dma_start(A.conv_w[:, j, :], I.dn_conv_w_2[l, j].rearrange("(c p) -> p c", p=P)).then_inc(S.small_landed, 16)
                for j in range(SCCONV):
                    sp.dma_start(A.sc_w[:, j, :], I.sc_conv_w_2[l, j].rearrange("(c p) -> p c", p=P)).then_inc(S.small_landed, 16)
                sp.dma_start(A.sc_g[:], I.sc_norm_g_2[l].rearrange("(c p) -> p c", p=P)).then_inc(S.small_landed, 16)
            for dst, vector in ((A.dt_bias, I.dn_dt_bias_2), (A.a_log, I.dn_a_log_2), (A.norm_g, I.dn_norm_g_2)):
                sp.dma_start(dst[:], vector[l].partition_broadcast(P)).then_inc(S.small_landed, 16)
            sp.wait_ge(S.small_landed, 16 * (DCONV + SCCONV + 4))

        small = 16 * (DCONV + SCCONV + 4)
        normed = [A.qkv[:, u, :] for u in range(2 * DH)] + [A.gate_c[:, c, :] for c in range(SCT)]

        @block.tensor
        def _(pe):
            def spread(g):
                pe.wait_ge(S.inverse_ready, g + 1)
                for u in range(4):
                    n = 4 * g + u
                    if n >= 4:
                        pe.wait_ge(S.scaled, n - 3)
                    pe.matmul(M.ps[:, 4 + u, :], M.spread_sel[:, u, :], A.inverse[:, g, :], start=True,
                              stop=True).then_inc(S.spread, 1)

            for g in range(3):
                for u in range(4):
                    pe.wait_ge(S.square_ready, 4 * g + u + 1)
                    pe.matmul(M.ps[:, g, :], M.sum_sel[:, 96 - 32 * u:224 - 32 * u], M.sq[:, u % 2, :], start=(u == 0),
                              stop=(u == 3)).then_inc(S.square_used, 1)
                if g >= 1:
                    spread(g - 1)
            spread(2)

        @block.scalar
        def _(act):
            act.wait_ge(S.small_landed, small)
            link = chain(act, S.act_chain)
            link(act.activation(A.a_neg[:], A.a_log[:], ACT.Exp))
            act.wait_ge(S.one_plus, 1)
            act.activation(A.dt_e[:], A.dt_e[:], ACT.Exp, scale=-1.0).then_inc(S.exp_ready, 1)
            act.wait_ge(S.one_plus, 2)
            act.activation(A.dt_ln[:], A.dt_u[:], ACT.Ln).then_inc(S.ln_ready, 1)
            link(act.activation(A.beta[:], A.ba[:, :, 0:DH], ACT.Sigmoid))

            def square(n):
                if n >= 2:
                    act.wait_ge(S.square_used, n - 1)
                act.activation(M.sq[:, n % 2, :], normed[n], ACT.Square).then_inc(S.square_ready, 1)

            def silu(u):
                act.wait_ge(S.conv, DCONV * (u + 1))
                act.activation(A.qkv[:, u, :], A.qkv[:, u, :], ACT.Silu).then_inc(S.silu_done, 1)

            for u in range(2 * DH):
                silu(u)
                if u:
                    act.wait_ge(S.silu_done, u)
                    square(u - 1)
            act.wait_ge(S.silu_done, 2 * DH)
            square(2 * DH - 1)
            for u in range(2 * DH, 3 * DH):
                silu(u)
            for g in range(3):
                if g == 2:
                    for c in range(SCT):
                        act.wait_ge(S.gated, c + 1)
                        square(2 * DH + c)
                act.wait_ge(S.summed, g + 1)
                act.activation(A.inverse[:, g, :], A.inverse[:, g, :], ACT.Sqrt).then_inc(S.root_ready, 1)

        @block.vector
        def _(dve):
            link = chain(dve, S.dve_chain)
            dve.memset(A.raw[:, :, 0:DCONV - 1], 0.0).then_inc(S.padded, 1)
            dve.memset(A.prod[:, :, 0:SCCONV - 1], 0.0).then_inc(S.padded, 1)
            dve.wait_ge(S.small_landed, small)
            link(dve.tensor_tensor(A.g[:], A.ba[:, :, DH:], A.dt_bias[:].unsqueeze(1).to_broadcast([P, TT, DH]), ALU.add))
            dve.scalar_tensor_tensor(out=A.dt_e[:], in0=A.g[:], scalar=-1.0, in1=A.g[:], op0=ALU.mult,
                                     op1=ALU.max).then_inc(S.one_plus, 1)
            dve.wait_ge(S.exp_ready, 1)
            dve.tensor_scalar(A.dt_u[:], A.dt_e[:], 1.0, None, ALU.add).then_inc(S.one_plus, 1)
            dve.wait_ge(S.one_plus, 2)
            link(dve.scalar_tensor_tensor(out=A.dt_r[:], in0=A.dt_u[:], scalar=-1.0, in1=A.dt_e[:], op0=ALU.add,
                                          op1=ALU.subtract))
            link(dve.tensor_scalar(A.g[:], A.g[:], 0.0, None, ALU.max))
            link(dve.tensor_tensor(A.g[:], A.g[:], A.dt_r[:], ALU.subtract))
            dve.wait_ge(S.ln_ready, 1)
            link(dve.tensor_tensor(A.g[:], A.g[:], A.dt_ln[:], ALU.add))
            dve.wait_ge(S.act_chain, 1)
            link(dve.scalar_tensor_tensor(out=A.g[:], in0=A.g[:], scalar=-1.0,
                                          in1=A.a_neg[:].unsqueeze(1).to_broadcast([P, TT, DH]),
                                          op0=ALU.mult, op1=ALU.mult))
            dve.wait_ge(S.padded, 2)

            def convolve(u):
                dve.tensor_scalar(A.qkv[:, u, :], A.raw[:, u, 0:T], A.conv_w[:, 0, u:u + 1], None, ALU.mult).then_inc(S.conv, 1)
                for j in range(1, DCONV):
                    dve.wait_ge(S.conv, DCONV * u + j)
                    dve.scalar_tensor_tensor(out=A.qkv[:, u, :], in0=A.raw[:, u, j:j + T], scalar=A.conv_w[:, j, u:u + 1],
                                             in1=A.qkv[:, u, :], op0=ALU.mult, op1=ALU.add).then_inc(S.conv, 1)

            affine = [(RMS_EPS, float(DHD)), (RMS_EPS, 1.0), (P * RMS_EPS, 1.0 / P)]

            def root(g):
                dve.wait_ge(S.square_used, 4 * (g + 1))
                dve.tensor_scalar(A.inverse[:, g, :], M.ps[:, g, :], affine[g][0], affine[g][1], ALU.add,
                                  ALU.mult).then_inc(S.summed, 1)

            def inverse(g):
                dve.wait_ge(S.root_ready, g + 1)
                dve.reciprocal(A.inverse[:, g, :], A.inverse[:, g, :]).then_inc(S.inverse_ready, 1)

            def scale(g):
                for u in range(4):
                    n = 4 * g + u
                    dve.wait_ge(S.spread, n + 1)
                    if g < 2:
                        dve.tensor_tensor(normed[n], normed[n], M.ps[:, 4 + u, :], ALU.mult).then_inc(S.scaled, 1)
                    else:
                        dve.scalar_tensor_tensor(out=M.hT[:, DT - SCT + u, :], in0=normed[n], scalar=A.sc_g[:, u:u + 1],
                                                 in1=M.ps[:, 4 + u, :], op0=ALU.mult, op1=ALU.mult).then_inc(S.scaled, 1)

            for u in range(2 * DH):
                convolve(u)
            for c in range(SCT):
                x, y = A.prod[:, c, :], A.gate_c[:, c, :]
                link(dve.tensor_tensor(x[:, SCCONV - 1:], x[:, SCCONV - 1:], y, ALU.mult))
                link(dve.tensor_scalar(y, x[:, 0:T], A.sc_w[:, 0, c:c + 1], None, ALU.mult))
                for j in range(1, SCCONV):
                    link(dve.scalar_tensor_tensor(out=y, in0=x[:, j:j + T], scalar=A.sc_w[:, j, c:c + 1], in1=y,
                                                  op0=ALU.mult, op1=ALU.add))
                dve.tensor_tensor(y, y, A.gate_b[:, c, :], ALU.mult).then_inc(S.gated, 1)
            root(0)
            root(1)
            for u in range(2 * DH, 3 * DH):
                convolve(u)
            inverse(0)
            inverse(1)
            root(2)
            scale(0)
            inverse(2)
            scale(1)
            scale(2)


def mixer2_delta(nc, M, A):
    with stage(nc, "delta", "sums chain gains gain_exp beta_rows g_rows g_copied diff decay e_rows rows_exp kk qk "
               "lt_ready qk_ready k_turned v_turned nat_ready masked t1 t1_copied x_up y_up xy_ready u_ready w_ready u_copied w_copied "
               "ws v_new o o_copied s_add s_ready o_chain root_in root_ready prep_free") as (block, S):
        tri = M.tri[:, 3 * P:4 * P]
        head = lambda ap, h: ap[:, h * P:(h + 1) * P]
        heads = lambda ap: ap.rearrange("p (h c) -> p h c", h=DH)
        cols = lambda ap, i: ap[:, DH * i:DH * (i + 1)].unsqueeze(2).to_broadcast([P, DH, P])
        g_all = A.g[:].rearrange("p i h -> p (i h)")
        beta_all = A.beta[:].rearrange("p i h -> p (i h)")
        q, k, v = (A.qkv[:, DH * n:DH * (n + 1), :] for n in range(3))
        tok = lambda ap, h, i: ap[:, h, i * P:(i + 1) * P]
        X = k.rearrange("p h t -> p (h t)").rearrange("p (i n) -> p i n", i=TT)
        Y = v.rearrange("p h t -> p (h t)").rearrange("p (i n) -> p i n", i=TT)

        @block.tensor
        def _(pe):
            pe.matmul(M.ps[:, 7, 0:16], tri, g_all, start=True, stop=True)
            pe.matmul(M.ps[:, 7, 16:32], M.ones[:], g_all, start=True, stop=True).then_inc(S.sums, 1)
            for i in range(TT):
                if i >= 1:
                    pe.wait_ge(S.prep_free, i)
                for h in range(DH):
                    mm = pe.matmul(head(M.ps[:, 0], h), g_all[:, DH * i + h:DH * i + h + 1].to_broadcast([P, P]), tri,
                                   start=True, stop=True)
                mm.then_inc(S.g_rows, 1)
                for h in range(DH):
                    pe.matmul(head(M.ps[:, 1], h), beta_all[:, DH * i + h:DH * i + h + 1].to_broadcast([P, P]), M.ident[:],
                              start=True, stop=True)
                for h in range(DH):
                    mm = pe.matmul(head(M.ps[:, 2], h), tok(k, h, i), tok(k, h, i), start=True, stop=True)
                mm.then_inc(S.kk, 1)
                for h in range(DH):
                    mm = pe.matmul(head(M.ps[:, 3], h), tok(k, h, i), tok(q, h, i), start=True, stop=True)
                mm.then_inc(S.qk, 1)
                for h in range(DH):
                    mm = pe.transpose(head(M.ps[:, 4], h), tok(k, h, i), M.ident[:])
                mm.then_inc(S.k_turned, 1)
                for h in range(DH):
                    mm = pe.transpose(head(M.ps[:, 5], h), tok(v, h, i), M.ident[:])
                mm.then_inc(S.v_turned, 1)
            pe.wait_ge(S.prep_free, TT)
            for n in range(LEVELS):
                for i in range(TT):
                    pe.wait_ge(S.masked, TT * n + i + 1)
                    if n:
                        pe.wait_ge(S.xy_ready, TT * (n - 1) + i + 1)
                    for h in range(DH):
                        mm = pe.matmul(head(M.ps[:, 2 * i], h), head(A.BT[:, i], h), head(X[:, i], h) if n else M.ident[:],
                                       start=True, stop=True)
                    mm.then_inc(S.t1, 1)
                for i in range(TT):
                    if n:
                        pe.wait_ge(S.t1_copied, TT * (n - 1) + i + 1)
                        if n < LEVELS - 1:
                            for h in range(DH):
                                pe.matmul(head(M.ps[:, 2 * i + 1], h), head(Y[:, i], h), head(A.T1[:, i], h), start=True,
                                          stop=True)
                        for h in range(DH):
                            mm = pe.matmul(head(M.ps[:, 2 * i], h), head(A.T1[:, i], h), head(Y[:, i], h), start=True,
                                           stop=True)
                        mm.then_inc(S.x_up, 1)
            for i in range(TT):
                pe.wait_ge(S.xy_ready, TT * (LEVELS - 1) + i + 1)
                for h in range(DH):
                    mm = pe.matmul(head(M.ps[:, 2 * i], h), head(Y[:, i], h), head(A.vb[:, i], h), start=True, stop=True)
                mm.then_inc(S.u_ready, 1)
                for h in range(DH):
                    mm = pe.matmul(head(M.ps[:, 2 * i + 1], h), head(A.kbg[:, i], h), head(Y[:, i], h), start=True, stop=True)
                mm.then_inc(S.w_ready, 1)
            pe.wait_ge(S.u_copied, TT)
            pe.wait_ge(S.w_copied, TT)
            for i in range(TT):
                if i:
                    pe.wait_ge(S.s_ready, i)
                    for h in range(DH):
                        mm = pe.matmul(head(M.ps[:, 0], h), head(A.wT[:, i], h), head(A.state, h), start=True, stop=True)
                    mm.then_inc(S.ws, 1)
                    pe.wait_ge(S.v_new, i)
                if i >= 2:
                    pe.wait_ge(S.o_copied, i - 1)
                vn = A.v_new if i else A.u[:, 0]
                for h in range(DH):
                    if i:
                        pe.matmul(head(M.ps[:, 1 + i % 2], h), tok(q, h, i), head(A.state, h), start=True, stop=False)
                    mm = pe.matmul(head(M.ps[:, 1 + i % 2], h), head(A.qk[:, i], h), head(vn, h), start=(i == 0), stop=True)
                mm.then_inc(S.o, 1)
                if i < TT - 1:
                    for h in range(DH):
                        mm = pe.matmul(head(M.ps[:, 3], h), head(A.kdec[:, i], h), head(vn, h), start=True, stop=True)
                    mm.then_inc(S.s_add, 1)

        @block.scalar
        def _(act):
            act.wait_ge(S.gains, 1)
            act.activation(A.gain[:], A.gain[:], ACT.Exp).then_inc(S.gain_exp, 1)
            for i in range(TT):
                act.wait_ge(S.g_rows, i + 1)
                act.activation(A.rows[:], M.ps[:, 0], ACT.Exp).then_inc(S.rows_exp, 1)
                act.wait_ge(S.diff, i + 1)
                act.activation(A.D[:, i], A.D[:, i], ACT.Exp).then_inc(S.decay, 1)
                act.wait_ge(S.prep_free, i + 1)
            for n in range(1, LEVELS):
                for i in range(TT):
                    act.wait_ge(S.t1, TT * n + i + 1)
                    if n > 1:
                        act.wait_ge(S.x_up, TT * (n - 2) + i + 1)
                    act.copy(A.T1[:, i], M.ps[:, 2 * i]).then_inc(S.t1_copied, 1)
            for i in range(TT):
                act.wait_ge(S.w_ready, i + 1)
                act.copy(A.wT[:, i], M.ps[:, 2 * i + 1]).then_inc(S.w_copied, 1)
            act.wait_ge(S.root_in, 1)
            act.activation(A.root[:], A.root[:], ACT.Sqrt).then_inc(S.root_ready, 1)

        @block.vector
        def _(dve):
            link = chain(dve, S.chain)
            dve.wait_ge(S.sums, 1)
            link(dve.tensor_copy(A.G[:], M.ps[:, 7, 0:16]))
            link(dve.tensor_copy(A.gain[:, 0:16], M.ps[:, 7, 0:16]))
            link(dve.tensor_tensor(A.gain[:, 16:32], M.ps[:, 7, 16:32], A.G[:], ALU.subtract))
            dve.tensor_copy(A.gain[:, 32:48], M.ps[:, 7, 16:32]).then_inc(S.gains, 1)
            dve.wait_ge(S.gain_exp, 1)
            link(dve.tensor_tensor(A.bg[:], A.gain[:, 0:16], beta_all, ALU.mult))
            for i in range(TT):
                D, LT = A.D[:, i], A.LT[:, i]
                dve.wait_ge(S.rows_exp, i + 1)
                link(dve.tensor_tensor(heads(D), heads(M.ps[:, 0]), cols(A.G, i), ALU.subtract))
                dve.scalar_tensor_tensor(out=heads(D), in0=heads(D), scalar=0.0, in1=M.mask_neg[:].unsqueeze(1).to_broadcast(
                    [P, DH, P]), op0=ALU.min, op1=ALU.add).then_inc(S.diff, 1)
                dve.wait_ge(S.decay, i + 1)
                dve.wait_ge(S.kk, i + 1)
                link(dve.tensor_tensor(LT, M.ps[:, 2], D, ALU.mult))
                link(dve.tensor_tensor(LT, LT, M.ps[:, 1], ALU.mult))
                dve.wait_ge(S.qk, i + 1)
                dve.tensor_tensor(A.qk[:, i], M.ps[:, 3], D, ALU.mult)
                dve.tensor_tensor(q[:, :, i * P:(i + 1) * P], q[:, :, i * P:(i + 1) * P], heads(A.rows[:]), ALU.mult)
                dve.wait_ge(S.k_turned, i + 1)
                dve.tensor_tensor(heads(A.kbg[:, i]), heads(M.ps[:, 4]), cols(A.bg, i), ALU.mult)
                dve.tensor_tensor(heads(A.kdec[:, i]), heads(M.ps[:, 4]), cols(A.gain[:, 16:32], i), ALU.mult)
                dve.wait_ge(S.v_turned, i + 1)
                dve.tensor_tensor(heads(A.vb[:, i]), heads(M.ps[:, 5]), cols(beta_all, i), ALU.mult).then_inc(S.prep_free, 1)
            dve.wait_ge(S.prep_free, TT)
            for n in range(LEVELS):
                mask = M.levels[:, n, :].unsqueeze(1).to_broadcast([P, DH, P])
                eye = M.ident[:].unsqueeze(1).to_broadcast([P, DH, P])
                for i in range(TT):
                    if n:
                        dve.wait_ge(S.t1, TT * (n - 1) + i + 1)
                    dve.tensor_tensor(heads(A.BT[:, i]), heads(A.LT[:, i]), mask, ALU.mult).then_inc(S.masked, 1)
                    if n == 0:
                        dve.wait_ge(S.masked, i + 1)
                        link(dve.tensor_tensor(heads(Y[:, i]), eye, heads(A.BT[:, i]), ALU.subtract))
                for i in range(TT):
                    if n == 0:
                        dve.wait_ge(S.t1, i + 1)
                        dve.tensor_tensor(heads(X[:, i]), eye, heads(M.ps[:, 2 * i]), ALU.subtract).then_inc(S.xy_ready, 1)
                    else:
                        dve.wait_ge(S.xy_ready, TT * (n - 1) + i + 1)
                        dve.wait_ge(S.x_up, TT * (n - 1) + i + 1)
                        if n < LEVELS - 1:
                            dve.tensor_tensor(X[:, i], X[:, i], M.ps[:, 2 * i + 1], ALU.subtract)
                        dve.tensor_tensor(Y[:, i], Y[:, i], M.ps[:, 2 * i], ALU.subtract).then_inc(S.xy_ready, 1)
            for i in range(TT):
                dve.wait_ge(S.u_ready, i + 1)
                dve.tensor_copy(A.u[:, i], M.ps[:, 2 * i]).then_inc(S.u_copied, 1)

            def output(i):
                dve.wait_ge(S.o, i + 1)
                dve.tensor_copy(A.mix[:, i, :], M.ps[:, 1 + i % 2]).then_inc(S.o_copied, 1)

            state, vn = heads(A.state[:]), A.v_new[:]
            for i in range(TT):
                if i:
                    dve.wait_ge(S.ws, i)
                    dve.tensor_tensor(vn, A.u[:, i], M.ps[:, 0], ALU.subtract).then_inc(S.v_new, 1)
                if i < TT - 1:
                    dve.wait_ge(S.s_add, i + 1)
                    if i:
                        dve.wait_ge(S.o, i + 1)
                        dve.wait_ge(S.s_ready, i)
                        link(dve.tensor_tensor(state, state, cols(A.gain[:, 32:48], i), ALU.mult))
                        dve.tensor_tensor(A.state[:], A.state[:], M.ps[:, 3], ALU.add).then_inc(S.s_ready, 1)
                    else:
                        dve.tensor_copy(A.state[:], M.ps[:, 3]).then_inc(S.s_ready, 1)
                output(i)
            dve.wait_ge(S.o_copied, TT)
            o = A.mix[:].rearrange("p i (h d) -> p (i h) d", h=DH)
            sq = A.BT[:].rearrange("p i (h d) -> p (i h) d", h=DH)
            link(dve.tensor_tensor(sq, o, o, ALU.mult))
            link(dve.tensor_reduce(A.root[:], sq, AX.X, ALU.add))
            dve.tensor_scalar(A.root[:], A.root[:], 1.0 / DHD, RMS_EPS, ALU.mult, ALU.add).then_inc(S.root_in, 1)
            link(dve.tensor_tensor(o, o, A.silz[:].rearrange("p i (h d) -> p (i h) d", h=DH), ALU.mult))
            link(dve.tensor_tensor(o, o, A.norm_g[:].unsqueeze(1).to_broadcast([P, TT * DH, DHD]), ALU.mult))
            dve.wait_ge(S.root_ready, 1)
            link(dve.reciprocal(A.root[:], A.root[:]))
            link(dve.tensor_tensor(o, o, A.root[:].unsqueeze(2).to_broadcast([P, TT * DH, DHD]), ALU.mult))


def mixer2(nc, M, I, l):
    with ExitStack() as memory:
        sb = tensors(nc, memory, "b_")
        A = Memory()
        A.qkv, A.silz, A.mix = sb("qkv", 3 * DH, T), sb("silz", TT, DW), sb("mix", TT, DW)
        A.g, A.beta, A.norm_g = sb("g", TT, DH), sb("beta", TT, DH), sb("norm_g", DHD)
        with ExitStack() as inner:
            sb = tensors(nc, inner, "b_")
            A.raw, A.prod = sb("raw", 3 * DH, T + DCONV - 1), sb("prod", SCT, T + SCCONV - 1)
            A.gate_b, A.gate_c = sb("gate_b", SCT, T), sb("gate_c", SCT, T)
            A.ba, A.inverse = sb("ba", TT, 2 * DH), sb("inverse", 3, T)
            A.conv_w, A.sc_w, A.sc_g = sb("conv_w", DCONV, 3 * DH), sb("sc_w", SCCONV, SCT), sb("sc_g", SCT)
            A.dt_bias, A.a_log, A.a_neg = sb("dt_bias", DH), sb("a_log", DH), sb("a_neg", DH)
            A.dt_e, A.dt_u, A.dt_r, A.dt_ln = (sb(f"dt_{x}", TT, DH) for x in "eurl")
            mixer2_project(nc, M, A, I, l)
            mixer2_conv(nc, M, A, I, l)
        with ExitStack() as inner:
            sb = tensors(nc, inner, "b_")
            A.D, A.LT, A.T1 = sb("D", TT, DW), sb("LT", TT, DW), sb("T1", TT, DW)
            A.qk, A.kdec, A.kbg, A.vb = sb("qk", TT, DW), sb("kdec", TT, DW), sb("kbg", TT, DW), sb("vb", TT, DW)
            A.rows, A.state, A.v_new = sb("rows", DW), sb("state", DW), sb("v_new", DW)
            A.G, A.gain, A.bg, A.root = sb("G", 16), sb("gain", 48), sb("bg", 16), sb("root", 16)
            A.BT, A.u, A.wT = A.D, A.D, A.LT
            mixer2_delta(nc, M, A)
        mix_out(nc, M, "out2", A.mix, range(DT - SCT, DT), I.w_out_2[l], None)


def finish(nc, M, I, out):
    with stage(nc, "finish", "turned copied stored") as (block, S):
        rows = M.x[:].rearrange("p d t -> p (d t)").rearrange("p (i n) -> p i n", i=TT)

        @block.tensor
        def _(pe):
            for n in range(2 * TT):
                i, half = n // 2, n % 2
                for d in range(4):
                    mm = pe.transpose(M.ps[:, n, d * P:(d + 1) * P], M.hT[:, 4 * half + d, i * P:(i + 1) * P], M.ident[:])
                mm.then_inc(S.turned, 1)

        @block.vector
        def _(dve):
            for n in range(2 * TT):
                dve.wait_ge(S.turned, n + 1)
                dve.tensor_copy(rows[:, n // 2, 512 * (n % 2):512 * (n % 2 + 1)], M.ps[:, n, :]).then_inc(S.copied, 1)

        @block.sync
        def _(sp):
            for i in range(TT):
                sp.wait_ge(S.copied, 2 * i + 2)
                sp.dma_start(out[0, i * P:(i + 1) * P, :], rows[:, i, :]).then_inc(S.stored, 16)
            sp.wait_ge(S.stored, 16 * TT)


def program(nc, I, out):
    with ExitStack() as memory:
        sb = tensors(nc, memory, "m_")
        M = Memory()
        M.x, M.hT = sb("x", DT, T), sb("hT", DT, T)
        M.wide, M.rows = sb("wide", 2, 2, DT, 256), sb("rows", 2, 2, D)
        M.ident, M.tri, M.ones, M.mean_d = sb("ident", P), sb("tri", T + 3 * P), sb("ones", P), sb("mean_d", P)
        M.sq, M.rstd = sb("sq", 2, T), sb("rstd", T)
        M.ps = memory.enter_context(nc.psum_tensor("m_ps", [P, 8, T], F32))
        with ExitStack() as inner:
            sb = tensors(nc, inner, "m_")
            M.bias = sb("bias", HEADS, T)
            M.ccol, M.prow, M.pcol, M.mod = sb("ccol", DT), sb("prow", P), sb("pcol", 120), sb("mod", 72)
            M.part = sb("part", 2, 512)
            M.relx = sb("relx", HEADS)
            M.onehot = M.wide[:, 0].rearrange("p a k n -> p (a k n)")[:, 0:T + P]
            M.tape = M.wide[:, 1].rearrange("p a k n -> p (a k n)")[:, 0:T + P]
            M.flip = M.sq[:, 0, 0:P]
            M.flipped = M.rows[:].rearrange("p s e n -> p (s e n)").rearrange("p (h t) -> p h t", h=HEADS)
            M.tape_dram = nc.dram_tensor("bias_tape", [HEADS, T + P], F32, kind="Internal").ap()
            setup(nc, M, I)
            with nc.Fori(0, DEPTH) as l:
                modulation(nc, M, I, l)
                ffn(nc, M, "ffn0", I.ffn_w1[l, 0], I.ffn_w3[l, 0], I.ffn_w2[l, 0], 0)
                mixer1(nc, M, I, l)
                ffn(nc, M, "ffn2", I.ffn_w1[l, 1], I.ffn_w3[l, 1], I.ffn_w2[l, 1], 2)
        sb = tensors(nc, memory, "m_")
        M.gain = sb("gain", DT)
        M.sum_sel, M.spread_sel = sb("sum_sel", 7 * 32), sb("spread_sel", 4, P)
        M.levels, M.mask_neg = sb("levels", LEVELS, P), sb("mask_neg", P)
        with stage(nc, "consts2", "landed") as (block, S):
            @block.sync
            def _(sp):
                for dst, value in ((M.sum_sel, sum_selectors()), (M.spread_sel, spread_selectors()),
                                   (M.levels, level_masks()), (M.mask_neg, (triangle()[:, 3 * P:4 * P] - 1) * 1e30)):
                    sp.dma_start(dst[:], nc.inline_tensor(value.astype(np.float32), name="c_" + dst.name).ap()).then_inc(S.landed, 16)
                sp.wait_ge(S.landed, 64)
        with nc.Fori(0, DEPTH) as l:
            rms(nc, M, "norm1", I.norm1_g_2[l])
            mixer2(nc, M, I, l)
            rms(nc, M, "norm2", I.norm2_g_2[l])
            ffn(nc, M, "ffn3", I.ffn_w_gate_2[l], I.ffn_w_up_2[l], I.ffn_w_down_2[l], None)
        rms(nc, M, "norm3", I.final_norm_g_2)
        finish(nc, M, I, out)


_NAMES = ["x", "c", "rel_bias", "ada_w", "ada_b", "ln_g", "ln_b", "ffn_w1", "ffn_w3", "ffn_w2", "w_in", "w_out",
          "cmp_pe", "cmp_w1", "cmp_b1", "cmp_w2", "gmlp_ln_g", "gmlp_ln_b", "gmlp_ws", "gmlp_bs", "ssm_conv_w",
          "ssm_conv_b", "ssm_dt_bias", "ssm_a_log", "ssm_d", "ssm_norm_g", "norm1_g_2", "w_in_2", "dn_conv_w_2",
          "dn_a_log_2", "dn_dt_bias_2", "dn_norm_g_2", "sc_conv_w_2", "sc_norm_g_2", "w_out_2", "norm2_g_2",
          "ffn_w_gate_2", "ffn_w_up_2", "ffn_w_down_2", "final_norm_g_2"]


def kernel(**inputs):
    import concourse.bacc as bacc
    from concourse.bass_utils import run_bass_kernel_spmd

    nc = bacc.Bacc("TRN2", target_bir_lowering=False, num_devices=1)
    arrays, aps = {}, {}
    for name in _NAMES:
        a = np.ascontiguousarray(inputs[name])
        arrays[f"in_{name}"] = a
        aps[name] = nc.dram_tensor(f"in_{name}", a.shape, mybir.dt.from_np(a.dtype), kind="ExternalInput").ap()
    out = nc.dram_tensor("out", (1, T, D), F32, kind="ExternalOutput").ap()
    program(nc, namedtuple("Inputs", _NAMES)(**aps), out)
    return run_bass_kernel_spmd(nc, [arrays], core_ids=[0]).results[0]["out"]
```

```python
import math
from collections import namedtuple
from contextlib import ExitStack, contextmanager

import numpy as np
import concourse.bass as bass
from concourse import mybir

F32 = mybir.dt.float32
F32R = mybir.dt.float32r
ALU = mybir.AluOpType
ACT = mybir.ActivationFunctionType
AX = mybir.AxisListType

P = 128
T = 512
TT = T // P
D = 1024
DT = D // P
F = 2816
FT = F // P
DEPTH = 2
ALPHA = (2 * DEPTH) ** 0.25
LN_EPS = 1e-5
RMS_EPS = 1e-6

HEADS, GROUPS, HD = 8, 2, 64
HPG = HEADS // GROUPS
KV = GROUPS * HD
N_BRANCH = 3
CMP_LEN, CMP_STRIDE, CMP_HID = 32, 16, 256
N_CMP = (T - CMP_LEN) // CMP_STRIDE + 1
BUCKETS, MAX_DIST = 32, 128
Q_OFF = 0
KC_OFF = HEADS * HD
VW_OFF = KC_OFF + 5 * KV
GATE_OFF = KC_OFF + 6 * KV
GMLP_OFF = GATE_OFF + HEADS * N_BRANCH
D_GMLP, GG, GGD = 256, 4, 64
Z_OFF = GMLP_OFF + 2 * D_GMLP
D_SSM, SH, SG, NSTATE, SCONV = 256, 4, 2, 128, 4
XBC_OFF = Z_OFF + D_SSM
D_XBC = D_SSM + 2 * SG * NSTATE
XT = D_XBC // P
DT_OFF = XBC_OFF + D_XBC
D_IN = DT_OFF + SH
MASKED = -1.0e30
FLOOR = -1.0e29

DH, DHD, DCONV = 4, 128, 4
DW = DH * DHD
SCW, SCCONV = 512, 3
SCT = SCW // P
W2_COLS = 4 * DW + 2 * DH + 3 * SCW
LEVELS = 7


def rel_bucket_onehot():
    dist = T - 1 - np.arange(T + P)
    n = np.maximum(dist, 0)
    exact = BUCKETS // 2
    nf = np.maximum(n, 1).astype(np.float32)
    large = exact + (np.log(nf / exact) / math.log(MAX_DIST / exact) * (BUCKETS - exact)).astype(np.int32)
    bucket = np.where(n < exact, n, np.minimum(large, BUCKETS - 1))
    out = np.zeros((BUCKETS + 1, T + P), np.float32)
    seen = dist >= 0
    out[bucket[seen], np.nonzero(seen)[0]] = 1
    out[BUCKETS, ~seen] = 1
    return out


def triangle():
    return (np.arange(T + P * 3)[None, :] - P * 3 >= np.arange(P)[:, None]).astype(np.float32)


def level_masks():
    i = np.arange(P)
    out = np.zeros((P, LEVELS, P), np.float32)
    for n in range(LEVELS):
        m = 1 << n
        out[:, n, :] = ((i[:, None] // (2 * m) == i[None, :] // (2 * m))
                        & ((i // m) % 2 == 0)[:, None] & ((i // m) % 2 == 1)[None, :])
    return out


class Memory:
    pass


@contextmanager
def stage(nc, name, signals):
    names = signals.split()
    sems = [nc.alloc_semaphore(f"{name}_{s}") for s in names]
    with nc.Block(name) as block:
        yield block, namedtuple("Signals", names)(*sems)
    nc.clear_and_free_semaphores(sems)
    nc.all_engine_barrier()


def tensors(nc, memory, prefix):
    return lambda name, *shape: memory.enter_context(nc.sbuf_tensor(prefix + name, [P, *shape], F32))


def rounded(nc, memory, prefix):
    return lambda name, *shape: memory.enter_context(nc.sbuf_tensor(prefix + name, [P, *shape], F32R))


def product(pe, out, stationary, moving, first, last):
    (sh, sl), (mh, ml) = stationary, moving
    pe.matmul(out, sh, mh, start=first, stop=False, skip_group_check=True)
    pe.matmul(out, sh, ml, start=False, stop=False, skip_group_check=True)
    return pe.matmul(out, sl, mh, start=False, stop=last, skip_group_check=True)


def low_part(dve, low, value, high):
    return dve.tensor_tensor(low, value, high.bitcast(F32), ALU.subtract)


def chain(engine, sem):
    done = [0]

    def link(instruction):
        done[0] += 1
        instruction.then_inc(sem, 1)
        engine.wait_ge(sem, done[0])
        return instruction
    return link


def setup(nc, M, I):
    with stage(nc, "setup", "consts onehot x_landed rel_landed mask_row turned copied tape_ready tape_copied "
               "tape_stored windows_landed flipped bias_copied bias_stored c_landed vectors_landed vectors_turned"
               ) as (block, S), ExitStack() as memory:
        sb = tensors(nc, memory, "s_")
        x_rows, bias, windows = sb("x_rows", TT, D), sb("bias", HEADS, T), sb("windows", HEADS, T)
        onehot, tape, relx, flip, vectors = sb("onehot", T + P), sb("tape", T + P), sb("relx", HEADS), sb("flip", P), sb("vectors", DEPTH, P)
        const = lambda value, name: nc.inline_tensor(np.ascontiguousarray(value, np.float32), name=name).ap()

        @block.sync
        def _(sp):
            sp.dma_start(M.ident[:], const(np.eye(P), "c_ident")).then_inc(S.consts, 16)
            for i in range(TT):
                sp.dma_start(x_rows[:, i, :], I.x[0, i * P:(i + 1) * P, :]).then_inc(S.x_landed, 16)
            sp.dma_start(onehot[0:BUCKETS + 1, :], const(rel_bucket_onehot(), "c_bucket")).then_inc(S.onehot, 16)
            sp.dma_start(relx[0:BUCKETS, :], I.rel_bias).then_inc(S.rel_landed, 16)
            with nc.allow_non_contiguous_dma(reason="one vector as columns"):
                sp.dma_start(M.ccol[:], I.c[0].rearrange("(k p) -> p k", p=P)).then_inc(S.c_landed, 16)
            for l in range(DEPTH):
                sp.dma_start(vectors[0:72, l, :], I.ada_b[l].rearrange("(r n) -> r n", n=P)).then_inc(S.vectors_landed, 16)
                sp.dma_start(vectors[72:96, l, :], I.ln_g[l].rearrange("s (d n) -> (s d) n", n=P)).then_inc(S.vectors_landed, 16)
                sp.dma_start(vectors[96:120, l, :], I.ln_b[l].rearrange("s (d n) -> (s d) n", n=P)).then_inc(S.vectors_landed, 16)
            sp.dma_start(flip[:], const(np.eye(P)[::-1], "c_flip")).then_inc(S.consts, 16)
            sp.dma_start(M.tri[:], const(triangle(), "c_tri")).then_inc(S.consts, 16)
            sp.dma_start(M.ones[:], const(np.ones((P, P)), "c_ones")).then_inc(S.consts, 16)
            sp.dma_start(M.mean_d[:], const(np.full((P, P), 1 / D), "c_mean")).then_inc(S.consts, 16)
            sp.wait_ge(S.tape_copied, 2)
            sp.dma_start(M.tape_dram, tape[0:HEADS, :]).then_inc(S.tape_stored, 16)
            sp.wait_ge(S.tape_stored, 16)
            for h in range(HEADS):
                rows = bass.AP(tensor=M.tape_dram.tensor, offset=h * (T + P), ap=[[1, P], [1, T]])
                sp.dma_start(windows[:, h, :], rows).then_inc(S.windows_landed, 16)
            sp.wait_ge(S.bias_copied, HEADS)
            sp.dma_start(M.bias_dram, bias[:]).then_inc(S.bias_stored, 16)
            sp.wait_ge(S.bias_stored, 16)

        @block.tensor
        def _(pe):
            pe.wait_ge(S.consts, 80)
            pe.wait_ge(S.x_landed, 16 * TT)
            for d in range(DT):
                for i in range(TT):
                    mm = pe.transpose(M.ps[:, d, i * P:(i + 1) * P], x_rows[:, i, d * P:(d + 1) * P], M.ident[:])
                mm.then_inc(S.turned, 1)
            pe.wait_ge(S.onehot, 16)
            pe.wait_ge(S.rel_landed, 16)
            pe.wait_ge(S.mask_row, 1)
            pe.wait_ge(S.copied, 4)
            pe.matmul(M.ps[0:HEADS, 0, :], relx[0:BUCKETS + 1, :], onehot[0:BUCKETS + 1, 0:T],
                      start=True, stop=True).then_inc(S.tape_ready, 1)
            pe.matmul(M.ps[0:HEADS, 1, 0:P], relx[0:BUCKETS + 1, :], onehot[0:BUCKETS + 1, T:T + P],
                      start=True, stop=True).then_inc(S.tape_ready, 1)
            pe.wait_ge(S.vectors_landed, 16 * 3 * DEPTH)
            for l in range(DEPTH):
                pe.transpose(M.ps[:, 2 + l, 0:120], vectors[0:120, l, :], M.ident[0:120, 0:120]).then_inc(S.vectors_turned, 1)
            pe.wait_ge(S.windows_landed, 16 * HEADS)
            pe.wait_ge(S.copied, DT + DEPTH)
            for h in range(HEADS):
                pe.matmul(M.ps[:, h, :], flip[:], windows[:, h, :], start=True, stop=True).then_inc(S.flipped, 1)

        @block.scalar
        def _(act):
            act.wait_ge(S.c_landed, 16)
            act.activation(M.ccol[:], M.ccol[:], ACT.Silu)

        @block.vector
        def _(dve):
            dve.memset(relx[BUCKETS:BUCKETS + 1, :], MASKED).then_inc(S.mask_row, 1)
            for d in range(DT):
                dve.wait_ge(S.turned, d + 1)
                dve.tensor_copy(M.x[:, d, :], M.ps[:, d, :]).then_inc(S.copied, 1)
            dve.wait_ge(S.tape_ready, 2)
            dve.tensor_copy(tape[0:HEADS, 0:T], M.ps[0:HEADS, 0, :]).then_inc(S.tape_copied, 1)
            dve.tensor_copy(tape[0:HEADS, T:T + P], M.ps[0:HEADS, 1, 0:P]).then_inc(S.tape_copied, 1)
            for l in range(DEPTH):
                dve.wait_ge(S.vectors_turned, l + 1)
                dve.tensor_copy(M.columns[:, l, :], M.ps[:, 2 + l, 0:120]).then_inc(S.copied, 1)
            for h in range(HEADS):
                dve.wait_ge(S.flipped, h + 1)
                dve.tensor_copy(bias[:, h, :], M.ps[:, h, :]).then_inc(S.bias_copied, 1)


ADA_SIGNALS = " ada0_landed ada1_landed ada_mac ada_partial ada_column mod_chain mod_ready"


def ada_load(queue, M, S, source, m, s):
    queue.dma_start(M.ada[:, s], source[:, :, bass.ds(m * P, P)]).then_inc([S.ada0_landed, S.ada1_landed][s], 16)


def ada_sum(dve, M, S, m, s, part, uses):
    dve.wait_ge([S.ada0_landed, S.ada1_landed][s], 16 * uses)
    dve.tensor_scalar(M.part[:, part, :], M.ada[:, s, 0, :], M.ccol[:, 0:1], None, ALU.mult).then_inc(S.ada_mac, 1)
    for k in range(1, DT):
        dve.wait_ge(S.ada_mac, m * (DT - 1) + k)
        dve.scalar_tensor_tensor(out=M.part[:, part, :], in0=M.ada[:, s, k, :], scalar=M.ccol[:, k:k + 1],
                                 in1=M.part[:, part, :], op0=ALU.mult, op1=ALU.add
                                 ).then_inc(S.ada_mac if k < DT - 1 else S.ada_partial, 1)


def ada_column(pe, M, S, m, part):
    pe.wait_ge(S.ada_partial, m + 1)
    pe.matmul(M.ps[:, 7, bass.ds(m, 1)], M.part[:, part, :], M.ones[:, 0:1], start=True, stop=True).then_inc(S.ada_column, 1)


def ada_finish(dve, M, S, subs, biases):
    link = chain(dve, S.mod_chain)
    n = 3 * DT * len(subs)
    dve.wait_ge(S.ada_column, n)
    mod = M.mod[:, 3 * DT * subs[0]:3 * DT * subs[0] + n]
    link(dve.tensor_tensor(mod, M.ps[:, 7, 0:n], biases, ALU.add))
    dve.sem_inc(S.mod_ready, 1)
    for sub in subs:
        weight = 1.0 if sub == 1 else 0.5
        scale, gate = (M.mod[:, sub * 24 + w * DT:sub * 24 + (w + 1) * DT] for w in (1, 2))
        link(dve.tensor_scalar(scale, scale, 1.0, None, ALU.add))
        link(dve.tensor_scalar(gate, gate, 1.0, weight / ALPHA, ALU.add, ALU.mult))


def first_modulation(nc, M, I):
    chunks = 3 * DT
    source = I.ada_w[0].rearrange("(k p) n -> p k n", p=P)
    with ExitStack() as memory, stage(nc, "ada", ADA_SIGNALS) as (block, S):
        M.ada = tensors(nc, memory, "ada_")("chunks", 2, DT, P)

        @block.sync
        def _(sp):
            for s in range(2):
                ada_load(sp, M, S, source, s, s)
            with sp.Fori(1, chunks // 2) as i:
                for s in range(2):
                    sp.wait_ge(S.ada_partial, 2 * i + s - 1)
                    ada_load(sp, M, S, source, 2 * i + s, s)

        @block.vector
        def _(dve):
            for s in range(2):
                ada_sum(dve, M, S, s, s, s, 1)
            with dve.Fori(1, chunks // 2) as i:
                for s in range(2):
                    dve.wait_ge(S.ada_column, 2 * i + s - 1)
                    ada_sum(dve, M, S, 2 * i + s, s, s, i + 1)
            ada_finish(dve, M, S, [0], M.columns[:, 0, 0:chunks])

        @block.tensor
        def _(pe):
            with pe.Fori(0, chunks // 2) as i:
                for s in range(2):
                    ada_column(pe, M, S, 2 * i + s, s)


NORM_SIGNALS = " z_ready mean_ready centered square_ready square_used var_ready root_ready rstd_ready xhat_ready"


def post_norm_pe(pe, M, S):
    for d in range(DT):
        pe.wait_ge(S.z_ready, d + 1)
        mm = pe.matmul(M.ps[:, 0, :], M.mean_d[:], M.x[:, d, :], start=(d == 0), stop=(d == DT - 1))
    mm.then_inc(S.mean_ready, 1)
    for d in range(DT):
        pe.wait_ge(S.square_ready, d + 1)
        pe.matmul(M.ps[:, 1, :], M.mean_d[:], M.sq[:, d % 2, :], start=(d == 0),
                  stop=(d == DT - 1)).then_inc(S.square_used, 1)


def post_norm_act(act, M, S, sub):
    for d in range(DT):
        act.wait_ge(S.centered, d + 1)
        if d >= 2:
            act.wait_ge(S.square_used, d - 1)
        act.activation(M.sq[:, d % 2, :], M.x[:, d, :], ACT.Square).then_inc(S.square_ready, 1)
    act.wait_ge(S.var_ready, 1)
    act.activation(M.rstd[:], M.rstd[:], ACT.Sqrt).then_inc(S.root_ready, 1)
    for d in range(DT):
        act.wait_ge(S.xhat_ready, d + 1)
        act.activation(M.x[:, d, :], M.x[:, d, :], ACT.Identity, scale=M.pcol[:, 72 + sub * DT + d:73 + sub * DT + d],
                       bias=M.pcol[:, 96 + sub * DT + d:97 + sub * DT + d])


def post_norm_dve(dve, M, S, sub):
    gate = M.mod[:, sub * 24 + 2 * DT:sub * 24 + 3 * DT]
    for d in range(DT):
        dve.wait_ge(S.y_ready, d + 1)
        dve.scalar_tensor_tensor(out=M.x[:, d, :], in0=M.ps[:, d, :], scalar=gate[:, d:d + 1],
                                 in1=M.x[:, d, :], op0=ALU.mult, op1=ALU.add).then_inc(S.z_ready, 1)
    dve.wait_ge(S.z_ready, DT)
    dve.wait_ge(S.mean_ready, 1)
    for d in range(DT):
        dve.tensor_tensor(M.x[:, d, :], M.x[:, d, :], M.ps[:, 0, :], ALU.subtract).then_inc(S.centered, 1)
    dve.wait_ge(S.square_used, DT)
    dve.tensor_scalar(M.rstd[:], M.ps[:, 1, :], LN_EPS / ALPHA ** 2, None, ALU.add).then_inc(S.var_ready, 1)
    dve.wait_ge(S.root_ready, 1)
    dve.reciprocal(M.rstd[:], M.rstd[:]).then_inc(S.rstd_ready, 1)
    dve.wait_ge(S.rstd_ready, 1)
    for d in range(DT):
        dve.tensor_tensor(M.x[:, d, :], M.x[:, d, :], M.rstd[:], ALU.mult).then_inc(S.xhat_ready, 1)


H_SIGNALS = " h_value h_high h_ready"


def round_h_dve(dve, M, S, value):
    def low(d):
        dve.wait_ge(S.h_high, d + 1)
        low_part(dve, M.h_low[:, d, :], M.sq[:, d % 2, :], M.h_high[:, d, :]).then_inc(S.h_ready, 1)

    for d in range(DT):
        if d >= 2:
            dve.wait_ge(S.h_ready, d - 1)
        value(d, M.sq[:, d % 2, :]).then_inc(S.h_value, 1)
        if d:
            low(d - 1)
    low(DT - 1)


def round_h_act(act, M, S):
    for d in range(DT):
        act.wait_ge(S.h_value, d + 1)
        act.copy(M.h_high[:, d, :], M.sq[:, d % 2, :]).then_inc(S.h_high, 1)


def modulate_dve(dve, M, S, sub):
    round_h_dve(dve, M, S, lambda d, out: dve.tensor_scalar(
        out, M.x[:, d, :], M.mod[:, sub * 24 + DT + d:sub * 24 + DT + d + 1],
        M.mod[:, sub * 24 + d:sub * 24 + d + 1], ALU.mult, ALU.add))


RMS_SIGNALS = " gain_landed square_in square_out mean_copied rms_root inverse_ready"


def rms_sp(sp, nc, M, S, gain):
    with nc.allow_non_contiguous_dma(reason="one vector as columns"):
        sp.dma_start(M.gain[:], gain.rearrange("(d p) -> p d", p=P)).then_inc(S.gain_landed, 16)


def rms_act(act, M, S):
    for d in range(DT):
        if d >= 2:
            act.wait_ge(S.square_out, d - 1)
        act.activation(M.sq[:, d % 2, :], M.x[:, d, :], ACT.Square).then_inc(S.square_in, 1)
    act.wait_ge(S.mean_copied, 1)
    act.activation(M.rstd[:], M.rstd[:], ACT.Sqrt).then_inc(S.rms_root, 1)


def rms_pe(pe, M, S, bank):
    for d in range(DT):
        pe.wait_ge(S.square_in, d + 1)
        pe.matmul(M.ps[:, bank, :], M.mean_d[:], M.sq[:, d % 2, :], start=(d == 0), stop=(d == DT - 1)).then_inc(S.square_out, 1)


def rms_dve(dve, M, S, bank):
    dve.wait_ge(S.square_out, DT)
    dve.tensor_scalar(M.rstd[:], M.ps[:, bank, :], RMS_EPS, None, ALU.add).then_inc(S.mean_copied, 1)
    dve.wait_ge(S.rms_root, 1)
    dve.reciprocal(M.rstd[:], M.rstd[:]).then_inc(S.inverse_ready, 1)
    dve.wait_ge(S.inverse_ready, 1)
    dve.wait_ge(S.gain_landed, 16)


def rms_value(dve, M, d, out):
    return dve.scalar_tensor_tensor(out=out, in0=M.x[:, d, :], scalar=M.gain[:, d:d + 1], in1=M.rstd[:],
                                    op0=ALU.mult, op1=ALU.mult)


def ffn(nc, M, tag, w_gate, w_up, w_down, sub, ada=None, vectors=None, gain=None):
    subs, ada_source, ada_bias = ada or ([], None, None)
    gate_v = w_gate.rearrange("(k p) f -> p k f", p=P)
    up_v = w_up.rearrange("(k p) f -> p k f", p=P)
    down_v = w_down.rearrange("(f p) n -> p f n", p=P)
    signals = ("wide0_landed wide1_landed rows0_landed rows1_landed wide_high wide_split projected silu_done hidden_done "
               "rows_high rows_split down_done y_ready vectors_copied")
    last = NORM_SIGNALS if sub is not None else RMS_SIGNALS
    with ExitStack() as memory, stage(nc, tag, signals + last + H_SIGNALS + ADA_SIGNALS) as (block, S):
        sb, sr = tensors(nc, memory, tag + "_"), rounded(nc, memory, tag + "_")
        hid, sil, raw, rows = sb("hid", FT, T), sb("sil", 2, T), sb("raw", 2, 2, DT, P), sb("rows", 2, D)
        M.h_high, M.h_low = sr("h_high", DT, T), sr("h_low", DT, T)
        w_high, w_low = sr("w_high", 2, 2, DT, P), sr("w_low", 2, 2, DT, P)
        rows_high, rows_low, hid_high, hid_low = sr("rows_high", 2, D), sr("rows_low", 2, D), sr("hid_high", 2, T), sr("hid_low", 2, T)
        if subs:
            M.ada = sb("ada_chunks", 2, DT, P)
        wide_landed = [S.wide0_landed, S.wide1_landed]
        rows_landed = [S.rows0_landed, S.rows1_landed]
        ada_landed = [S.ada0_landed, S.ada1_landed]
        per_step = len(subs)
        row = lambda ap, f: ap[:, bass.ds(f, 1), :].rearrange("p a t -> p (a t)")
        flat = lambda ap: ap.rearrange("p w k n -> p (w k n)")

        @block.sync
        def _(sp):
            def load_wide(s, n):
                sp.dma_start(raw[:, s, 0], gate_v[:, :, bass.ds(n * P, P)]).then_inc(wide_landed[s], 16)
                sp.dma_start(raw[:, s, 1], up_v[:, :, bass.ds(n * P, P)]).then_inc(wide_landed[s], 16)

            def load_rows(s, n):
                sp.dma_start(rows[:, s], row(down_v, n)).then_inc(rows_landed[s], 16)

            load_wide(0, 0)
            load_wide(1, 1)
            if gain is not None:
                rms_sp(sp, nc, M, S, gain)
            load_rows(0, 0)
            load_rows(1, 1)
            with sp.Fori(1, FT // 2) as i:
                for s in range(2):
                    sp.wait_ge(S.wide_split, 2 * i + s - 1)
                    load_wide(s, 2 * i + s)
            with sp.Fori(1, FT // 2) as i:
                for s in range(2):
                    sp.wait_ge(S.rows_split, 2 * i + s - 1)
                    load_rows(s, 2 * i + s)

        if subs:
            @block.gpsimd
            def _(pool):
                for m in range(2):
                    ada_load(pool, M, S, ada_source, m, m)
                with pool.Fori(1, 3 * DT * per_step // 2) as i:
                    for s in range(2):
                        pool.wait_ge(S.ada_partial, 2 * i + s - 1)
                        ada_load(pool, M, S, ada_source, 2 * i + s, s)

        @block.tensor
        def _(pe):
            def project(s, f, first):
                pe.wait_ge(S.wide_split, f + 1)
                if not first:
                    pe.wait_ge(S.hidden_done, f - 1)
                for which in range(2):
                    for k in range(DT):
                        if first:
                            pe.wait_ge(S.h_ready, k + 1)
                        mm = product(pe, M.ps[:, 2 * s + which, :], (w_high[:, s, which, k], w_low[:, s, which, k]),
                                     (M.h_high[:, k, :], M.h_low[:, k, :]), k == 0, k == DT - 1)
                mm.then_inc(S.projected, 1)

            def columns(s, n):
                for e in range(per_step):
                    ada_column(pe, M, S, n * per_step + e, s * per_step + e)

            if gain is not None:
                rms_pe(pe, M, S, 4)
            project(0, 0, True)
            project(1, 1, True)
            columns(0, 0)
            with pe.Fori(1, FT // 2) as i:
                project(0, 2 * i, False)
                columns(1, 2 * i - 1)
                project(1, 2 * i + 1, False)
                columns(0, 2 * i)

            def down(s, d, first, last):
                cols = slice(d * P, (d + 1) * P)
                return product(pe, M.ps[:, d, :], (rows_high[:, s, cols], rows_low[:, s, cols]),
                               (hid_high[:, s, :], hid_low[:, s, :]), first, last)

            pe.wait_ge(S.rows_split, 1)
            for d in (4, 5, 6, 0, 1, 2, 3):
                if d == 0:
                    pe.wait_ge(S.hidden_done, FT)
                down(0, d, True, False)
            for n in range(FT - 1, FT + 2):
                columns(n % 2, n)
            pe.wait_ge(S.rows_split, 2)
            for d in range(DT - 1):
                down(1, d, False, False)
            if subs:
                pe.wait_ge(S.mod_ready, 1)
            down(0, DT - 1, True, False).then_inc(S.down_done, 1)
            down(1, DT - 1, False, False).then_inc(S.down_done, 1)
            with pe.Fori(1, FT // 2 - 1) as i:
                for s in range(2):
                    pe.wait_ge(S.rows_split, 2 * i + s + 1)
                    for d in range(DT):
                        mm = down(s, d, False, False)
                    mm.then_inc(S.down_done, 1)
            pe.wait_ge(S.rows_split, FT)
            for d in range(DT):
                down(0, d, False, False)
                down(1, d, False, True).then_inc(S.y_ready, 1)
            if sub is not None:
                post_norm_pe(pe, M, S)

        @block.scalar
        def _(act):
            def split(s, n, landings, first):
                act.wait_ge(wide_landed[s], landings)
                if not first:
                    act.wait_ge(S.projected, n - 1)
                act.copy(flat(w_high[:, s]), flat(raw[:, s])).then_inc(S.wide_high, 1)

            def silu(s, f, first):
                act.wait_ge(S.projected, f + 1)
                if not first:
                    act.wait_ge(S.hidden_done, f - 1)
                act.activation(sil[:, s, :], M.ps[:, 2 * s, :], ACT.Silu).then_inc(S.silu_done, 1)

            def split_rows(s, f, landings, first):
                act.wait_ge(rows_landed[s], landings)
                if not first:
                    act.wait_ge(S.down_done, f - 1)
                act.copy(rows_high[:, s], rows[:, s])
                act.copy(hid_high[:, s], row(hid, f)).then_inc(S.rows_high, 1)

            if gain is not None:
                rms_act(act, M, S)
            split(0, 0, 32, True)
            round_h_act(act, M, S)
            split(1, 1, 32, True)
            silu(0, 0, True)
            split(0, 2, 64, False)
            silu(1, 1, True)
            split(1, 3, 64, False)
            with act.Fori(2, FT // 2) as i:
                for s in range(2):
                    silu(s, 2 * i + s - 2, False)
                    split(s, 2 * i + s, 32 * i + 32, False)
            silu(0, FT - 2, False)
            for s in range(2):
                split_rows(s, s, 16, True)
            silu(1, FT - 1, False)
            act.wait_ge(S.hidden_done, FT)
            with act.Fori(1, FT // 2) as i:
                for s in range(2):
                    split_rows(s, 2 * i + s, 16 * i + 16, False)
            if sub is not None:
                post_norm_act(act, M, S, sub)

        @block.vector
        def _(dve):
            def split(s, n):
                dve.wait_ge(S.wide_high, n + 1)
                low_part(dve, flat(w_low[:, s]), flat(raw[:, s]), flat(w_high[:, s])).then_inc(S.wide_split, 1)

            def hidden(s, f):
                dve.wait_ge(S.silu_done, f + 1)
                dve.tensor_tensor(row(hid, f), sil[:, s, :], M.ps[:, 2 * s + 1, :], ALU.mult).then_inc(S.hidden_done, 1)

            def split_rows(s, f):
                dve.wait_ge(S.rows_high, f + 1)
                low_part(dve, rows_low[:, s], rows[:, s], rows_high[:, s])
                low_part(dve, hid_low[:, s], row(hid, f), hid_high[:, s]).then_inc(S.rows_split, 1)

            def ada_step(s, n, half, first):
                if per_step and not first:
                    dve.wait_ge(S.ada_column, (n - 1) * per_step)
                for e in range(per_step):
                    slot = (s * per_step + e) % 2
                    ada_sum(dve, M, S, n * per_step + e, slot, s * per_step + e,
                            half * per_step + (s * per_step + e) // 2 + 1)

            if vectors is not None:
                dve.tensor_copy(M.pcol[:], vectors[0]).then_inc(S.vectors_copied, 1)
                dve.tensor_copy(M.bnext[:], vectors[1]).then_inc(S.vectors_copied, 1)
            if sub is not None:
                split(0, 0)
                modulate_dve(dve, M, S, sub)
            else:
                rms_dve(dve, M, S, 4)
                split(0, 0)
                round_h_dve(dve, M, S, lambda d, out: rms_value(dve, M, d, out))
            split(1, 1)
            ada_step(0, 0, 0, True)
            hidden(0, 0)
            split(0, 2)
            ada_step(1, 1, 0, True)
            hidden(1, 1)
            split(1, 3)
            ada_step(0, 2, 1, False)
            with dve.Fori(2, FT // 2) as i:
                hidden(0, 2 * i - 2)
                split(0, 2 * i)
                ada_step(1, 2 * i - 1, i - 1, False)
                hidden(1, 2 * i - 1)
                split(1, 2 * i + 1)
                ada_step(0, 2 * i, i, False)
            hidden(0, FT - 2)
            split_rows(0, 0)
            split_rows(1, 1)
            hidden(1, FT - 1)
            for n in range(FT - 1, FT + 2):
                ada_step(n % 2, n, n // 2, False)
            if subs:
                if vectors is not None:
                    dve.wait_ge(S.vectors_copied, 2)
                ada_finish(dve, M, S, subs, ada_bias)
            with dve.Fori(1, FT // 2) as i:
                for s in range(2):
                    split_rows(s, 2 * i + s)
            if sub is not None:
                post_norm_dve(dve, M, S, sub)
            else:
                for d in range(DT):
                    dve.wait_ge(S.y_ready, d + 1)
                    dve.tensor_tensor(M.x[:, d, :], M.x[:, d, :], M.ps[:, d, :], ALU.add)


def modulate_act(act, M, S, sub):
    for d in range(DT):
        act.activation(M.hT[:, d, :], M.x[:, d, :], ACT.Identity, scale=M.mod[:, sub * 24 + DT + d:sub * 24 + DT + d + 1],
                       bias=M.mod[:, sub * 24 + d:sub * 24 + d + 1]).then_inc(S.h_ready, 1)


def project(nc, M, tag, chunks, tiles, sub, gain=None, others=()):
    slots = [M.wide[:, s].rearrange("p a k n -> p (a k n)").rearrange("p (k n) -> p k n", k=DT) for s in range(2)]
    last_tile = [max(n for n, t in enumerate(tiles) if t[0] == c) for c in range(len(chunks))]
    engine_of = [t[3] for t in tiles]

    def evacuated(n):
        return engine_of[:n + 1].count(engine_of[n])

    with stage(nc, tag, "h_ready w0_landed w1_landed product act_evacuated dve_evacuated others_landed" + RMS_SIGNALS) as (block, S):
        landed = [S.w0_landed, S.w1_landed]
        done = {"act": S.act_evacuated, "dve": S.dve_evacuated}
        landings = [16 * sum(len(chunks[j]) for j in range(c % 2, c + 1, 2)) for c in range(len(chunks))]

        @block.sync
        def _(sp):
            for c, pieces in enumerate(chunks):
                if c >= 2:
                    sp.wait_ge(S.product, last_tile[c - 2] + 1)
                for cols, src in pieces:
                    sp.dma_start(slots[c % 2][:, :, cols], src).then_inc(landed[c % 2], 16)
                if c == 0 and gain is not None:
                    rms_sp(sp, nc, M, S, gain)
            for dst, src in others:
                sp.dma_start(dst, src).then_inc(S.others_landed, 16)
            if others:
                sp.wait_ge(S.others_landed, 16 * len(others))

        @block.tensor
        def _(pe):
            if gain is not None:
                rms_pe(pe, M, S, 7)
            pe.wait_ge(S.h_ready, DT)
            for n, (c, cols, i, _, _) in enumerate(tiles):
                if n == 0 or tiles[n - 1][0] != c:
                    pe.wait_ge(landed[c % 2], landings[c])
                if n >= 8:
                    pe.wait_ge(done[engine_of[n - 8]], evacuated(n - 8))
                w = slots[c % 2][:, :, cols]
                for k in range(DT):
                    if i is None:
                        mm = pe.matmul(M.ps[:, n % 8, :], w[:, k, :], M.hT[:, k, :], start=(k == 0), stop=(k == DT - 1))
                    else:
                        mm = pe.matmul(M.ps[:, n % 8, 0:w.shape[2]], M.hT[:, k, i * P:(i + 1) * P], w[:, k, :],
                                       start=(k == 0), stop=(k == DT - 1))
                mm.then_inc(S.product, 1)

        @block.scalar
        def _(act):
            if sub is not None:
                modulate_act(act, M, S, sub)
            else:
                rms_act(act, M, S)
            for n, (_, _, i, engine, evacuate) in enumerate(tiles):
                if engine == "act":
                    act.wait_ge(S.product, n + 1)
                    evacuate(act, M.ps[:, n % 8, :], i).then_inc(S.act_evacuated, 1)

        @block.vector
        def _(dve):
            if gain is not None:
                rms_dve(dve, M, S, 7)
                for d in range(DT):
                    rms_value(dve, M, d, M.hT[:, d, :]).then_inc(S.h_ready, 1)
            for n, (_, _, i, engine, evacuate) in enumerate(tiles):
                if engine == "dve":
                    dve.wait_ge(S.product, n + 1)
                    evacuate(dve, M.ps[:, n % 8, :], i).then_inc(S.dve_evacuated, 1)


def mixer1_project(nc, M, A, I, l):
    w = I.w_in[l].rearrange("(k p) n -> p k n", p=P)
    q_pieces = [(slice(P * a + HD * g, P * a + HD * (g + 1)), w[:, :, (a + HPG * g) * HD:(a + HPG * g + 1) * HD])
                for a in range(HPG) for g in range(GROUPS)]
    bounds = [KC_OFF, KC_OFF + 4 * KV, GMLP_OFF, Z_OFF, XBC_OFF, XBC_OFF + 4 * P, D_IN]
    chunks = [q_pieces] + [[(slice(0, b - a), w[:, :, a:b])] for a, b in zip(bounds, bounds[1:])]
    cols = lambda a, n: slice(a, a + n)

    def q_tile(a):
        return lambda act, ps, i: act.activation(A.qT[:, a, :], ps, ACT.Copy, scale=HD ** -0.5)

    def blocks(j):
        return lambda dve, ps, i: dve.tensor_copy(
            A.blk[:, j, :, 0:N_CMP], bass.AP(tensor=ps.tensor, offset=ps.offset,
                                             ap=[list(ps.ap[0]), [1, CMP_LEN], [CMP_STRIDE, N_CMP]]))

    def copy_to(dst):
        return lambda dve, ps, i: dve.tensor_copy(dst, ps[:, 0:dst.shape[-1]])

    def vs_tile(dve, ps, i):
        return dve.tensor_copy(A.vs[:, i, :], ps[:, 0:KV])

    def vw_gate_tile(act, ps, i):
        act.copy(A.vw[:, i, :], ps[:, 0:KV])
        return act.activation(A.gates[:, i, :], ps[:, KV:KV + HEADS * N_BRANCH], ACT.Sigmoid)

    tiles = [(0, cols(P * a, P), None, "act", q_tile(a)) for a in range(HPG)]
    tiles += [(1, cols(0, P), None, "dve", blocks(0)), (1, cols(P, P), None, "dve", blocks(1)),
              (1, cols(2 * P, P), None, "dve", copy_to(A.ksT[:]))]
    tiles += [(1, cols(3 * P, KV), i, "dve", vs_tile) for i in range(TT)]
    tiles += [(2, cols(0, P), None, "dve", copy_to(A.kwT[:]))]
    tiles += [(2, cols(P, KV + HEADS * N_BRANCH), i, "act", vw_gate_tile) for i in range(TT)]
    tiles += [(3, cols(0, 2 * D_GMLP), i, "act",
               lambda act, ps, i: act.activation(A.uv[:, i, :], ps, ACT.Gelu_apprx_tanh)) for i in range(TT)]
    tiles += [(4, cols(0, D_SSM), i, "act",
               lambda act, ps, i: act.activation(A.silz[:, i, :], ps[:, 0:D_SSM], ACT.Silu)) for i in range(TT)]
    tiles += [(5 + c // 4, cols(P * (c % 4), P), None, "dve", copy_to(A.raw[:, c, SCONV - 1:])) for c in range(XT)]
    tiles += [(6, cols(2 * P, SH), i, "dve", lambda dve, ps, i: dve.tensor_copy(A.dt[:, i, :], ps[:, 0:SH]))
              for i in range(TT)]
    project(nc, M, "proj1", chunks, tiles, 1, others=[(M.bias[:], M.bias_dram)])


def mixer1_local(nc, M, A, I, l):
    with stage(nc, "local", "w0_landed w1_landed w_half_used pe_landed small_landed ws_landed cmp_sum bias_col "
               "hidden keys_ready taps_padded conv_acc conv_done ws_turned ws_copied "
               "v_normed spatial act_chain dve_chain var_ready root_ready exp_ready one_plus ln_ready") as (block, S):
        w_landed = [S.w0_landed, S.w1_landed]
        slots = [M.wide[:, s].rearrange("p a k n -> p (a k n)").rearrange("p (l n) -> p l n", l=16) for s in range(2)]

        @block.sync
        def _(sp):
            with nc.allow_non_contiguous_dma(reason="small vectors as columns"):
                for j in range(2):
                    for g in range(GROUPS):
                        sp.dma_start(A.blk[HD * g:HD * (g + 1), j, :, N_CMP], I.cmp_pe[l, j].rearrange("l d -> d l")
                                     ).then_inc(S.pe_landed, 16)
            for n in range(4):
                if n >= 2:
                    sp.wait_ge(S.w_half_used, n - 1)
                src = I.cmp_w1[l, n // 2].rearrange("(l d) n -> d l n", d=HD)[:, 16 * (n % 2):16 * (n % 2) + 16, :]
                for g in range(GROUPS):
                    sp.dma_start(slots[n % 2][HD * g:HD * (g + 1)], src).then_inc(w_landed[n % 2], 16)
            with nc.allow_non_contiguous_dma(reason="small vectors as columns"):
                sp.dma_start(A.cmp_b[:], I.cmp_b1[l].rearrange("j (m p) -> p (j m)", p=P)).then_inc(S.small_landed, 16)
                sp.dma_start(A.conv_w[:], I.ssm_conv_w[l].rearrange("j (c p) -> p j c", p=P)).then_inc(S.small_landed, 16)
                sp.dma_start(A.conv_b[:], I.ssm_conv_b[l].rearrange("(c p) -> p c", p=P)).then_inc(S.small_landed, 16)
                sp.dma_start(A.ws_b[:], I.gmlp_bs[l].rearrange("g p -> p g")).then_inc(S.small_landed, 16)
            for j in range(2):
                for g in range(GROUPS):
                    sp.dma_start(A.cmp_w2[:, j, :, g, :], I.cmp_w2[l, j].rearrange("(m p) d -> p m d", p=P)
                                 ).then_inc(S.small_landed, 16)
            for dst, vector in ((A.dt_bias, I.ssm_dt_bias), (A.a_log, I.ssm_a_log), (A.d_skip, I.ssm_d),
                                (A.norm_g, I.ssm_norm_g), (A.ln_g, I.gmlp_ln_g), (A.ln_b, I.gmlp_ln_b)):
                sp.dma_start(dst[:], vector[l].partition_broadcast(P)).then_inc(S.small_landed, 16)
            sp.dma_start(A.ws[:], I.gmlp_ws[l].rearrange("g t s -> t g s")).then_inc(S.ws_landed, 16)

        small = 16 * 14

        @block.tensor
        def _(pe):
            pe.wait_ge(S.pe_landed, 64)
            for n in range(4):
                j, half = n // 2, n % 2
                pe.wait_ge(w_landed[n % 2], 32 * (n // 2 + 1))
                for m in range(2):
                    for g in range(GROUPS):
                        rows = slice(HD * g, HD * (g + 1))
                        for q in range(16):
                            mm = pe.matmul(M.ps[:, 4 * j + 2 * m + g, 0:N_CMP + 1],
                                           slots[n % 2][rows, q, m * P:(m + 1) * P], A.blk[rows, j, 16 * half + q, :],
                                           start=(half == 0 and q == 0), stop=(half == 1 and q == 15))
                mm.then_inc(S.w_half_used, 1)
            pe.wait_ge(S.hidden, 4)
            pe.wait_ge(S.small_landed, small)
            for g in range(GROUPS):
                for m in range(2):
                    mm = pe.matmul(M.ps[:, g, 0:N_CMP], A.cmp_w2[:, 0, m].rearrange("p g d -> p (g d)"),
                                   A.cmp_h[:, 0, m, g, :], start=(m == 0), stop=(m == 1))
            pe.wait_ge(S.hidden, 8)
            for g in range(GROUPS):
                for m in range(2):
                    mm = pe.matmul(M.ps[0:N_CMP, 2 + g, 0:HD], A.cmp_h[:, 1, m, g, :], A.cmp_w2[:, 1, m, 0, :],
                                   start=(m == 0), stop=(m == 1))
            mm.then_inc(S.keys_ready, 1)
            pe.wait_ge(S.ws_landed, 16)
            for g in range(GG):
                mm = pe.transpose(M.ps[:, 4, g * P:(g + 1) * P], A.ws[:, g, :], M.ident[:])
            mm.then_inc(S.ws_turned, 1)
            pe.wait_ge(S.ws_copied, 1)
            pe.wait_ge(S.v_normed, 1)
            for g in range(GG):
                rhs = A.uv[:, :, D_GMLP + GGD * g:D_GMLP + GGD * (g + 1)]
                out = M.ps[:, 5 + g // 2, (g % 2) * 256:(g % 2) * 256 + 256].rearrange("p (c d) -> p c d", c=TT)
                mm = pe.matmul(out, A.wsT[:, g, :], rhs, start=True, stop=True)
            mm.then_inc(S.spatial, 1)

        @block.scalar
        def _(act):
            link = chain(act, S.act_chain)
            act.wait_ge(S.small_landed, small)
            link(act.activation(A.a_neg[:], A.a_log[:], ACT.Exp))
            act.wait_ge(S.one_plus, 1)
            act.activation(A.dt_e[:], A.dt_e[:], ACT.Exp, scale=-1.0).then_inc(S.exp_ready, 1)
            act.wait_ge(S.one_plus, 2)
            act.activation(A.dt_ln[:], A.dt_u[:], ACT.Ln).then_inc(S.ln_ready, 1)
            for c in range(XT):
                act.wait_ge(S.conv_acc, SCONV * (c + 1))
                act.activation(A.xbc[:, c, :], A.xbc[:, c, :], ACT.Silu, bias=A.conv_b[:, c:c + 1]).then_inc(S.conv_done, 1)
            for j in range(2):
                act.wait_ge(S.bias_col, j + 1)
                for m in range(2):
                    for g in range(GROUPS):
                        act.activation(A.cmp_h[:, j, m, g, :], M.ps[:, 4 * j + 2 * m + g, 0:N_CMP], ACT.Gelu_apprx_tanh,
                                       bias=A.cmp_b[:, 2 * j + m:2 * j + m + 1]).then_inc(S.hidden, 1)
            act.wait_ge(S.var_ready, 1)
            act.activation(A.root[:, 0:TT], A.root[:, 0:TT], ACT.Sqrt).then_inc(S.root_ready, 1)

        @block.vector
        def _(dve):
            dve.memset(A.raw[:, :, 0:SCONV - 1], 0.0).then_inc(S.taps_padded, 1)
            dve.wait_ge(S.taps_padded, 1)
            dve.wait_ge(S.small_landed, small)
            link = chain(dve, S.dve_chain)
            link(dve.tensor_tensor(A.dt[:], A.dt[:], A.dt_bias[:].unsqueeze(1).to_broadcast([P, TT, SH]), ALU.add))
            dve.scalar_tensor_tensor(out=A.dt_e[:], in0=A.dt[:], scalar=-1.0, in1=A.dt[:], op0=ALU.mult,
                                     op1=ALU.max).then_inc(S.one_plus, 1)
            dve.wait_ge(S.exp_ready, 1)
            dve.tensor_scalar(A.dt_u[:], A.dt_e[:], 1.0, None, ALU.add).then_inc(S.one_plus, 1)
            dve.wait_ge(S.one_plus, 2)
            link(dve.scalar_tensor_tensor(out=A.dt_r[:], in0=A.dt_u[:], scalar=-1.0, in1=A.dt_e[:], op0=ALU.add,
                                          op1=ALU.subtract))
            link(dve.tensor_scalar(A.dt[:], A.dt[:], 0.0, None, ALU.max))
            link(dve.tensor_tensor(A.dt[:], A.dt[:], A.dt_r[:], ALU.subtract))
            dve.wait_ge(S.ln_ready, 1)
            link(dve.tensor_tensor(A.dt[:], A.dt[:], A.dt_ln[:], ALU.add))
            dve.wait_ge(S.act_chain, 1)
            link(dve.scalar_tensor_tensor(out=A.a[:], in0=A.dt[:], scalar=-1.0,
                                          in1=A.a_neg[:].unsqueeze(1).to_broadcast([P, TT, SH]),
                                          op0=ALU.mult, op1=ALU.mult))
            for c in range(XT):
                dve.tensor_scalar(A.xbc[:, c, :], A.raw[:, c, 0:T], A.conv_w[:, 0, c:c + 1], None,
                                  ALU.mult).then_inc(S.conv_acc, 1)
                for j in range(1, SCONV):
                    dve.wait_ge(S.conv_acc, SCONV * c + j)
                    dve.scalar_tensor_tensor(out=A.xbc[:, c, :], in0=A.raw[:, c, j:j + T],
                                             scalar=A.conv_w[:, j, c:c + 1], in1=A.xbc[:, c, :],
                                             op0=ALU.mult, op1=ALU.add).then_inc(S.conv_acc, 1)
            for i in range(TT):
                link(dve.bn_stats(A.stats[:, i, :], A.uv[:, i, D_GMLP:]))
            for i in range(TT):
                link(dve.bn_aggr(A.mv[:, i, :], A.stats[:, i, :]))
            dve.tensor_scalar(A.root[:, 0:TT], A.mv[:, :, 1], LN_EPS, None, ALU.add).then_inc(S.var_ready, 1)
            for j in range(2):
                dve.wait_ge(S.w_half_used, 2 * j + 2)
                for m in range(2):
                    link(dve.tensor_tensor(A.cmp_b[:, 2 * j + m:2 * j + m + 1], A.cmp_b[:, 2 * j + m:2 * j + m + 1],
                                           M.ps[:, 4 * j + 2 * m, N_CMP:N_CMP + 1], ALU.add))
                dve.sem_inc(S.bias_col, 1)
            dve.wait_ge(S.root_ready, 1)
            link(dve.reciprocal(A.root[:, 0:TT], A.root[:, 0:TT]))
            for i in range(TT):
                v = A.uv[:, i, D_GMLP:]
                link(dve.tensor_scalar(v, v, A.mv[:, i, 0:1], A.root[:, i:i + 1], ALU.subtract, ALU.mult))
                link(dve.tensor_tensor(v, v, A.ln_g[:], ALU.mult))
                ins = dve.tensor_tensor(v, v, A.ln_b[:], ALU.add)
            ins.then_inc(S.v_normed, 1)
            dve.wait_ge(S.keys_ready, 1)
            for g in range(GROUPS):
                dve.tensor_copy(A.kcT[HD * g:HD * (g + 1), :], M.ps[HD * g:HD * (g + 1), g, 0:N_CMP])
                dve.tensor_copy(A.vc[0:N_CMP, g, :], M.ps[0:N_CMP, 2 + g, 0:HD])
            dve.wait_ge(S.ws_turned, 1)
            dve.tensor_tensor(A.wsT[:], M.ps[:, 4, :].rearrange("p (g t) -> p g t", g=GG),
                              M.tri[:, 3 * P:4 * P].unsqueeze(1).to_broadcast([P, GG, P]),
                              ALU.mult).then_inc(S.ws_copied, 1)
            dve.wait_ge(S.spatial, 1)
            for g in range(GG):
                ps = M.ps[:, 5 + g // 2, (g % 2) * 256:(g % 2) * 256 + 256].rearrange("p (c d) -> p c d", c=TT)
                dve.scalar_tensor_tensor(out=A.mix[:, :, HEADS * HD + GGD * g:HEADS * HD + GGD * (g + 1)], in0=ps,
                                         scalar=A.ws_b[:, g:g + 1], in1=A.uv[:, :, GGD * g:GGD * (g + 1)],
                                         op0=ALU.add, op1=ALU.mult)


def mixer1_compressed(nc, M, A):
    with stage(nc, "cmp", "bias_init bias_c scores chain shifted probs normed turned turned_copied pv mixed") as (block, S):

        @block.tensor
        def _(pe):
            def outputs(i):
                pe.wait_ge(S.normed, i + 1)
                if i >= 2:
                    pe.wait_ge(S.turned_copied, i - 1)
                for h in range(HEADS):
                    mm = pe.transpose(M.ps[0:N_CMP, 4 * (i % 2) + 1 + h // 4, (h % 4) * P:(h % 4 + 1) * P], A.score_c[:, i, h, :],
                                      M.ident[:])
                mm.then_inc(S.turned, 1)
                pe.wait_ge(S.turned_copied, i + 1)
                for h in range(HEADS):
                    mm = pe.matmul(M.ps[:, 4 * (i % 2) + 3, HD * h:HD * (h + 1)], A.turned_c[0:N_CMP, i % 2, h * P:(h + 1) * P],
                                   A.vc[0:N_CMP, h // HPG, :], start=True, stop=True)
                mm.then_inc(S.pv, 1)

            for i in range(TT):
                if i >= 2:
                    pe.wait_ge(S.mixed, i - 1)
                for h in range(HEADS):
                    rows = slice(HD * (h // HPG), HD * (h // HPG + 1))
                    mm = pe.matmul(M.ps[:, 4 * (i % 2) + 3 * (h // HPG), N_CMP * (h % HPG):N_CMP * (h % HPG + 1)], A.qT[rows, h % HPG, i * P:(i + 1) * P],
                                   A.kcT[rows, :], start=True, stop=True)
                mm.then_inc(S.scores, 1)
                if i >= 1:
                    outputs(i - 1)
            outputs(TT - 1)

        @block.scalar
        def _(act):
            for i in range(TT):
                act.wait_ge(S.shifted, i + 1)
                act.activation(A.score_c[:, i], A.score_c[:, i], ACT.Exp).then_inc(S.probs, 1)

        @block.vector
        def _(dve):
            dve.memset(A.bias_c[:], MASKED).then_inc(S.bias_init, 1)
            dve.wait_ge(S.bias_init, 1)
            for i in range(TT):
                start = (TT - 1 - i) * P + CMP_LEN - 1
                n = min(N_CMP, -(-(T - start) // CMP_STRIDE))
                ins = dve.tensor_copy(A.bias_c[:, i, :, 0:n], A.bias_all[:, :, start:start + CMP_STRIDE * (n - 1) + 1:CMP_STRIDE])
            ins.then_inc(S.bias_c, 1)
            dve.wait_ge(S.bias_c, 1)
            link = chain(dve, S.chain)
            spread = lambda ap: ap.unsqueeze(2).to_broadcast([P, HEADS, N_CMP])

            def probabilities(i):
                s, d = A.score_c[:, i], A.denom_c[:, i, :]
                dve.wait_ge(S.scores, i + 1)
                for g in range(GROUPS):
                    heads = slice(HPG * g, HPG * (g + 1))
                    link(dve.tensor_tensor(s[:, heads], M.ps[:, 4 * (i % 2) + 3 * g, 0:HPG * N_CMP]
                                           .rearrange("p (h n) -> p h n", h=HPG), A.bias_c[:, i, heads], ALU.add))
                link(dve.tensor_reduce(d, s, AX.X, ALU.max))
                link(dve.tensor_scalar(d, d, FLOOR, None, ALU.max))
                dve.tensor_tensor(s, s, spread(d), ALU.subtract).then_inc(S.shifted, 1)

            def normalise(i):
                s, d = A.score_c[:, i], A.denom_c[:, i, :]
                dve.wait_ge(S.probs, i + 1)
                link(dve.tensor_reduce(d, s, AX.X, ALU.add))
                link(dve.tensor_scalar(d, d, 1e-30, None, ALU.max))
                link(dve.reciprocal(d, d))
                gates = A.gates[:, i, :].rearrange("p (h b) -> p h b", b=N_BRANCH)[:, :, 0]
                link(dve.tensor_tensor(d, d, gates, ALU.mult))
                dve.tensor_tensor(s, s, spread(d), ALU.mult).then_inc(S.normed, 1)

            def outputs(i):
                if i >= 2:
                    dve.wait_ge(S.pv, i - 1)
                dve.wait_ge(S.turned, i + 1)
                dve.tensor_copy(A.turned_c[0:N_CMP, i % 2, 0:4 * P], M.ps[0:N_CMP, 4 * (i % 2) + 1, :])
                dve.tensor_copy(A.turned_c[0:N_CMP, i % 2, 4 * P:], M.ps[0:N_CMP, 4 * (i % 2) + 2, :]).then_inc(S.turned_copied, 1)
                dve.wait_ge(S.pv, i + 1)
                dve.tensor_copy(A.mix[:, i, 0:HEADS * HD], M.ps[:, 4 * (i % 2) + 3, :]).then_inc(S.mixed, 1)

            probabilities(0)
            for i in range(TT):
                normalise(i)
                if i + 1 < TT:
                    probabilities(i + 1)
                outputs(i)


def mixer1_attention(nc, M, A):
    units = [(i, h) for i in range(TT) for h in range(HEADS)]
    N = len(units)
    with stage(nc, "attn", "scores score_biased row_max shifted probs turned slc_copied "
               "win_copied pv mixed denominators norm_chain") as (block, S):

        def branch_bias(i, h):
            start = (TT - 1 - i) * P
            return A.bias_all[:, h, start:start + (i + 1) * P]

        @block.tensor
        def _(pe):
            def scores(u):
                i, h = units[u]
                g, a = h // HPG, h % HPG
                rows, keys = slice(HD * g, HD * (g + 1)), (i + 1) * P
                q = A.qT[rows, a, i * P:(i + 1) * P]
                if u >= 2:
                    pe.wait_ge(S.score_biased, u - 1)
                pe.matmul(M.ps[:, 2 * (u % 2), 0:keys], q, A.ksT[rows, 0:keys], start=True, stop=True)
                pe.matmul(M.ps[:, 2 * (u % 2) + 1, 0:keys], q, A.kwT[rows, 0:keys], start=True, stop=True
                          ).then_inc(S.scores, 1)

            def turn(u):
                i, h = units[u]
                pe.wait_ge(S.probs, u + 1)
                if u >= 1:
                    pe.wait_ge(S.slc_copied, u)
                    pe.wait_ge(S.win_copied, u)
                for j in range(i + 1):
                    pe.transpose(M.ps[:, 6, j * P:(j + 1) * P], A.probs[:, u % 2, 0, j * P:(j + 1) * P], M.ident[:])
                for j in range(i + 1):
                    mm = pe.transpose(M.ps[:, 7, j * P:(j + 1) * P], A.probs[:, u % 2, 1, j * P:(j + 1) * P], M.ident[:])
                mm.then_inc(S.turned, 1)

            def values(u):
                i, h = units[u]
                cols = slice(HD * (h // HPG), HD * (h // HPG + 1))
                bank = M.ps[:, 4 + u % 2, :]
                pe.wait_ge(S.slc_copied, u + 1)
                pe.wait_ge(S.win_copied, u + 1)
                if u >= 2:
                    pe.wait_ge(S.mixed, u - 1)
                for j in range(i + 1):
                    pe.matmul(bank[:, 0:HD], A.turned[:, u % 2, 0, j * P:(j + 1) * P], A.vs[:, j, cols],
                              start=(j == 0), stop=(j == i))
                for j in range(i + 1):
                    mm = pe.matmul(bank[:, HD:2 * HD], A.turned[:, u % 2, 1, j * P:(j + 1) * P], A.vw[:, j, cols],
                                   start=(j == 0), stop=(j == i))
                mm.then_inc(S.pv, 1)

            for step in range(N + 2):
                if step < N:
                    scores(step)
                if step >= 2:
                    values(step - 2)
                if 1 <= step <= N:
                    turn(step - 1)

        @block.scalar
        def _(act):
            def exps(u):
                i, h = units[u]
                keys = (i + 1) * P
                act.wait_ge(S.shifted, u + 1)
                if u >= 2:
                    act.wait_ge(S.turned, u - 1)
                for b in range(2):
                    ins = act.activation(A.probs[:, u % 2, b, 0:keys], A.score[:, u % 2, b, 0:keys], ACT.Exp,
                                         bias=A.shift[:, u % 2, b:b + 1], accum_out=A.sums[:, u % 2, b:b + 1])
                ins.then_inc(S.probs, 1)

            def copy(u):
                i, h = units[u]
                act.wait_ge(S.turned, u + 1)
                if u >= 2:
                    act.wait_ge(S.pv, u - 1)
                act.copy(A.turned[:, u % 2, 0, 0:(i + 1) * P], M.ps[:, 6, 0:(i + 1) * P]).then_inc(S.slc_copied, 1)

            for step in range(N + 1):
                if step < N:
                    exps(step)
                if step >= 1:
                    copy(step - 1)

        @block.vector
        def _(dve):
            def biased(u):
                i, h = units[u]
                keys = (i + 1) * P
                dve.wait_ge(S.scores, u + 1)
                if u >= 2:
                    dve.wait_ge(S.probs, u - 1)
                for b in range(2):
                    ins = dve.tensor_tensor_reduce(A.score[:, u % 2, b, 0:keys], M.ps[:, 2 * (u % 2) + b, 0:keys],
                                                   branch_bias(i, h), 1.0, FLOOR, ALU.add, ALU.max,
                                                   A.top[:, u % 2, b:b + 1])
                ins.then_inc(S.score_biased, 1)
                dve.wait_ge(S.score_biased, u + 1)
                dve.tensor_scalar(A.shift[:, u % 2, :], A.top[:, u % 2, :], FLOOR, -1.0, ALU.max, ALU.mult
                                  ).then_inc(S.shifted, 1)

            def copy(u):
                i, h = units[u]
                dve.wait_ge(S.turned, u + 1)
                if u >= 2:
                    dve.wait_ge(S.pv, u - 1)
                dve.tensor_copy(A.turned[:, u % 2, 1, 0:(i + 1) * P], M.ps[:, 7, 0:(i + 1) * P]).then_inc(S.win_copied, 1)

            def combine(u):
                i, h = units[u]
                n = 4 * u
                d, out = A.denom[:, u % 2, :], A.mix[:, i, HD * h:HD * (h + 1)]
                dve.tensor_scalar(d, A.sums[:, u % 2, :], 1e-30, None, ALU.max).then_inc(S.norm_chain, 1)
                dve.wait_ge(S.norm_chain, n + 1)
                dve.reciprocal(d, d).then_inc(S.norm_chain, 1)
                dve.wait_ge(S.norm_chain, n + 2)
                dve.tensor_tensor(d, d, A.gates[:, i, N_BRANCH * h + 1:N_BRANCH * (h + 1)],
                                  ALU.mult).then_inc(S.norm_chain, 1)
                dve.wait_ge(S.norm_chain, n + 3)
                dve.wait_ge(S.pv, u + 1)
                bank = M.ps[:, 4 + u % 2, :]
                dve.scalar_tensor_tensor(out=out, in0=bank[:, 0:HD], scalar=d[:, 0:1], in1=out, op0=ALU.mult,
                                         op1=ALU.add).then_inc(S.norm_chain, 1)
                dve.wait_ge(S.norm_chain, n + 4)
                dve.scalar_tensor_tensor(out=out, in0=bank[:, HD:2 * HD], scalar=d[:, 1:2], in1=out, op0=ALU.mult,
                                         op1=ALU.add).then_inc(S.mixed, 1)

            for step in range(N + 2):
                if step >= 2:
                    combine(step - 2)
                if step < N:
                    biased(step)
                if 1 <= step <= N:
                    copy(step - 1)


def mixer1_ssd(nc, M, A):
    hpg = SH // SG
    with stage(nc, "ssd", "x_turned x_copied sums_col col_copied sums_row cb diff decay kept weighted "
               "y_ready chain squares_done root_ready gated") as (block, S):
        tri = lambda k, n0, n1: M.tri[:, 3 * P - k * P + n0:3 * P - k * P + n1]
        steps = [(g, k) for g in range(SG) for k in range(TT)]

        @block.tensor
        def _(pe):
            for c in range(2):
                for i in range(TT):
                    mm = pe.transpose(M.ps[:, c, i * P:(i + 1) * P], A.xbc[:, c, i * P:(i + 1) * P], M.ident[:])
                mm.then_inc(S.x_turned, 1)
            for k in range(TT):
                for j in range(k + 1):
                    mm = pe.matmul(M.ps[:, 2, SH * k:SH * (k + 1)], tri(j, k * P, (k + 1) * P), A.a[:, j, :],
                                   start=(j == 0), stop=(j == k))
            mm.then_inc(S.sums_col, 1)
            for h in range(SH):
                for j in range(TT):
                    mm = pe.matmul(M.ps[:, 4 + h, :], A.a[:, j, h:h + 1].to_broadcast([P, P]), tri(j, 0, T),
                                   start=(j == 0), stop=(j == TT - 1))
                mm.then_inc(S.sums_row, 1)
            pe.wait_ge(S.x_copied, 2)
            for n, (g, k) in enumerate(steps):
                if n >= 2:
                    pe.wait_ge(S.weighted, hpg * (n - 1))
                if n < 2:
                    pe.wait_ge(S.col_copied, 1)
                pe.matmul(M.ps[:, n % 2, k * P:T], A.xbc[:, 2 + g, k * P:(k + 1) * P], A.xbc[:, 2 + SG + g, k * P:T],
                          start=True, stop=True).then_inc(S.cb, 1)
            pe.wait_ge(S.weighted, hpg * len(steps))
            for i in range(TT):
                for h in range(SH):
                    for k in range(i + 1):
                        mm = pe.matmul(M.ps[:, 2 + i // 2, (i % 2) * 256 + HD * h:(i % 2) * 256 + HD * (h + 1)],
                                       A.decay[:, h, k, i * P:(i + 1) * P], A.xdt[:, k, h * HD:(h + 1) * HD],
                                       start=(k == 0), stop=(k == i))
            mm.then_inc(S.y_ready, 1)

        @block.scalar
        def _(act):
            n = 0
            for g, k in steps:
                for h in range(hpg * g, hpg * (g + 1)):
                    n += 1
                    act.wait_ge(S.diff, n)
                    act.activation(A.decay[:, h, k, k * P:T], A.decay[:, h, k, k * P:T], ACT.Exp).then_inc(S.decay, 1)
            act.wait_ge(S.squares_done, 1)
            act.activation(A.root[:], A.root[:], ACT.Sqrt).then_inc(S.root_ready, 1)

        @block.vector
        def _(dve):
            link = chain(dve, S.chain)
            for c in range(2):
                dve.wait_ge(S.x_turned, c + 1)
                dve.tensor_copy(A.xs[:, :, c * P:(c + 1) * P], M.ps[:, c, :].rearrange("p (i d) -> p i d", i=TT)
                                ).then_inc(S.x_copied, 1)
            dve.wait_ge(S.x_copied, 2)
            link(dve.tensor_tensor(A.xdt[:].rearrange("p i (h d) -> p (i h) d", h=SH),
                                   A.xs[:].rearrange("p i (h d) -> p (i h) d", h=SH),
                                   A.dt[:].rearrange("p i h -> p (i h)").unsqueeze(2).to_broadcast([P, TT * SH, HD]), ALU.mult))
            dve.wait_ge(S.sums_col, 1)
            dve.tensor_copy(A.cs[:], M.ps[:, 2, 0:SH * TT]).then_inc(S.col_copied, 1)
            dve.wait_ge(S.col_copied, 1)
            units = [(g, k, h) for g, k in steps for h in range(hpg * g, hpg * (g + 1))]

            def difference(n):
                g, k, h = units[n]
                dve.wait_ge(S.sums_row, h + 1)
                dve.tensor_scalar(A.decay[:, h, k, k * P:T], M.ps[:, 4 + h, k * P:T], A.cs[:, SH * k + h:SH * k + h + 1],
                                  0.0, ALU.subtract, ALU.min).then_inc(S.diff, 1)

            def weigh(n):
                g, k, h = units[n]
                dve.wait_ge(S.decay, n + 1)
                dve.wait_ge(S.cb, n // hpg + 1)
                link(dve.tensor_tensor(A.decay[:, h, k, k * P:T], A.decay[:, h, k, k * P:T], tri(0, 0, T - k * P), ALU.mult))
                dve.tensor_tensor(A.decay[:, h, k, k * P:T], A.decay[:, h, k, k * P:T], M.ps[:, (n // hpg) % 2, k * P:T],
                                  ALU.mult).then_inc(S.weighted, 1)

            difference(0)
            difference(1)
            for n in range(len(units)):
                if n + 2 < len(units):
                    difference(n + 2)
                weigh(n)
            out = A.mix[:, :, HEADS * HD + D_GMLP:]
            heads = lambda ap: ap.rearrange("p i (h d) -> p i h d", h=SH)
            for i in range(TT):
                link(dve.tensor_tensor(out[:, i, :].rearrange("p (h d) -> p h d", h=SH),
                                       A.xs[:, i, :].rearrange("p (h d) -> p h d", h=SH),
                                       A.d_skip[:].unsqueeze(2).to_broadcast([P, SH, HD]), ALU.mult))
            dve.wait_ge(S.y_ready, 1)
            for i in range(2):
                pair = out[:, 2 * i:2 * i + 2, :]
                link(dve.tensor_tensor(pair, pair, M.ps[:, 2 + i, :].rearrange("p (i d) -> p i d", i=2), ALU.add))
            link(dve.tensor_tensor(out, out, A.silz[:], ALU.mult))
            link(dve.tensor_tensor(A.xdt[:], out, out, ALU.mult))
            link(dve.tensor_reduce(A.root[:], A.xdt[:].rearrange("p i (g d) -> p (i g) d", g=SG), AX.X, ALU.add))
            dve.tensor_scalar(A.root[:], A.root[:], SG / D_SSM, LN_EPS, ALU.mult, ALU.add).then_inc(S.squares_done, 1)
            dve.wait_ge(S.root_ready, 1)
            link(dve.reciprocal(A.root[:], A.root[:]))
            for i in range(TT):
                o = out[:, i, :]
                og = o.rearrange("p (g d) -> p g d", g=SG)
                link(dve.tensor_tensor(og, og, A.root[:, SG * i:SG * (i + 1)].unsqueeze(2).to_broadcast([P, SG, D_SSM // SG]),
                                       ALU.mult))
                link(dve.tensor_tensor(o, o, A.norm_g[:], ALU.mult))


def mix_out(nc, M, tag, mix, turned, w_out, sub):
    w = w_out.rearrange("(k p) n -> p k n", p=P)
    wide = M.wide[:].rearrange("p s a k n -> p (s a k n)").rearrange("p (k n) -> p k n", k=DT)
    with stage(nc, tag, "w0_landed w1_landed mix_turned mix_copied y_ready" + NORM_SIGNALS) as (block, S):
        landed = [S.w0_landed, S.w1_landed]
        tiles = [k for k in range(DT) if k not in turned]

        @block.sync
        def _(sp):
            for s in range(2):
                sp.dma_start(wide[:, 4 * s:4 * s + 4, :], w[:, 4 * s:4 * s + 4, :]).then_inc(landed[s], 16)

        @block.tensor
        def _(pe):
            for n, k in enumerate(tiles):
                for i in range(TT):
                    mm = pe.transpose(M.ps[:, n, i * P:(i + 1) * P], mix[:, i, k * P:(k + 1) * P], M.ident[:])
                mm.then_inc(S.mix_turned, 1)
            pe.wait_ge(S.mix_copied, len(tiles))
            pe.wait_ge(landed[0], 16)
            pe.wait_ge(landed[1], 16)
            for d in range(DT):
                for k in range(DT):
                    mm = pe.matmul(M.ps[:, d, :], wide[:, k, d * P:(d + 1) * P], M.hT[:, k, :], start=(k == 0),
                                   stop=(k == DT - 1))
                mm.then_inc(S.y_ready, 1)
            if sub is not None:
                post_norm_pe(pe, M, S)

        @block.scalar
        def _(act):
            for n, k in enumerate(tiles):
                if n % 2:
                    act.wait_ge(S.mix_turned, n + 1)
                    act.copy(M.hT[:, k, :], M.ps[:, n, :]).then_inc(S.mix_copied, 1)
            if sub is not None:
                post_norm_act(act, M, S, sub)

        @block.vector
        def _(dve):
            for n, k in enumerate(tiles):
                if n % 2 == 0:
                    dve.wait_ge(S.mix_turned, n + 1)
                    dve.tensor_copy(M.hT[:, k, :], M.ps[:, n, :]).then_inc(S.mix_copied, 1)
            if sub is not None:
                post_norm_dve(dve, M, S, sub)
            else:
                for d in range(DT):
                    dve.wait_ge(S.y_ready, d + 1)
                    dve.tensor_tensor(M.x[:, d, :], M.x[:, d, :], M.ps[:, d, :], ALU.add)


def mixer1(nc, M, I, l):
    with ExitStack() as memory:
        sb = tensors(nc, memory, "a_")
        A = Memory()
        M.hT, M.wide, M.bias = sb("hT", DT, T), sb("wide", 2, 2, DT, 256), sb("bias", HEADS, T)
        A.bias_all = M.bias
        A.mix = sb("mix", TT, D)
        A.qT = sb("qT", HPG, T)
        A.ksT, A.kwT = sb("ksT", T), sb("kwT", T)
        A.vs, A.vw = sb("vs", TT, KV), sb("vw", TT, KV)
        A.gates = sb("gates", TT, HEADS * N_BRANCH)
        A.kcT, A.vc = sb("kcT", N_CMP), sb("vc", GROUPS, HD)
        A.silz, A.dt, A.a = sb("silz", TT, D_SSM), sb("dt", TT, SH), sb("a", TT, SH)
        A.xbc = sb("xbc", XT, T)
        A.d_skip, A.norm_g = sb("d_skip", SH), sb("norm_g", D_SSM)
        A.root = sb("root", TT * SG)
        with ExitStack() as inner:
            sb = tensors(nc, inner, "a_")
            A.uv = sb("uv", TT, 2 * D_GMLP)
            A.raw = sb("raw", XT, T + SCONV - 1)
            A.blk = sb("blk", 2, CMP_LEN, N_CMP + 1)
            A.cmp_b, A.cmp_w2 = sb("cmp_b", 4), sb("cmp_w2", 2, 2, GROUPS, HD)
            A.cmp_h = sb("cmp_h", 2, 2, GROUPS, N_CMP)
            A.conv_w, A.conv_b = sb("conv_w", SCONV, XT), sb("conv_b", XT)
            A.ws, A.wsT, A.ws_b = sb("ws", GG, P), sb("wsT", GG, P), sb("ws_b", GG)
            A.ln_g, A.ln_b = sb("ln_g", D_GMLP), sb("ln_b", D_GMLP)
            A.dt_bias, A.a_log, A.a_neg = sb("dt_bias", SH), sb("a_log", SH), sb("a_neg", SH)
            A.dt_e, A.dt_u, A.dt_r, A.dt_ln = (sb(f"dt_{x}", TT, SH) for x in "eurl")
            A.stats, A.mv = sb("stats", TT, 6), sb("mv", TT, 2)
            mixer1_project(nc, M, A, I, l)
            mixer1_local(nc, M, A, I, l)
        with ExitStack() as inner:
            sb = tensors(nc, inner, "a_")
            A.bias_c, A.score_c = sb("bias_c", TT, HEADS, N_CMP), sb("score_c", TT, HEADS, N_CMP)
            A.turned_c, A.denom_c = sb("turned_c", 2, HEADS * P), sb("denom_c", TT, HEADS)
            mixer1_compressed(nc, M, A)
        with ExitStack() as inner:
            sb = tensors(nc, inner, "a_")
            A.score, A.probs, A.turned = sb("score", 2, 2, T), sb("probs", 2, 2, T), sb("turned", 2, 2, T)
            A.top, A.shift, A.sums, A.denom = (sb(x, 2, 2) for x in ("top", "shift", "sums", "denom"))
            mixer1_attention(nc, M, A)
        with ExitStack() as inner:
            sb = tensors(nc, inner, "a_")
            A.xs, A.xdt = sb("xs", TT, D_SSM), sb("xdt", TT, D_SSM)
            A.cs = sb("cs", TT * SH)
            A.decay = sb("decay", SH, TT, T)
            mixer1_ssd(nc, M, A)
        mix_out(nc, M, "out1", A.mix, (), I.w_out[l], 1)


def sum_selectors():
    out = np.zeros((P, 7 * 32), np.float32)
    out[:, 96:128] = 1
    return out


def spread_selectors():
    out = np.zeros((P, 4, P), np.float32)
    for u in range(4):
        out[32 * u, u] = 1
    return out


def mixer2_project(nc, M, A, I, l):
    w = I.w_in_2[l].rearrange("(k p) n -> p k n", p=P)
    z, ba = 3 * DW, 4 * DW
    sc = ba + 2 * DH
    bounds = [0, DW, 2 * DW, z, ba, sc, sc + SCW, sc + 2 * SCW, W2_COLS]
    chunks = [[(slice(0, b - a), w[:, :, a:b])] for a, b in zip(bounds, bounds[1:])]
    cols = lambda a, n: slice(a, a + n)

    def act_copy(dst):
        return lambda act, ps, i: act.copy(dst, ps)

    def dve_copy(dst):
        return lambda dve, ps, i: dve.tensor_copy(dst, ps)

    tiles = []
    for c in range(3):
        for h in range(DH):
            dst = A.raw[:, DH * c + h, DCONV - 1:]
            tiles.append((c, cols(P * h, P), None, "dve" if h % 2 else "act", (dve_copy if h % 2 else act_copy)(dst)))
    tiles += [(3, cols(0, DW), i, "act", lambda act, ps, i: act.activation(A.silz[:, i, :], ps, ACT.Silu)) for i in range(TT)]
    tiles += [(4, cols(0, 2 * DH), i, "dve", lambda dve, ps, i: dve.tensor_copy(A.ba[:, i, :], ps[:, 0:2 * DH]))
              for i in range(TT)]
    tiles += [(5, cols(P * c, P), None, "dve", dve_copy(A.gate_b[:, c, :])) for c in range(SCT)]
    tiles += [(6, cols(P * c, P), None, "act", act_copy(A.gate_c[:, c, :])) for c in range(SCT)]
    tiles += [(7, cols(P * c, P), None, "dve", dve_copy(A.prod[:, c, SCCONV - 1:])) for c in range(SCT)]
    project(nc, M, "proj2", chunks, tiles, None, gain=I.norm1_g_2[l])


def mixer2_conv(nc, M, A, I, l):
    with stage(nc, "conv2", "small_landed padded conv conv_y gated silu_done square_ready square_used summed root_ready "
               "inverse_ready spread scaled act_chain dve_chain exp_ready one_plus ln_ready") as (block, S):

        @block.sync
        def _(sp):
            with nc.allow_non_contiguous_dma(reason="small vectors as columns"):
                for j in range(DCONV):
                    sp.dma_start(A.conv_w[:, j, :], I.dn_conv_w_2[l, j].rearrange("(c p) -> p c", p=P)).then_inc(S.small_landed, 16)
                for j in range(SCCONV):
                    sp.dma_start(A.sc_w[:, j, :], I.sc_conv_w_2[l, j].rearrange("(c p) -> p c", p=P)).then_inc(S.small_landed, 16)
                sp.dma_start(A.sc_g[:], I.sc_norm_g_2[l].rearrange("(c p) -> p c", p=P)).then_inc(S.small_landed, 16)
            for dst, vector in ((A.dt_bias, I.dn_dt_bias_2), (A.a_log, I.dn_a_log_2), (A.norm_g, I.dn_norm_g_2)):
                sp.dma_start(dst[:], vector[l].partition_broadcast(P)).then_inc(S.small_landed, 16)
            sp.wait_ge(S.small_landed, 16 * (DCONV + SCCONV + 4))

        small = 16 * (DCONV + SCCONV + 4)
        normed = [A.qkv[:, u, :] for u in range(2 * DH)] + [A.gate_c[:, c, :] for c in range(SCT)]

        @block.tensor
        def _(pe):
            def spread(g):
                pe.wait_ge(S.inverse_ready, g + 1)
                for u in range(4):
                    n = 4 * g + u
                    if n >= 4:
                        pe.wait_ge(S.scaled, n - 3)
                    pe.matmul(M.ps[:, 4 + u, :], M.spread_sel[:, u, :], A.inverse[:, g, :], start=True,
                              stop=True).then_inc(S.spread, 1)

            for g in range(3):
                for u in range(4):
                    pe.wait_ge(S.square_ready, 4 * g + u + 1)
                    pe.matmul(M.ps[:, g, :], M.sum_sel[:, 96 - 32 * u:224 - 32 * u], M.sq[:, u % 2, :], start=(u == 0),
                              stop=(u == 3)).then_inc(S.square_used, 1)
                if g >= 1:
                    spread(g - 1)
            spread(2)

        @block.scalar
        def _(act):
            act.wait_ge(S.small_landed, small)
            link = chain(act, S.act_chain)
            link(act.activation(A.a_neg[:], A.a_log[:], ACT.Exp))
            act.wait_ge(S.one_plus, 1)
            act.activation(A.dt_e[:], A.dt_e[:], ACT.Exp, scale=-1.0).then_inc(S.exp_ready, 1)
            act.wait_ge(S.one_plus, 2)
            act.activation(A.dt_ln[:], A.dt_u[:], ACT.Ln).then_inc(S.ln_ready, 1)
            link(act.activation(A.beta[:], A.ba[:, :, 0:DH], ACT.Sigmoid))

            def square(n):
                if n >= 2:
                    act.wait_ge(S.square_used, n - 1)
                act.activation(M.sq[:, n % 2, :], normed[n], ACT.Square).then_inc(S.square_ready, 1)

            def silu(u):
                act.wait_ge(S.conv, DCONV * (u + 1))
                act.activation(A.qkv[:, u, :], A.qkv[:, u, :], ACT.Silu).then_inc(S.silu_done, 1)

            for u in range(2 * DH):
                silu(u)
                if u:
                    act.wait_ge(S.silu_done, u)
                    square(u - 1)
            act.wait_ge(S.silu_done, 2 * DH)
            square(2 * DH - 1)
            for u in range(2 * DH, 3 * DH):
                silu(u)
            for g in range(3):
                if g == 2:
                    for c in range(SCT):
                        act.wait_ge(S.gated, c + 1)
                        square(2 * DH + c)
                act.wait_ge(S.summed, g + 1)
                act.activation(A.inverse[:, g, :], A.inverse[:, g, :], ACT.Sqrt).then_inc(S.root_ready, 1)

        @block.vector
        def _(dve):
            link = chain(dve, S.dve_chain)
            dve.memset(A.raw[:, :, 0:DCONV - 1], 0.0).then_inc(S.padded, 1)
            dve.memset(A.prod[:, :, 0:SCCONV - 1], 0.0).then_inc(S.padded, 1)
            dve.wait_ge(S.small_landed, small)
            link(dve.tensor_tensor(A.g[:], A.ba[:, :, DH:], A.dt_bias[:].unsqueeze(1).to_broadcast([P, TT, DH]), ALU.add))
            dve.scalar_tensor_tensor(out=A.dt_e[:], in0=A.g[:], scalar=-1.0, in1=A.g[:], op0=ALU.mult,
                                     op1=ALU.max).then_inc(S.one_plus, 1)
            dve.wait_ge(S.exp_ready, 1)
            dve.tensor_scalar(A.dt_u[:], A.dt_e[:], 1.0, None, ALU.add).then_inc(S.one_plus, 1)
            dve.wait_ge(S.one_plus, 2)
            link(dve.scalar_tensor_tensor(out=A.dt_r[:], in0=A.dt_u[:], scalar=-1.0, in1=A.dt_e[:], op0=ALU.add,
                                          op1=ALU.subtract))
            link(dve.tensor_scalar(A.g[:], A.g[:], 0.0, None, ALU.max))
            link(dve.tensor_tensor(A.g[:], A.g[:], A.dt_r[:], ALU.subtract))
            dve.wait_ge(S.ln_ready, 1)
            link(dve.tensor_tensor(A.g[:], A.g[:], A.dt_ln[:], ALU.add))
            dve.wait_ge(S.act_chain, 1)
            link(dve.scalar_tensor_tensor(out=A.g[:], in0=A.g[:], scalar=-1.0,
                                          in1=A.a_neg[:].unsqueeze(1).to_broadcast([P, TT, DH]),
                                          op0=ALU.mult, op1=ALU.mult))
            dve.wait_ge(S.padded, 2)

            def convolve(u):
                dve.tensor_scalar(A.qkv[:, u, :], A.raw[:, u, 0:T], A.conv_w[:, 0, u:u + 1], None, ALU.mult).then_inc(S.conv, 1)
                for j in range(1, DCONV):
                    dve.wait_ge(S.conv, DCONV * u + j)
                    dve.scalar_tensor_tensor(out=A.qkv[:, u, :], in0=A.raw[:, u, j:j + T], scalar=A.conv_w[:, j, u:u + 1],
                                             in1=A.qkv[:, u, :], op0=ALU.mult, op1=ALU.add).then_inc(S.conv, 1)

            affine = [(RMS_EPS, float(DHD)), (RMS_EPS, 1.0), (P * RMS_EPS, 1.0 / P)]

            def root(g):
                dve.wait_ge(S.square_used, 4 * (g + 1))
                dve.tensor_scalar(A.inverse[:, g, :], M.ps[:, g, :], affine[g][0], affine[g][1], ALU.add,
                                  ALU.mult).then_inc(S.summed, 1)

            def inverse(g):
                dve.wait_ge(S.root_ready, g + 1)
                dve.reciprocal(A.inverse[:, g, :], A.inverse[:, g, :]).then_inc(S.inverse_ready, 1)

            def scale(g):
                for u in range(4):
                    n = 4 * g + u
                    dve.wait_ge(S.spread, n + 1)
                    if g < 2:
                        dve.tensor_tensor(normed[n], normed[n], M.ps[:, 4 + u, :], ALU.mult).then_inc(S.scaled, 1)
                    else:
                        dve.scalar_tensor_tensor(out=M.hT[:, DT - SCT + u, :], in0=normed[n], scalar=A.sc_g[:, u:u + 1],
                                                 in1=M.ps[:, 4 + u, :], op0=ALU.mult, op1=ALU.mult).then_inc(S.scaled, 1)

            for u in range(2 * DH):
                convolve(u)
            for c in range(SCT):
                x, y = A.prod[:, c, :], A.gate_c[:, c, :]
                link(dve.tensor_tensor(x[:, SCCONV - 1:], x[:, SCCONV - 1:], y, ALU.mult))
                link(dve.tensor_scalar(y, x[:, 0:T], A.sc_w[:, 0, c:c + 1], None, ALU.mult))
                for j in range(1, SCCONV):
                    link(dve.scalar_tensor_tensor(out=y, in0=x[:, j:j + T], scalar=A.sc_w[:, j, c:c + 1], in1=y,
                                                  op0=ALU.mult, op1=ALU.add))
                dve.tensor_tensor(y, y, A.gate_b[:, c, :], ALU.mult).then_inc(S.gated, 1)
            root(0)
            root(1)
            for u in range(2 * DH, 3 * DH):
                convolve(u)
            inverse(0)
            inverse(1)
            root(2)
            scale(0)
            inverse(2)
            scale(1)
            scale(2)


def mixer2_delta(nc, M, A):
    with stage(nc, "delta", "sums chain gains gain_exp beta_rows g_rows g_copied diff decay e_rows rows_exp kk qk "
               "lt_ready qk_ready k_turned v_turned nat_ready masked t1 t1_copied x_up y_up xy_ready u_ready w_ready u_copied w_copied "
               "ws v_new o o_copied s_add s_ready o_chain root_in root_ready prep_free") as (block, S):
        tri = M.tri[:, 3 * P:4 * P]
        head = lambda ap, h: ap[:, h * P:(h + 1) * P]
        heads = lambda ap: ap.rearrange("p (h c) -> p h c", h=DH)
        cols = lambda ap, i: ap[:, DH * i:DH * (i + 1)].unsqueeze(2).to_broadcast([P, DH, P])
        g_all = A.g[:].rearrange("p i h -> p (i h)")
        beta_all = A.beta[:].rearrange("p i h -> p (i h)")
        q, k, v = (A.qkv[:, DH * n:DH * (n + 1), :] for n in range(3))
        tok = lambda ap, h, i: ap[:, h, i * P:(i + 1) * P]
        X = k.rearrange("p h t -> p (h t)").rearrange("p (i n) -> p i n", i=TT)
        Y = v.rearrange("p h t -> p (h t)").rearrange("p (i n) -> p i n", i=TT)

        @block.tensor
        def _(pe):
            pe.matmul(M.ps[:, 7, 0:16], tri, g_all, start=True, stop=True)
            pe.matmul(M.ps[:, 7, 16:32], M.ones[:], g_all, start=True, stop=True).then_inc(S.sums, 1)
            for i in range(TT):
                if i >= 1:
                    pe.wait_ge(S.prep_free, i)
                for h in range(DH):
                    mm = pe.matmul(head(M.ps[:, 0], h), g_all[:, DH * i + h:DH * i + h + 1].to_broadcast([P, P]), tri,
                                   start=True, stop=True)
                mm.then_inc(S.g_rows, 1)
                for h in range(DH):
                    pe.matmul(head(M.ps[:, 1], h), beta_all[:, DH * i + h:DH * i + h + 1].to_broadcast([P, P]), M.ident[:],
                              start=True, stop=True)
                for h in range(DH):
                    mm = pe.matmul(head(M.ps[:, 2], h), tok(k, h, i), tok(k, h, i), start=True, stop=True)
                mm.then_inc(S.kk, 1)
                for h in range(DH):
                    mm = pe.matmul(head(M.ps[:, 3], h), tok(k, h, i), tok(q, h, i), start=True, stop=True)
                mm.then_inc(S.qk, 1)
                for h in range(DH):
                    mm = pe.transpose(head(M.ps[:, 4], h), tok(k, h, i), M.ident[:])
                mm.then_inc(S.k_turned, 1)
                for h in range(DH):
                    mm = pe.transpose(head(M.ps[:, 5], h), tok(v, h, i), M.ident[:])
                mm.then_inc(S.v_turned, 1)
            pe.wait_ge(S.prep_free, TT)
            for n in range(LEVELS):
                for i in range(TT):
                    pe.wait_ge(S.masked, TT * n + i + 1)
                    if n:
                        pe.wait_ge(S.xy_ready, TT * (n - 1) + i + 1)
                    for h in range(DH):
                        mm = pe.matmul(head(M.ps[:, 2 * i], h), head(A.BT[:, i], h), head(X[:, i], h) if n else M.ident[:],
                                       start=True, stop=True)
                    mm.then_inc(S.t1, 1)
                for i in range(TT):
                    if n:
                        pe.wait_ge(S.t1_copied, TT * (n - 1) + i + 1)
                        if n < LEVELS - 1:
                            for h in range(DH):
                                pe.matmul(head(M.ps[:, 2 * i + 1], h), head(Y[:, i], h), head(A.T1[:, i], h), start=True,
                                          stop=True)
                        for h in range(DH):
                            mm = pe.matmul(head(M.ps[:, 2 * i], h), head(A.T1[:, i], h), head(Y[:, i], h), start=True,
                                           stop=True)
                        mm.then_inc(S.x_up, 1)
            for i in range(TT):
                pe.wait_ge(S.xy_ready, TT * (LEVELS - 1) + i + 1)
                for h in range(DH):
                    mm = pe.matmul(head(M.ps[:, 2 * i], h), head(Y[:, i], h), head(A.vb[:, i], h), start=True, stop=True)
                mm.then_inc(S.u_ready, 1)
                for h in range(DH):
                    mm = pe.matmul(head(M.ps[:, 2 * i + 1], h), head(A.kbg[:, i], h), head(Y[:, i], h), start=True, stop=True)
                mm.then_inc(S.w_ready, 1)
            pe.wait_ge(S.u_copied, TT)
            pe.wait_ge(S.w_copied, TT)
            for i in range(TT):
                if i:
                    pe.wait_ge(S.s_ready, i)
                    for h in range(DH):
                        mm = pe.matmul(head(M.ps[:, 0], h), head(A.wT[:, i], h), head(A.state, h), start=True, stop=True)
                    mm.then_inc(S.ws, 1)
                    pe.wait_ge(S.v_new, i)
                if i >= 2:
                    pe.wait_ge(S.o_copied, i - 1)
                vn = A.v_new if i else A.u[:, 0]
                for h in range(DH):
                    if i:
                        pe.matmul(head(M.ps[:, 1 + i % 2], h), tok(q, h, i), head(A.state, h), start=True, stop=False)
                    mm = pe.matmul(head(M.ps[:, 1 + i % 2], h), head(A.qk[:, i], h), head(vn, h), start=(i == 0), stop=True)
                mm.then_inc(S.o, 1)
                if i < TT - 1:
                    for h in range(DH):
                        mm = pe.matmul(head(M.ps[:, 3], h), head(A.kdec[:, i], h), head(vn, h), start=True, stop=True)
                    mm.then_inc(S.s_add, 1)

        @block.scalar
        def _(act):
            act.wait_ge(S.gains, 1)
            act.activation(A.gain[:], A.gain[:], ACT.Exp).then_inc(S.gain_exp, 1)
            for i in range(TT):
                act.wait_ge(S.g_rows, i + 1)
                act.activation(A.rows[:], M.ps[:, 0], ACT.Exp).then_inc(S.rows_exp, 1)
                act.wait_ge(S.diff, i + 1)
                act.activation(A.D[:, i], A.D[:, i], ACT.Exp).then_inc(S.decay, 1)
                act.wait_ge(S.prep_free, i + 1)
            for n in range(1, LEVELS):
                for i in range(TT):
                    act.wait_ge(S.t1, TT * n + i + 1)
                    if n > 1:
                        act.wait_ge(S.x_up, TT * (n - 2) + i + 1)
                    act.copy(A.T1[:, i], M.ps[:, 2 * i]).then_inc(S.t1_copied, 1)
            for i in range(TT):
                act.wait_ge(S.w_ready, i + 1)
                act.copy(A.wT[:, i], M.ps[:, 2 * i + 1]).then_inc(S.w_copied, 1)
            act.wait_ge(S.root_in, 1)
            act.activation(A.root[:], A.root[:], ACT.Sqrt).then_inc(S.root_ready, 1)

        @block.vector
        def _(dve):
            link = chain(dve, S.chain)
            dve.wait_ge(S.sums, 1)
            link(dve.tensor_copy(A.G[:], M.ps[:, 7, 0:16]))
            link(dve.tensor_copy(A.gain[:, 0:16], M.ps[:, 7, 0:16]))
            link(dve.tensor_tensor(A.gain[:, 16:32], M.ps[:, 7, 16:32], A.G[:], ALU.subtract))
            dve.tensor_copy(A.gain[:, 32:48], M.ps[:, 7, 16:32]).then_inc(S.gains, 1)
            dve.wait_ge(S.gain_exp, 1)
            link(dve.tensor_tensor(A.bg[:], A.gain[:, 0:16], beta_all, ALU.mult))
            for i in range(TT):
                D, LT = A.D[:, i], A.LT[:, i]
                dve.wait_ge(S.rows_exp, i + 1)
                link(dve.tensor_tensor(heads(D), heads(M.ps[:, 0]), cols(A.G, i), ALU.subtract))
                dve.scalar_tensor_tensor(out=heads(D), in0=heads(D), scalar=0.0, in1=M.mask_neg[:].unsqueeze(1).to_broadcast(
                    [P, DH, P]), op0=ALU.min, op1=ALU.add).then_inc(S.diff, 1)
                dve.wait_ge(S.decay, i + 1)
                dve.wait_ge(S.kk, i + 1)
                link(dve.tensor_tensor(LT, M.ps[:, 2], D, ALU.mult))
                link(dve.tensor_tensor(LT, LT, M.ps[:, 1], ALU.mult))
                dve.wait_ge(S.qk, i + 1)
                dve.tensor_tensor(A.qk[:, i], M.ps[:, 3], D, ALU.mult)
                dve.tensor_tensor(q[:, :, i * P:(i + 1) * P], q[:, :, i * P:(i + 1) * P], heads(A.rows[:]), ALU.mult)
                dve.wait_ge(S.k_turned, i + 1)
                dve.tensor_tensor(heads(A.kbg[:, i]), heads(M.ps[:, 4]), cols(A.bg, i), ALU.mult)
                dve.tensor_tensor(heads(A.kdec[:, i]), heads(M.ps[:, 4]), cols(A.gain[:, 16:32], i), ALU.mult)
                dve.wait_ge(S.v_turned, i + 1)
                dve.tensor_tensor(heads(A.vb[:, i]), heads(M.ps[:, 5]), cols(beta_all, i), ALU.mult).then_inc(S.prep_free, 1)
            dve.wait_ge(S.prep_free, TT)
            for n in range(LEVELS):
                mask = M.levels[:, n, :].unsqueeze(1).to_broadcast([P, DH, P])
                eye = M.ident[:].unsqueeze(1).to_broadcast([P, DH, P])
                for i in range(TT):
                    if n:
                        dve.wait_ge(S.t1, TT * (n - 1) + i + 1)
                    dve.tensor_tensor(heads(A.BT[:, i]), heads(A.LT[:, i]), mask, ALU.mult).then_inc(S.masked, 1)
                    if n == 0:
                        dve.wait_ge(S.masked, i + 1)
                        link(dve.tensor_tensor(heads(Y[:, i]), eye, heads(A.BT[:, i]), ALU.subtract))
                for i in range(TT):
                    if n == 0:
                        dve.wait_ge(S.t1, i + 1)
                        dve.tensor_tensor(heads(X[:, i]), eye, heads(M.ps[:, 2 * i]), ALU.subtract).then_inc(S.xy_ready, 1)
                    else:
                        dve.wait_ge(S.xy_ready, TT * (n - 1) + i + 1)
                        dve.wait_ge(S.x_up, TT * (n - 1) + i + 1)
                        if n < LEVELS - 1:
                            dve.tensor_tensor(X[:, i], X[:, i], M.ps[:, 2 * i + 1], ALU.subtract)
                        dve.tensor_tensor(Y[:, i], Y[:, i], M.ps[:, 2 * i], ALU.subtract).then_inc(S.xy_ready, 1)
            for i in range(TT):
                dve.wait_ge(S.u_ready, i + 1)
                dve.tensor_copy(A.u[:, i], M.ps[:, 2 * i]).then_inc(S.u_copied, 1)

            def output(i):
                dve.wait_ge(S.o, i + 1)
                dve.tensor_copy(A.mix[:, i, :], M.ps[:, 1 + i % 2]).then_inc(S.o_copied, 1)

            state, vn = heads(A.state[:]), A.v_new[:]
            for i in range(TT):
                if i:
                    dve.wait_ge(S.ws, i)
                    dve.tensor_tensor(vn, A.u[:, i], M.ps[:, 0], ALU.subtract).then_inc(S.v_new, 1)
                if i < TT - 1:
                    dve.wait_ge(S.s_add, i + 1)
                    if i:
                        dve.wait_ge(S.o, i + 1)
                        dve.wait_ge(S.s_ready, i)
                        link(dve.tensor_tensor(state, state, cols(A.gain[:, 32:48], i), ALU.mult))
                        dve.tensor_tensor(A.state[:], A.state[:], M.ps[:, 3], ALU.add).then_inc(S.s_ready, 1)
                    else:
                        dve.tensor_copy(A.state[:], M.ps[:, 3]).then_inc(S.s_ready, 1)
                output(i)
            dve.wait_ge(S.o_copied, TT)
            o = A.mix[:].rearrange("p i (h d) -> p (i h) d", h=DH)
            sq = A.BT[:].rearrange("p i (h d) -> p (i h) d", h=DH)
            link(dve.tensor_tensor(sq, o, o, ALU.mult))
            link(dve.tensor_reduce(A.root[:], sq, AX.X, ALU.add))
            dve.tensor_scalar(A.root[:], A.root[:], 1.0 / DHD, RMS_EPS, ALU.mult, ALU.add).then_inc(S.root_in, 1)
            link(dve.tensor_tensor(o, o, A.silz[:].rearrange("p i (h d) -> p (i h) d", h=DH), ALU.mult))
            link(dve.tensor_tensor(o, o, A.norm_g[:].unsqueeze(1).to_broadcast([P, TT * DH, DHD]), ALU.mult))
            dve.wait_ge(S.root_ready, 1)
            link(dve.reciprocal(A.root[:], A.root[:]))
            link(dve.tensor_tensor(o, o, A.root[:].unsqueeze(2).to_broadcast([P, TT * DH, DHD]), ALU.mult))


def mixer2(nc, M, I, l):
    with ExitStack() as memory:
        sb = tensors(nc, memory, "b_")
        A = Memory()
        M.hT, M.wide = sb("hT", DT, T), sb("wide", 2, 2, DT, 256)
        A.qkv, A.silz, A.mix = sb("qkv", 3 * DH, T), sb("silz", TT, DW), sb("mix", TT, DW)
        A.g, A.beta, A.norm_g = sb("g", TT, DH), sb("beta", TT, DH), sb("norm_g", DHD)
        with ExitStack() as inner:
            sb = tensors(nc, inner, "b_")
            A.raw, A.prod = sb("raw", 3 * DH, T + DCONV - 1), sb("prod", SCT, T + SCCONV - 1)
            A.gate_b, A.gate_c = sb("gate_b", SCT, T), sb("gate_c", SCT, T)
            A.ba, A.inverse = sb("ba", TT, 2 * DH), sb("inverse", 3, T)
            A.conv_w, A.sc_w, A.sc_g = sb("conv_w", DCONV, 3 * DH), sb("sc_w", SCCONV, SCT), sb("sc_g", SCT)
            A.dt_bias, A.a_log, A.a_neg = sb("dt_bias", DH), sb("a_log", DH), sb("a_neg", DH)
            A.dt_e, A.dt_u, A.dt_r, A.dt_ln = (sb(f"dt_{x}", TT, DH) for x in "eurl")
            mixer2_project(nc, M, A, I, l)
            mixer2_conv(nc, M, A, I, l)
        with ExitStack() as inner:
            sb = tensors(nc, inner, "b_")
            A.D, A.LT, A.T1 = sb("D", TT, DW), sb("LT", TT, DW), sb("T1", TT, DW)
            A.qk, A.kdec, A.kbg, A.vb = sb("qk", TT, DW), sb("kdec", TT, DW), sb("kbg", TT, DW), sb("vb", TT, DW)
            A.rows, A.state, A.v_new = sb("rows", DW), sb("state", DW), sb("v_new", DW)
            A.G, A.gain, A.bg, A.root = sb("G", 16), sb("gain", 48), sb("bg", 16), sb("root", 16)
            A.BT, A.u, A.wT = A.D, A.D, A.LT
            mixer2_delta(nc, M, A)
        mix_out(nc, M, "out2", A.mix, range(DT - SCT, DT), I.w_out_2[l], None)


def finish(nc, M, I, out):
    with ExitStack() as memory, stage(nc, "finish", "h_ready turned copied stored" + RMS_SIGNALS) as (block, S):
        sb = tensors(nc, memory, "f_")
        h, rows = sb("h", DT, T), sb("rows", TT, D)

        @block.scalar
        def _(act):
            rms_act(act, M, S)

        @block.tensor
        def _(pe):
            rms_pe(pe, M, S, 7)
            pe.wait_ge(S.h_ready, DT)
            for n in range(2 * TT):
                i, half = n // 2, n % 2
                for d in range(4):
                    mm = pe.transpose(M.ps[:, n, d * P:(d + 1) * P], h[:, 4 * half + d, i * P:(i + 1) * P], M.ident[:])
                mm.then_inc(S.turned, 1)

        @block.vector
        def _(dve):
            rms_dve(dve, M, S, 7)
            for d in range(DT):
                rms_value(dve, M, d, h[:, d, :]).then_inc(S.h_ready, 1)
            for n in range(2 * TT):
                dve.wait_ge(S.turned, n + 1)
                dve.tensor_copy(rows[:, n // 2, 512 * (n % 2):512 * (n % 2 + 1)], M.ps[:, n, :]).then_inc(S.copied, 1)

        @block.sync
        def _(sp):
            rms_sp(sp, nc, M, S, I.final_norm_g_2)
            for i in range(TT):
                sp.wait_ge(S.copied, 2 * i + 2)
                sp.dma_start(out[0, i * P:(i + 1) * P, :], rows[:, i, :]).then_inc(S.stored, 16)
            sp.wait_ge(S.stored, 16 * TT)


def ada_columns(w, subs):
    return w.rearrange("(k p) n -> p k n", p=P)[:, :, 3 * D * subs[0]:3 * D * (subs[-1] + 1)]


def first_stack_layer(nc, M, I, l):
    after = 1 - l
    vectors = (M.columns[:, bass.ds(l, 1), :].rearrange("p a t -> p (a t)"),
               M.columns[:, bass.ds(after, 1), 0:3 * DT].rearrange("p a t -> p (a t)"))
    ffn(nc, M, "ffn0", I.ffn_w1[l, 0], I.ffn_w3[l, 0], I.ffn_w2[l, 0], 0, vectors=vectors,
        ada=([1, 2], ada_columns(I.ada_w[l], [1, 2]), M.pcol[:, 24:72]))
    mixer1(nc, M, I, l)
    ffn(nc, M, "ffn2", I.ffn_w1[l, 1], I.ffn_w3[l, 1], I.ffn_w2[l, 1], 2,
        ada=([0], ada_columns(I.ada_w[after], [0]), M.bnext[:]))


def program(nc, I, out):
    with ExitStack() as memory:
        sb = tensors(nc, memory, "m_")
        M = Memory()
        M.x = sb("x", DT, T)
        M.ident, M.tri, M.ones, M.mean_d = sb("ident", P), sb("tri", T + 3 * P), sb("ones", P), sb("mean_d", P)
        M.sq, M.rstd = sb("sq", 2, T), sb("rstd", T)
        M.ps = memory.enter_context(nc.psum_tensor("m_ps", [P, 8, T], F32))
        with ExitStack() as inner:
            sb = tensors(nc, inner, "m_")
            M.ccol, M.columns, M.pcol, M.bnext, M.mod = sb("ccol", DT), sb("columns", DEPTH, 120), sb("pcol", 120), sb("bnext", 3 * DT), sb("mod", 72)
            M.part = sb("part", 4, P)
            M.tape_dram = nc.dram_tensor("bias_tape", [HEADS, T + P], F32, kind="Internal").ap()
            M.bias_dram = nc.dram_tensor("bias_windows", [P, HEADS, T], F32, kind="Internal").ap()
            setup(nc, M, I)
            first_modulation(nc, M, I)
            with nc.Fori(0, DEPTH) as l:
                first_stack_layer(nc, M, I, l)
        sb = tensors(nc, memory, "m_")
        M.gain = sb("gain", DT)
        M.sum_sel, M.spread_sel = sb("sum_sel", 7 * 32), sb("spread_sel", 4, P)
        M.levels, M.mask_neg = sb("levels", LEVELS, P), sb("mask_neg", P)
        with stage(nc, "consts2", "landed") as (block, S):
            @block.sync
            def _(sp):
                for dst, value in ((M.sum_sel, sum_selectors()), (M.spread_sel, spread_selectors()),
                                   (M.levels, level_masks()), (M.mask_neg, (triangle()[:, 3 * P:4 * P] - 1) * 1e30)):
                    sp.dma_start(dst[:], nc.inline_tensor(value.astype(np.float32), name="c_" + dst.name).ap()).then_inc(S.landed, 16)
                sp.wait_ge(S.landed, 64)
        with nc.Fori(0, DEPTH) as l:
            mixer2(nc, M, I, l)
            ffn(nc, M, "ffn3", I.ffn_w_gate_2[l], I.ffn_w_up_2[l], I.ffn_w_down_2[l], None, gain=I.norm2_g_2[l])
        finish(nc, M, I, out)


_NAMES = ["x", "c", "rel_bias", "ada_w", "ada_b", "ln_g", "ln_b", "ffn_w1", "ffn_w3", "ffn_w2", "w_in", "w_out",
          "cmp_pe", "cmp_w1", "cmp_b1", "cmp_w2", "gmlp_ln_g", "gmlp_ln_b", "gmlp_ws", "gmlp_bs", "ssm_conv_w",
          "ssm_conv_b", "ssm_dt_bias", "ssm_a_log", "ssm_d", "ssm_norm_g", "norm1_g_2", "w_in_2", "dn_conv_w_2",
          "dn_a_log_2", "dn_dt_bias_2", "dn_norm_g_2", "sc_conv_w_2", "sc_norm_g_2", "w_out_2", "norm2_g_2",
          "ffn_w_gate_2", "ffn_w_up_2", "ffn_w_down_2", "final_norm_g_2"]


def kernel(**inputs):
    import concourse.bacc as bacc
    from concourse.bass_utils import run_bass_kernel_spmd

    nc = bacc.Bacc("TRN2", target_bir_lowering=False, num_devices=1)
    arrays, aps = {}, {}
    for name in _NAMES:
        a = np.ascontiguousarray(inputs[name])
        arrays[f"in_{name}"] = a
        aps[name] = nc.dram_tensor(f"in_{name}", a.shape, mybir.dt.from_np(a.dtype), kind="ExternalInput").ap()
    out = nc.dram_tensor("out", (1, T, D), F32, kind="ExternalOutput").ap()
    program(nc, namedtuple("Inputs", _NAMES)(**aps), out)
    return run_bass_kernel_spmd(nc, [arrays], core_ids=[0]).results[0]["out"]
```

```python
import math
from collections import namedtuple
from contextlib import ExitStack, contextmanager

import numpy as np
import concourse.bass as bass
from concourse import mybir

F32 = mybir.dt.float32
F32R = mybir.dt.float32r
ALU = mybir.AluOpType
ACT = mybir.ActivationFunctionType
AX = mybir.AxisListType

P = 128
T = 512
TT = T // P
D = 1024
DT = D // P
F = 2816
FT = F // P
DEPTH = 2
ALPHA = (2 * DEPTH) ** 0.25
LN_EPS = 1e-5
RMS_EPS = 1e-6

HEADS, GROUPS, HD = 8, 2, 64
HPG = HEADS // GROUPS
KV = GROUPS * HD
N_BRANCH = 3
CMP_LEN, CMP_STRIDE, CMP_HID = 32, 16, 256
N_CMP = (T - CMP_LEN) // CMP_STRIDE + 1
BUCKETS, MAX_DIST = 32, 128
Q_OFF = 0
KC_OFF = HEADS * HD
VW_OFF = KC_OFF + 5 * KV
GATE_OFF = KC_OFF + 6 * KV
GMLP_OFF = GATE_OFF + HEADS * N_BRANCH
D_GMLP, GG, GGD = 256, 4, 64
Z_OFF = GMLP_OFF + 2 * D_GMLP
D_SSM, SH, SG, NSTATE, SCONV = 256, 4, 2, 128, 4
XBC_OFF = Z_OFF + D_SSM
D_XBC = D_SSM + 2 * SG * NSTATE
XT = D_XBC // P
DT_OFF = XBC_OFF + D_XBC
D_IN = DT_OFF + SH
MASKED = -1.0e30
FLOOR = -1.0e29

DH, DHD, DCONV = 4, 128, 4
DW = DH * DHD
SCW, SCCONV = 512, 3
SCT = SCW // P
W2_COLS = 4 * DW + 2 * DH + 3 * SCW
LEVELS = 7


def rel_bucket_onehot():
    dist = T - 1 - np.arange(T + P)
    n = np.maximum(dist, 0)
    exact = BUCKETS // 2
    nf = np.maximum(n, 1).astype(np.float32)
    large = exact + (np.log(nf / exact) / math.log(MAX_DIST / exact) * (BUCKETS - exact)).astype(np.int32)
    bucket = np.where(n < exact, n, np.minimum(large, BUCKETS - 1))
    out = np.zeros((BUCKETS + 1, T + P), np.float32)
    seen = dist >= 0
    out[bucket[seen], np.nonzero(seen)[0]] = 1
    out[BUCKETS, ~seen] = 1
    return out


def triangle():
    return (np.arange(T + P * 3)[None, :] - P * 3 >= np.arange(P)[:, None]).astype(np.float32)


def level_masks():
    i = np.arange(P)
    out = np.zeros((P, LEVELS, P), np.float32)
    for n in range(LEVELS):
        m = 1 << n
        out[:, n, :] = ((i[:, None] // (2 * m) == i[None, :] // (2 * m))
                        & ((i // m) % 2 == 0)[:, None] & ((i // m) % 2 == 1)[None, :])
    return out


class Memory:
    pass


class Ahead:

    def __init__(self, nc, tag, load):
        self.landed = [nc.alloc_semaphore(f"{tag}_ahead{s}") for s in range(2)]
        self.load = lambda sp: load(sp, self.landed)


@contextmanager
def stage(nc, name, signals, ahead=None):
    names = signals.split()
    sems = [nc.alloc_semaphore(f"{name}_{s}") for s in names]
    with nc.Block(name) as block:
        yield block, namedtuple("Signals", names)(*sems)
    nc.clear_and_free_semaphores(sems + (ahead.landed if ahead else []))
    nc.all_engine_barrier()


def tensors(nc, memory, prefix):
    return lambda name, *shape: memory.enter_context(nc.sbuf_tensor(prefix + name, [P, *shape], F32))


def rounded(nc, memory, prefix):
    return lambda name, *shape: memory.enter_context(nc.sbuf_tensor(prefix + name, [P, *shape], F32R))


def product(pe, out, stationary, moving, first, last):
    (sh, sl), (mh, ml) = stationary, moving
    pe.matmul(out, sh, mh, start=first, stop=False, skip_group_check=True)
    pe.matmul(out, sh, ml, start=False, stop=False, skip_group_check=True)
    return pe.matmul(out, sl, mh, start=False, stop=last, skip_group_check=True)


def low_part(dve, low, value, high):
    return dve.tensor_tensor(low, value, high.bitcast(F32), ALU.subtract)


def chain(engine, sem):
    done = [0]

    def link(instruction):
        done[0] += 1
        instruction.then_inc(sem, 1)
        engine.wait_ge(sem, done[0])
        return instruction
    return link


def setup(nc, M, I):
    chunk = 512
    chunks = 3 * D // chunk
    with stage(nc, "setup", "consts onehot x_landed rel_landed mask_row turned copied tape_ready tape_copied "
               "tape_stored windows_landed flipped bias_copied bias_stored c_landed c_ready vectors_landed vectors_turned "
               "ada0 ada1 ada2 ada3 ada4 ada5 ada_mac ada_partial ada_column mod_chain mod_ready") as (block, S), ExitStack() as memory:
        sb = tensors(nc, memory, "s_")
        x_rows, bias, windows = sb("x_rows", TT, D), sb("bias", HEADS, T), sb("windows", HEADS, T)
        onehot, tape, relx, flip, vectors = sb("onehot", T + P), sb("tape", T + P), sb("relx", HEADS), sb("flip", P), sb("vectors", DEPTH, P)
        ada, part = sb("ada_chunks", chunks, DT, chunk), sb("ada_part", 2, chunk)
        ada_landed = [S.ada0, S.ada1, S.ada2, S.ada3, S.ada4, S.ada5]
        const = lambda value, name: nc.inline_tensor(np.ascontiguousarray(value, np.float32), name=name).ap()

        @block.sync
        def _(sp):
            sp.dma_start(M.ident[:], const(np.eye(P), "c_ident")).then_inc(S.consts, 16)
            with nc.allow_non_contiguous_dma(reason="one vector as columns"):
                sp.dma_start(M.ccol[:], I.c[0].rearrange("(k p) -> p k", p=P)).then_inc(S.c_landed, 16)
            for i in range(TT):
                sp.dma_start(x_rows[:, i, :], I.x[0, i * P:(i + 1) * P, :]).then_inc(S.x_landed, 16)
            sp.dma_start(onehot[0:BUCKETS + 1, :], const(rel_bucket_onehot(), "c_bucket")).then_inc(S.onehot, 16)
            sp.dma_start(relx[0:BUCKETS, :], I.rel_bias).then_inc(S.rel_landed, 16)
            for l in range(DEPTH):
                sp.dma_start(vectors[0:72, l, :], I.ada_b[l].rearrange("(r n) -> r n", n=P)).then_inc(S.vectors_landed, 16)
                sp.dma_start(vectors[72:96, l, :], I.ln_g[l].rearrange("s (d n) -> (s d) n", n=P)).then_inc(S.vectors_landed, 16)
                sp.dma_start(vectors[96:120, l, :], I.ln_b[l].rearrange("s (d n) -> (s d) n", n=P)).then_inc(S.vectors_landed, 16)
            sp.dma_start(flip[:], const(np.eye(P)[::-1], "c_flip")).then_inc(S.consts, 16)
            sp.dma_start(M.tri[:], const(triangle(), "c_tri")).then_inc(S.consts, 16)
            sp.dma_start(M.ones[:], const(np.ones((P, P)), "c_ones")).then_inc(S.consts, 16)
            sp.dma_start(M.mean_d[:], const(np.full((P, P), 1 / D), "c_mean")).then_inc(S.consts, 16)
            sp.wait_ge(S.tape_copied, 2)
            sp.dma_start(M.tape_dram, tape[0:HEADS, :]).then_inc(S.tape_stored, 16)
            sp.wait_ge(S.tape_stored, 16)
            for h in range(HEADS):
                rows = bass.AP(tensor=M.tape_dram.tensor, offset=h * (T + P), ap=[[1, P], [1, T]])
                sp.dma_start(windows[:, h, :], rows).then_inc(S.windows_landed, 16)
            sp.wait_ge(S.bias_copied, HEADS)
            sp.dma_start(M.bias_dram, bias[:]).then_inc(S.bias_stored, 16)
            sp.wait_ge(S.bias_stored, 16)

        @block.gpsimd
        def _(pool):
            pool.wait_ge(S.vectors_landed, 16 * 3 * DEPTH)
            for n in range(chunks):
                if n >= 2:
                    pool.wait_ge(ada_landed[n - 2], 16)
                pool.dma_start(ada[:, n], I.ada_w[0].rearrange("(k p) n -> p k n", p=P)[:, :, chunk * n:chunk * (n + 1)]
                               ).then_inc(ada_landed[n], 16)

        @block.tensor
        def _(pe):
            pe.wait_ge(S.consts, 80)
            pe.wait_ge(S.x_landed, 16 * TT)
            for d in range(DT):
                for i in range(TT):
                    mm = pe.transpose(M.ps[:, d, i * P:(i + 1) * P], x_rows[:, i, d * P:(d + 1) * P], M.ident[:])
                mm.then_inc(S.turned, 1)
            pe.wait_ge(S.onehot, 16)
            pe.wait_ge(S.rel_landed, 16)
            pe.wait_ge(S.mask_row, 1)
            pe.wait_ge(S.copied, 4)
            pe.matmul(M.ps[0:HEADS, 0, :], relx[0:BUCKETS + 1, :], onehot[0:BUCKETS + 1, 0:T],
                      start=True, stop=True).then_inc(S.tape_ready, 1)
            pe.matmul(M.ps[0:HEADS, 1, 0:P], relx[0:BUCKETS + 1, :], onehot[0:BUCKETS + 1, T:T + P],
                      start=True, stop=True).then_inc(S.tape_ready, 1)
            pe.wait_ge(S.vectors_landed, 16 * 3 * DEPTH)
            for l in range(DEPTH):
                pe.transpose(M.ps[:, 2 + l, 0:120], vectors[0:120, l, :], M.ident[0:120, 0:120]).then_inc(S.vectors_turned, 1)
            pe.wait_ge(S.windows_landed, 16 * HEADS)
            pe.wait_ge(S.copied, DT + DEPTH)
            for h in range(HEADS):
                if h == HEADS - 1:
                    pe.wait_ge(S.bias_copied, 1)
                pe.matmul(M.ps[:, h % 7, :], flip[:], windows[:, h, :], start=True, stop=True).then_inc(S.flipped, 1)
            for n in range(chunks):
                pe.wait_ge(S.ada_partial, n + 1)
                for q in range(chunk // P):
                    m = chunk // P * n + q
                    mm = pe.matmul(M.ps[:, 7, m:m + 1], part[:, n % 2, q * P:(q + 1) * P], M.ones[:, 0:1], start=True, stop=True)
                mm.then_inc(S.ada_column, ADA_CHUNKS // chunks)

        @block.scalar
        def _(act):
            act.wait_ge(S.c_landed, 16)
            act.activation(M.ccol[:], M.ccol[:], ACT.Silu).then_inc(S.c_ready, 1)

        @block.vector
        def _(dve):
            dve.memset(relx[BUCKETS:BUCKETS + 1, :], MASKED).then_inc(S.mask_row, 1)
            for d in range(DT):
                dve.wait_ge(S.turned, d + 1)
                dve.tensor_copy(M.x[:, d, :], M.ps[:, d, :]).then_inc(S.copied, 1)
            dve.wait_ge(S.tape_ready, 2)
            dve.tensor_copy(tape[0:HEADS, 0:T], M.ps[0:HEADS, 0, :]).then_inc(S.tape_copied, 1)
            dve.tensor_copy(tape[0:HEADS, T:T + P], M.ps[0:HEADS, 1, 0:P]).then_inc(S.tape_copied, 1)
            for l in range(DEPTH):
                dve.wait_ge(S.vectors_turned, l + 1)
                dve.tensor_copy(M.columns[:, l, :], M.ps[:, 2 + l, 0:120]).then_inc(S.copied, 1)
            dve.wait_ge(S.c_ready, 1)

            def ada_chunk(n):
                dve.wait_ge(ada_landed[n], 16)
                if n >= 2:
                    dve.wait_ge(S.ada_column, ADA_CHUNKS // chunks * (n - 1))
                dve.tensor_scalar(part[:, n % 2, :], ada[:, n, 0, :], M.ccol[:, 0:1], None, ALU.mult).then_inc(S.ada_mac, 1)
                for k in range(1, DT):
                    dve.wait_ge(S.ada_mac, n * (DT - 1) + k)
                    dve.scalar_tensor_tensor(out=part[:, n % 2, :], in0=ada[:, n, k, :], scalar=M.ccol[:, k:k + 1],
                                             in1=part[:, n % 2, :], op0=ALU.mult, op1=ALU.add
                                             ).then_inc(S.ada_mac if k < DT - 1 else S.ada_partial, 1)

            ada_chunk(0)
            ada_chunk(1)
            for h in range(HEADS):
                dve.wait_ge(S.flipped, h + 1)
                dve.tensor_copy(bias[:, h, :], M.ps[:, h % 7, :]).then_inc(S.bias_copied, 1)
            for n in range(2, chunks):
                ada_chunk(n)
            ada_finish(dve, M, S, [0], M.columns[:, 0, 0:3 * DT])


ADA_SIGNALS = " ada0_landed ada1_landed ada_mac ada_partial ada_column mod_chain mod_ready"


ADA_CHUNKS = 3 * DT


def ada_load(queue, M, S, source, m, s):
    width = M.ada.shape[-1]
    queue.dma_start(M.ada[:, s], source[:, :, bass.ds(m * width, width)]).then_inc([S.ada0_landed, S.ada1_landed][s], 16)


def ada_sum(dve, M, S, m, s, uses):
    part = M.part[:, s, 0:M.ada.shape[-1]]
    dve.wait_ge([S.ada0_landed, S.ada1_landed][s], 16 * uses)
    dve.tensor_scalar(part, M.ada[:, s, 0, :], M.ccol[:, 0:1], None, ALU.mult).then_inc(S.ada_mac, 1)
    for k in range(1, DT):
        dve.wait_ge(S.ada_mac, m * (DT - 1) + k)
        dve.scalar_tensor_tensor(out=part, in0=M.ada[:, s, k, :], scalar=M.ccol[:, k:k + 1], in1=part,
                                 op0=ALU.mult, op1=ALU.add).then_inc(S.ada_mac if k < DT - 1 else S.ada_partial, 1)


def ada_columns_pe(pe, M, S, m, s):
    pe.wait_ge(S.ada_partial, m + 1)
    tiles = M.ada.shape[-1] // P
    for e in range(tiles):
        mm = pe.matmul(M.ps[:, 7, bass.ds(m * tiles + e, 1)], M.part[:, s, e * P:(e + 1) * P], M.ones[:, 0:1],
                       start=True, stop=True)
    mm.then_inc(S.ada_column, 1)


def ada_finish(dve, M, S, subs, biases):
    link = chain(dve, S.mod_chain)
    n = 3 * DT * len(subs)
    dve.wait_ge(S.ada_column, ADA_CHUNKS)
    mod = M.mod[:, 3 * DT * subs[0]:3 * DT * subs[0] + n]
    link(dve.tensor_tensor(mod, M.ps[:, 7, 0:n], biases, ALU.add))
    dve.sem_inc(S.mod_ready, 1)
    for sub in subs:
        weight = 1.0 if sub == 1 else 0.5
        scale, gate = (M.mod[:, sub * 24 + w * DT:sub * 24 + (w + 1) * DT] for w in (1, 2))
        link(dve.tensor_scalar(scale, scale, 1.0, None, ALU.add))
        link(dve.tensor_scalar(gate, gate, 1.0, weight / ALPHA, ALU.add, ALU.mult))


NORM_SIGNALS = " z_ready mean_ready centered square_ready square_used var_ready root_ready rstd_ready xhat_ready"


def post_norm_pe(pe, M, S):
    for d in range(DT):
        pe.wait_ge(S.z_ready, d + 1)
        mm = pe.matmul(M.ps[:, 0, :], M.mean_d[:], M.x[:, d, :], start=(d == 0), stop=(d == DT - 1))
    mm.then_inc(S.mean_ready, 1)
    for d in range(DT):
        pe.wait_ge(S.square_ready, d + 1)
        pe.matmul(M.ps[:, 1, :], M.mean_d[:], M.sq[:, d % 2, :], start=(d == 0),
                  stop=(d == DT - 1)).then_inc(S.square_used, 1)


def post_norm_act(act, M, S, sub):
    for d in range(DT):
        act.wait_ge(S.centered, d + 1)
        if d >= 2:
            act.wait_ge(S.square_used, d - 1)
        act.activation(M.sq[:, d % 2, :], M.x[:, d, :], ACT.Square).then_inc(S.square_ready, 1)
    act.wait_ge(S.var_ready, 1)
    act.activation(M.rstd[:], M.rstd[:], ACT.Sqrt).then_inc(S.root_ready, 1)
    for d in range(DT):
        act.wait_ge(S.xhat_ready, d + 1)
        act.activation(M.x[:, d, :], M.x[:, d, :], ACT.Identity, scale=M.pcol[:, 72 + sub * DT + d:73 + sub * DT + d],
                       bias=M.pcol[:, 96 + sub * DT + d:97 + sub * DT + d])


def post_norm_dve(dve, M, S, sub, before=None):
    gate = M.mod[:, sub * 24 + 2 * DT:sub * 24 + 3 * DT]
    for d in range(DT):
        if before is not None:
            before(d)
        dve.wait_ge(S.y_ready, d + 1)
        dve.scalar_tensor_tensor(out=M.x[:, d, :], in0=M.ps[:, d, :], scalar=gate[:, d:d + 1],
                                 in1=M.x[:, d, :], op0=ALU.mult, op1=ALU.add).then_inc(S.z_ready, 1)
    dve.wait_ge(S.z_ready, DT)
    dve.wait_ge(S.mean_ready, 1)
    for d in range(DT):
        dve.tensor_tensor(M.x[:, d, :], M.x[:, d, :], M.ps[:, 0, :], ALU.subtract).then_inc(S.centered, 1)
    dve.wait_ge(S.square_used, DT)
    dve.tensor_scalar(M.rstd[:], M.ps[:, 1, :], LN_EPS / ALPHA ** 2, None, ALU.add).then_inc(S.var_ready, 1)
    dve.wait_ge(S.root_ready, 1)
    dve.reciprocal(M.rstd[:], M.rstd[:]).then_inc(S.rstd_ready, 1)
    dve.wait_ge(S.rstd_ready, 1)
    for d in range(DT):
        dve.tensor_tensor(M.x[:, d, :], M.x[:, d, :], M.rstd[:], ALU.mult).then_inc(S.xhat_ready, 1)


H_SIGNALS = " h_value h_high h_ready h_odd_ready"


def round_h_dve(dve, M, S, value, between, buffers=None):
    if buffers is not None:
        for d in range(DT):
            value(d, buffers[:, d, :]).then_inc(S.h_value, 1)
            if d == 1:
                between()
            if d % 2:
                dve.wait_ge(S.h_high, d)
                low_part(dve, M.h_low[:, d - 1, :], buffers[:, d - 1, :], M.h_high[:, d - 1, :]).then_inc(S.h_ready, 1)
        return

    def low(d):
        dve.wait_ge(S.h_high, d + 1)
        low_part(dve, M.h_low[:, d, :], M.sq[:, d % 2, :], M.h_high[:, d, :]).then_inc(S.h_ready, 1)

    for d in range(DT):
        if d >= 2:
            dve.wait_ge(S.h_ready, d - 1)
        value(d, M.sq[:, d % 2, :]).then_inc(S.h_value, 1)
        if d == 1:
            between()
        if d:
            low(d - 1)
    low(DT - 1)


def round_h_act(act, M, S, buffers=None):
    for d in range(DT):
        act.wait_ge(S.h_value, d + 1)
        act.copy(M.h_high[:, d, :], M.sq[:, d % 2, :] if buffers is None else buffers[:, d, :]).then_inc(S.h_high, 1)


def round_h_pool(pool, M, S, buffers):
    for d in range(1, DT, 2):
        pool.wait_ge(S.h_high, d + 1)
        low_part(pool, M.h_low[:, d, :], buffers[:, d, :], M.h_high[:, d, :]).then_inc(S.h_odd_ready, 1)


def modulate_dve(dve, M, S, sub, between, buffers=None):
    round_h_dve(dve, M, S, lambda d, out: dve.tensor_scalar(
        out, M.x[:, d, :], M.mod[:, sub * 24 + DT + d:sub * 24 + DT + d + 1],
        M.mod[:, sub * 24 + d:sub * 24 + d + 1], ALU.mult, ALU.add), between, buffers)


ROOT_SIGNALS = " x_summed square_in square_out mean_copied rms_root"
GAIN_SIGNALS = " gain_landed"


def rms_sp(sp, nc, M, S, gain):
    with nc.allow_non_contiguous_dma(reason="one vector as columns"):
        sp.dma_start(M.gain[:], gain.rearrange("(d p) -> p d", p=P)).then_inc(S.gain_landed, 16)


def rms_act(act, M, S, summed):
    for d in range(DT):
        if summed:
            act.wait_ge(S.x_summed, d + 1)
        if d >= 2:
            act.wait_ge(S.square_out, d - 1)
        act.activation(M.sq[:, d % 2, :], M.x[:, d, :], ACT.Square).then_inc(S.square_in, 1)
    act.wait_ge(S.mean_copied, 1)
    act.activation(M.rstd[:], M.rstd[:], ACT.Sqrt).then_inc(S.rms_root, 1)


def rms_pe(pe, M, S):
    for d in range(DT):
        pe.wait_ge(S.square_in, d + 1)
        pe.matmul(M.ps[:, 0, :], M.mean_d[:], M.sq[:, d % 2, :], start=(d == 0), stop=(d == DT - 1)).then_inc(S.square_out, 1)


def rms_dve(dve, M, S):
    dve.wait_ge(S.square_out, DT)
    dve.tensor_scalar(M.rstd[:], M.ps[:, 0, :], RMS_EPS, None, ALU.add).then_inc(S.mean_copied, 1)
    dve.wait_ge(S.rms_root, 1)
    dve.reciprocal(M.rstd[:], M.rstd[:])


def add_y_dve(dve, M, S, before=None):
    for d in range(DT):
        if before is not None:
            before(d)
        dve.wait_ge(S.y_ready, d + 1)
        dve.tensor_tensor(M.x[:, d, :], M.x[:, d, :], M.ps[:, d, :], ALU.add).then_inc(S.x_summed, 1)
    rms_dve(dve, M, S)


def first_root(nc, M):
    with stage(nc, "root", ROOT_SIGNALS) as (block, S):
        @block.scalar
        def _(act):
            rms_act(act, M, S, False)

        @block.tensor
        def _(pe):
            rms_pe(pe, M, S)

        @block.vector
        def _(dve):
            rms_dve(dve, M, S)


def rms_value(dve, M, d, out):
    return dve.scalar_tensor_tensor(out=out, in0=M.x[:, d, :], scalar=M.gain[:, d:d + 1], in1=M.rstd[:],
                                    op0=ALU.mult, op1=ALU.mult)


def ffn_load(sp, M, landed, w_gate, w_up, s, n):
    for which, w in enumerate((w_gate, w_up)):
        raw = M.raw[:, s, which * D:(which + 1) * D].rearrange("p (k n) -> p k n", k=DT)
        sp.dma_start(raw, w.rearrange("(k p) f -> p k f", p=P)[:, :, bass.ds(n * P, P)]).then_inc(landed[s], 16)


def ffn_ahead(nc, M, tag, w_gate, w_up):
    return Ahead(nc, tag, lambda sp, landed: [ffn_load(sp, M, landed, w_gate, w_up, s, s) for s in range(2)])


def ffn(nc, M, tag, w_gate, w_up, w_down, sub, ada=None, vectors=None, gain=None, mine=None, ahead=None):
    subs, ada_source, ada_bias = ada or ([], None, None)
    down_v = w_down.rearrange("(f p) n -> p f n", p=P)
    signals = ("wide0_landed wide1_landed rows0_landed rows1_landed wide_high wide_split projected silu_done hidden_done "
               "rows_high rows_split down_done y_ready vectors_copied")
    last = NORM_SIGNALS if sub is not None else ROOT_SIGNALS + GAIN_SIGNALS
    with ExitStack() as memory, stage(nc, tag, signals + last + H_SIGNALS + ADA_SIGNALS, mine) as (block, S):
        sb, sr = tensors(nc, memory, tag + "_"), rounded(nc, memory, tag + "_")
        hid, sil, rows = sb("hid", FT, T), sb("sil", 2, T), sb("rows", 2, D)
        M.h_high, M.h_low = sr("h_high", DT, T), sr("h_low", DT, T)
        h_buffers = hid[:, 0:DT, :]
        w_high, w_low = sr("w_high", 2, 2, DT, P), sr("w_low", 2, 2, DT, P)
        rows_high, rows_low, hid_high, hid_low = sr("rows_high", 2, D), sr("rows_low", 2, D), sr("hid_high", 2, T), sr("hid_low", 2, T)
        if subs:
            M.ada = sb("ada_chunks", 2, DT, len(subs) * P)
        wide_landed = mine.landed if mine else [S.wide0_landed, S.wide1_landed]
        rows_landed = [S.rows0_landed, S.rows1_landed]
        row = lambda ap, f: ap[:, bass.ds(f, 1), :].rearrange("p a t -> p (a t)")
        flat = lambda ap: ap.rearrange("p w k n -> p (w k n)")

        @block.sync
        def _(sp):
            def load_rows(s, n):
                sp.dma_start(rows[:, s], row(down_v, n)).then_inc(rows_landed[s], 16)

            if mine is None:
                ffn_load(sp, M, wide_landed, w_gate, w_up, 0, 0)
                ffn_load(sp, M, wide_landed, w_gate, w_up, 1, 1)
            if gain is not None:
                rms_sp(sp, nc, M, S, gain)
            load_rows(0, 0)
            load_rows(1, 1)
            with sp.Fori(1, FT // 2) as i:
                for s in range(2):
                    sp.wait_ge(S.wide_split, 2 * i + s - 1)
                    ffn_load(sp, M, wide_landed, w_gate, w_up, s, 2 * i + s)
            if ahead is not None:
                sp.wait_ge(S.wide_split, FT)
                ahead.load(sp)
            with sp.Fori(1, FT // 2) as i:
                for s in range(2):
                    sp.wait_ge(S.rows_split, 2 * i + s - 1)
                    load_rows(s, 2 * i + s)

        @block.gpsimd
        def _(pool):
            if subs:
                for m in range(2):
                    ada_load(pool, M, S, ada_source, m, m)
            round_h_pool(pool, M, S, h_buffers)
            if subs:
                with pool.Fori(1, ADA_CHUNKS // 2) as i:
                    for s in range(2):
                        pool.wait_ge(S.ada_partial, 2 * i + s - 1)
                        ada_load(pool, M, S, ada_source, 2 * i + s, s)

        @block.tensor
        def _(pe):
            def project(s, f, first):
                pe.wait_ge(S.wide_split, f + 1)
                if not first:
                    pe.wait_ge(S.hidden_done, f - 1)
                for which in range(2):
                    for k in range(DT):
                        if first:
                            pe.wait_ge([S.h_ready, S.h_odd_ready][k % 2], k // 2 + 1)
                        mm = product(pe, M.ps[:, 2 * s + which, :], (w_high[:, s, which, k], w_low[:, s, which, k]),
                                     (M.h_high[:, k, :], M.h_low[:, k, :]), k == 0, k == DT - 1)
                mm.then_inc(S.projected, 1)

            def columns(s, m):
                if subs:
                    ada_columns_pe(pe, M, S, m, s)

            project(0, 0, True)
            columns(0, 0)
            columns(1, 1)
            project(1, 1, True)
            columns(0, 2)
            with pe.Fori(1, FT // 2) as i:
                project(0, 2 * i, False)
                columns(1, 2 * i + 1)
                project(1, 2 * i + 1, False)
                columns(0, 2 * i + 2)

            def down(s, d, first, last):
                cols = slice(d * P, (d + 1) * P)
                return product(pe, M.ps[:, d, :], (rows_high[:, s, cols], rows_low[:, s, cols]),
                               (hid_high[:, s, :], hid_low[:, s, :]), first, last)

            pe.wait_ge(S.rows_split, 1)
            for d in (4, 5, 6, 0, 1, 2, 3):
                if d == 0:
                    pe.wait_ge(S.hidden_done, FT)
                down(0, d, True, False)
            columns(1, ADA_CHUNKS - 1)
            pe.wait_ge(S.rows_split, 2)
            for d in range(DT - 1):
                down(1, d, False, False)
            if subs:
                pe.wait_ge(S.mod_ready, 1)
            down(0, DT - 1, True, False).then_inc(S.down_done, 1)
            down(1, DT - 1, False, False).then_inc(S.down_done, 1)
            with pe.Fori(1, FT // 2 - 1) as i:
                for s in range(2):
                    pe.wait_ge(S.rows_split, 2 * i + s + 1)
                    for d in range(DT):
                        mm = down(s, d, False, False)
                    mm.then_inc(S.down_done, 1)
            pe.wait_ge(S.rows_split, FT)
            for d in range(DT):
                down(0, d, False, False)
                down(1, d, False, True).then_inc(S.y_ready, 1)
            if sub is not None:
                post_norm_pe(pe, M, S)
            else:
                rms_pe(pe, M, S)

        @block.scalar
        def _(act):
            def split(s, n, landings, first):
                act.wait_ge(wide_landed[s], landings)
                if not first:
                    act.wait_ge(S.projected, n - 1)
                act.copy(flat(w_high[:, s]), M.raw[:, s]).then_inc(S.wide_high, 1)

            def silu(s, f, first):
                act.wait_ge(S.projected, f + 1)
                if not first:
                    act.wait_ge(S.hidden_done, f - 1)
                act.activation(sil[:, s, :], M.ps[:, 2 * s, :], ACT.Silu).then_inc(S.silu_done, 1)

            def split_rows(s, f, landings, first):
                act.wait_ge(rows_landed[s], landings)
                if not first:
                    act.wait_ge(S.down_done, f - 1)
                act.copy(rows_high[:, s], rows[:, s])
                act.copy(hid_high[:, s], row(hid, f)).then_inc(S.rows_high, 1)

            split(0, 0, 32, True)
            round_h_act(act, M, S, h_buffers)
            split(1, 1, 32, True)
            silu(0, 0, True)
            split(0, 2, 64, False)
            silu(1, 1, True)
            split(1, 3, 64, False)
            with act.Fori(2, FT // 2) as i:
                for s in range(2):
                    silu(s, 2 * i + s - 2, False)
                    split(s, 2 * i + s, 32 * i + 32, False)
            silu(0, FT - 2, False)
            for s in range(2):
                split_rows(s, s, 16, True)
            silu(1, FT - 1, False)
            act.wait_ge(S.hidden_done, FT)
            with act.Fori(1, FT // 2) as i:
                for s in range(2):
                    split_rows(s, 2 * i + s, 16 * i + 16, False)
            if sub is not None:
                post_norm_act(act, M, S, sub)
            else:
                rms_act(act, M, S, True)

        @block.vector
        def _(dve):
            def split(s, n):
                dve.wait_ge(S.wide_high, n + 1)
                low_part(dve, flat(w_low[:, s]), M.raw[:, s], flat(w_high[:, s])).then_inc(S.wide_split, 1)

            def hidden(s, f):
                dve.wait_ge(S.silu_done, f + 1)
                dve.tensor_tensor(row(hid, f), sil[:, s, :], M.ps[:, 2 * s + 1, :], ALU.mult).then_inc(S.hidden_done, 1)

            def split_rows(s, f):
                dve.wait_ge(S.rows_high, f + 1)
                low_part(dve, rows_low[:, s], rows[:, s], rows_high[:, s])
                low_part(dve, hid_low[:, s], row(hid, f), hid_high[:, s]).then_inc(S.rows_split, 1)

            def ada_step(s, m, uses, first=False):
                if subs:
                    if not first:
                        dve.wait_ge(S.ada_column, m - 1)
                    ada_sum(dve, M, S, m, s, uses)

            if vectors is not None:
                dve.tensor_copy(M.pcol[:], vectors[0]).then_inc(S.vectors_copied, 1)
                dve.tensor_copy(M.bnext[:], vectors[1]).then_inc(S.vectors_copied, 1)
            if sub is not None:
                modulate_dve(dve, M, S, sub, lambda: split(0, 0), h_buffers)
            else:
                dve.wait_ge(S.gain_landed, 16)
                round_h_dve(dve, M, S, lambda d, out: rms_value(dve, M, d, out),
                            lambda: split(0, 0), h_buffers)
            split(1, 1)
            ada_step(0, 0, 1, True)
            ada_step(1, 1, 1, True)
            hidden(0, 0)
            split(0, 2)
            ada_step(0, 2, 2)
            ada_step(1, 3, 2)
            hidden(1, 1)
            split(1, 3)
            ada_step(0, 4, 3)
            with dve.Fori(2, FT // 2) as i:
                hidden(0, 2 * i - 2)
                split(0, 2 * i)
                ada_step(1, 2 * i + 1, i + 1)
                hidden(1, 2 * i - 1)
                split(1, 2 * i + 1)
                ada_step(0, 2 * i + 2, i + 2)
            hidden(0, FT - 2)
            split_rows(0, 0)
            split_rows(1, 1)
            hidden(1, FT - 1)
            ada_step(1, ADA_CHUNKS - 1, ADA_CHUNKS // 2)
            if subs:
                if vectors is not None:
                    dve.wait_ge(S.vectors_copied, 2)
                ada_finish(dve, M, S, subs, ada_bias)
            with dve.Fori(1, FT // 2) as i:
                for s in range(2):
                    split_rows(s, 2 * i + s)
            if sub is not None:
                post_norm_dve(dve, M, S, sub)
            else:
                add_y_dve(dve, M, S)


SPLIT_SIGNALS = " w0_landed w1_landed w_high w_split"


def load_chunk(sp, M, landed, pieces, c):
    slot = M.raw[:, c % 2].rearrange("p (k n) -> p k n", k=DT)
    for cols, src in pieces[c]:
        sp.dma_start(slot[:, :, cols], src).then_inc(landed[c % 2], 16)


def chunks_ahead(nc, M, tag, pieces):
    return Ahead(nc, tag, lambda sp, landed: [load_chunk(sp, M, landed, pieces, c) for c in range(2)])


class Chunks:
    WIDTH = 256

    def __init__(self, nc, memory, tag, M, pieces, landed):
        self.M, self.pieces, self.landed = M, pieces, landed
        self.raw = M.raw[:].rearrange("p s (k n) -> p s k n", k=DT)
        self.high, self.low = (rounded(nc, memory, tag + "_")(name, 2, DT, self.WIDTH) for name in ("w_high", "w_low"))
        self.width = [max(cols.stop for cols, _ in p) for p in pieces]
        self.landings = [16 * sum(len(pieces[j]) for j in range(c % 2, c + 1, 2)) for c in range(len(pieces))]

    def load_all(self, sp, S, first, ahead):
        for c in range(first, len(self.pieces)):
            if c >= 2:
                sp.wait_ge(S.w_split, c - 1)
            load_chunk(sp, self.M, self.landed, self.pieces, c)
        if ahead is not None:
            sp.wait_ge(S.w_split, len(self.pieces))
            ahead.load(sp)

    def round_high(self, act, S, c):
        act.wait_ge(self.landed[c % 2], self.landings[c])
        cols = slice(0, self.width[c])
        act.copy(self.high[:, c % 2, :, cols], self.raw[:, c % 2, :, cols]).then_inc(S.w_high, 1)

    def round_low(self, dve, S, c):
        dve.wait_ge(S.w_high, c + 1)
        cols = slice(0, self.width[c])
        low_part(dve, self.low[:, c % 2, :, cols], self.raw[:, c % 2, :, cols], self.high[:, c % 2, :, cols]).then_inc(S.w_split, 1)

    def parts(self, c, k, cols):
        return self.high[:, c % 2, k, cols], self.low[:, c % 2, k, cols]


def project(nc, M, tag, chunks, tiles, sub, gain=None, others=(), mine=None, ahead=None, dve_steps=None, act_steps=None):
    last_tile = [max(n for n, t in enumerate(tiles) if t[0] == c) for c in range(len(chunks))]
    engine_of = [t[3] for t in tiles]

    def evacuated(n):
        return engine_of[:n + 1].count(engine_of[n])

    signals = "product act_evacuated dve_evacuated others_landed step_chain conv_done" + SPLIT_SIGNALS + H_SIGNALS + GAIN_SIGNALS
    with ExitStack() as memory, stage(nc, tag, signals, mine) as (block, S):
        W = Chunks(nc, memory, tag, M, chunks, mine.landed if mine else [S.w0_landed, S.w1_landed])
        M.h_high, M.h_low = (rounded(nc, memory, tag + "_")(name, DT, T) for name in ("h_high", "h_low"))
        done = {"act": S.act_evacuated, "dve": S.dve_evacuated}

        @block.sync
        def _(sp):
            if gain is not None:
                rms_sp(sp, nc, M, S, gain)
            W.load_all(sp, S, 2 if mine else 0, ahead)

        @block.gpsimd
        def _(pool):
            with nc.allow_non_contiguous_dma(reason="small vectors as columns"):
                for dst, src in others:
                    pool.dma_start(dst, src).then_inc(S.others_landed, 16)
            if others:
                pool.wait_ge(S.others_landed, 16 * len(others))

        @block.tensor
        def _(pe):
            for n, (c, cols, i, _, _) in enumerate(tiles):
                if n == 0 or tiles[n - 1][0] != c:
                    pe.wait_ge(S.w_split, c + 1)
                if n >= 8:
                    pe.wait_ge(done[engine_of[n - 8]], evacuated(n - 8))
                for k in range(DT):
                    if n == 0:
                        pe.wait_ge(S.h_ready, k + 1)
                    w = W.parts(c, k, cols)
                    if i is None:
                        mm = product(pe, M.ps[:, n % 8, :], w, (M.h_high[:, k, :], M.h_low[:, k, :]), k == 0, k == DT - 1)
                    else:
                        tokens = slice(i * P, (i + 1) * P)
                        mm = product(pe, M.ps[:, n % 8, 0:cols.stop - cols.start],
                                     (M.h_high[:, k, tokens], M.h_low[:, k, tokens]), w, k == 0, k == DT - 1)
                mm.then_inc(S.product, 1)

        @block.scalar
        def _(act):
            W.round_high(act, S, 0)
            round_h_act(act, M, S)
            W.round_high(act, S, 1)
            for n, (c, _, i, engine, evacuate) in enumerate(tiles):
                if engine == "act":
                    act.wait_ge(S.product, n + 1)
                    evacuate(act, M.ps[:, n % 8, :], i).then_inc(S.act_evacuated, 1)
                if act_steps and n in act_steps:
                    act_steps[n](act, S)
                if n == last_tile[c] and c + 2 < len(chunks):
                    act.wait_ge(S.product, n + 1)
                    W.round_high(act, S, c + 2)

        @block.vector
        def _(dve):
            link = chain(dve, S.step_chain)
            if gain is not None:
                dve.wait_ge(S.gain_landed, 16)
                round_h_dve(dve, M, S, lambda d, out: rms_value(dve, M, d, out), lambda: W.round_low(dve, S, 0))
            else:
                modulate_dve(dve, M, S, sub, lambda: W.round_low(dve, S, 0))
            W.round_low(dve, S, 1)
            for n, (c, _, i, engine, evacuate) in enumerate(tiles):
                if engine == "dve":
                    dve.wait_ge(S.product, n + 1)
                    evacuate(dve, M.ps[:, n % 8, :], i).then_inc(S.dve_evacuated, 1)
                if dve_steps and n in dve_steps:
                    dve.wait_ge(done[engine], evacuated(n))
                    dve_steps[n](dve, S, link)
                if n == last_tile[c] and c + 2 < len(chunks):
                    W.round_low(dve, S, c + 2)


def mixer1_chunks(w_in):
    w = w_in.rearrange("(k p) n -> p k n", p=P)
    q_piece = lambda a, g: (slice(P * (a % 2) + HD * g, P * (a % 2) + HD * (g + 1)),
                            w[:, :, (a + HPG * g) * HD:(a + HPG * g + 1) * HD])
    chunks = [[q_piece(a, g) for a in (b, b + 1) for g in range(GROUPS)] for b in (0, 2)]
    chunks += [[(slice(HD * u, HD * (u + 1)), w[:, :, KC_OFF + KV * j + HD * (u // 2):KC_OFF + KV * j + HD * (u // 2 + 1)])
                for u in range(4)] for j in range(2)]
    starts = [KC_OFF + 2 * KV, KC_OFF + 4 * KV, GMLP_OFF, GMLP_OFF + 256, Z_OFF, XBC_OFF, XBC_OFF + 256, XBC_OFF + 512]
    chunks += [[(slice(0, 256), w[:, :, a:a + 256])] for a in starts]
    n = HEADS * N_BRANCH
    return chunks + [[(slice(0, n), w[:, :, GATE_OFF:GATE_OFF + n]), (slice(n, n + SH), w[:, :, DT_OFF:DT_OFF + SH])]]


def mixer1_project(nc, M, A, I, l, mine, ahead):
    chunks = mixer1_chunks(I.w_in[l])
    n_gates = HEADS * N_BRANCH
    cols = lambda a, n: slice(a, a + n)

    def q_tile(a):
        return lambda act, ps, i: act.activation(A.qT[:, a, :], ps, ACT.Copy, scale=HD ** -0.5)

    def blocks(j, g):
        def evacuate(dve, ps, i):
            for parity in range(2):
                half = ps[HD * parity:HD * (parity + 1)]
                ins = dve.tensor_copy(A.blk[HD * parity:HD * (parity + 1), j, g], bass.AP(
                    tensor=half.tensor, offset=half.offset + parity,
                    ap=[list(half.ap[0]), [2, CMP_LEN // 2], [CMP_STRIDE, N_CMP]]))
            return ins
        return evacuate

    def copy_to(dst):
        return lambda dve, ps, i: dve.tensor_copy(dst, ps[:, 0:dst.shape[-1]])

    def act_tile(dst, function, a, n):
        return lambda act, ps, i: act.activation(dst[:, i, a:a + n], ps[:, 0:n], function)

    def gate_dt_tile(act, ps, i):
        act.activation(A.gates[:, i, :], ps[:, 0:n_gates], ACT.Sigmoid)
        return act.copy(A.dt[:, i, :], ps[:, n_gates:n_gates + SH])

    tiles = [(a // 2, cols(P * (a % 2), P), None, "act", q_tile(a)) for a in range(HPG)]
    tiles += [(2 + j, cols(P * g, P), None, "dve", blocks(j, g)) for j in range(2) for g in range(GROUPS)]
    tiles += [(4, cols(0, P), None, "dve", copy_to(A.ksT[:]))]
    tiles += [(4, cols(P, KV), i, "dve", lambda dve, ps, i: dve.tensor_copy(A.vs[:, i, :], ps[:, 0:KV])) for i in range(TT)]
    tiles += [(5, cols(0, P), None, "dve", copy_to(A.kwT[:]))]
    tiles += [(5, cols(P, KV), i, "dve", lambda dve, ps, i: dve.tensor_copy(A.vw[:, i, :], ps[:, 0:KV])) for i in range(TT)]
    tiles += [(6 + half, cols(0, 256), i, "act", act_tile(A.uv, ACT.Gelu_apprx_tanh, 256 * half, 256))
              for half in range(2) for i in range(TT)]
    tiles += [(8, cols(0, D_SSM), i, "act", act_tile(A.silz, ACT.Silu, 0, D_SSM)) for i in range(TT)]
    tiles += [(9 + c // 2, cols(P * (c % 2), P), None, "dve", copy_to(A.raw[:, c, SCONV - 1:])) for c in range(XT)]
    tiles += [(12, cols(0, n_gates + SH), i, "act", gate_dt_tile) for i in range(TT)]
    others = [(M.bias[:], M.bias_dram), (A.ws[:], I.gmlp_ws[l].rearrange("g t s -> t g s"))]
    others += [(A.cmp_pos[:, j, :], I.cmp_pe[l, j].rearrange("(m r) d -> (r d) m", r=2)) for j in range(2)]
    others += [(A.cmp_w2[:, j, :, g, :], I.cmp_w2[l, j].rearrange("(m p) d -> p m d", p=P))
               for j in range(2) for g in range(GROUPS)]
    others += [(A.cmp_b, I.cmp_b1[l].rearrange("j n -> (j n)").partition_broadcast(P)),
               (A.conv_w[:], I.ssm_conv_w[l].rearrange("j (c p) -> p j c", p=P)),
               (A.conv_b[:], I.ssm_conv_b[l].rearrange("(c p) -> p c", p=P)),
               (A.ws_b[:], I.gmlp_bs[l].rearrange("g p -> p g"))]
    others += [(dst[:], vector[l].partition_broadcast(P)) for dst, vector in (
        (A.dt_bias, I.ssm_dt_bias), (A.a_log, I.ssm_a_log), (A.d_skip, I.ssm_d), (A.norm_g, I.ssm_norm_g),
        (A.ln_g, I.gmlp_ln_g), (A.ln_b, I.gmlp_ln_b))]
    project(nc, M, "proj1", chunks, tiles, 1, others=others, mine=mine, ahead=ahead)


PAIRS = CMP_LEN // 2


def compression_load(sp, M, landed, cmp_w1, n):
    slot = M.raw[:, n % 2].rearrange("p (m n) -> p m n", m=PAIRS // 2)
    src = cmp_w1[n // 2].rearrange("(m p) n -> p m n", p=P)[:, PAIRS // 2 * (n % 2):PAIRS // 2 * (n % 2 + 1), :]
    sp.dma_start(slot, src).then_inc(landed[n % 2], 16)


def compression_ahead(nc, M, tag, cmp_w1):
    return Ahead(nc, tag, lambda sp, landed: [compression_load(sp, M, landed, cmp_w1, n) for n in range(2)])


def mixer1_local(nc, M, A, I, l, mine, ahead):
    with stage(nc, "local", "half_used pos_added pre_ready hidden h_turned h_copied keys_ready taps_padded conv_acc conv_done "
               "ws_turned ws_copied v_normed spatial act_chain dve_chain var_ready root_ready exp_ready one_plus ln_ready",
               mine) as (block, S):
        landed = mine.landed
        slots = M.raw[:].rearrange("p s (m n) -> p s m n", m=PAIRS // 2)

        @block.sync
        def _(sp):
            for n in range(2, 4):
                sp.wait_ge(S.half_used, n - 1)
                compression_load(sp, M, landed, I.cmp_w1[l], n)
            sp.wait_ge(S.half_used, 4)
            ahead.load(sp)

        @block.tensor
        def _(pe):
            for g in range(GG):
                mm = pe.transpose(M.ps[:, 6, g * P:(g + 1) * P], A.ws[:, g, :], M.ident[:])
            mm.then_inc(S.ws_turned, 1)
            for n in range(4):
                j, half = n // 2, n % 2
                pe.wait_ge(S.pos_added, j + 1)
                pe.wait_ge(landed[n % 2], 16 * (n // 2 + 1))
                for g in range(GROUPS):
                    for q in range(PAIRS // 2):
                        mm = pe.matmul(M.ps[0:N_CMP, 2 * j + g, 0:CMP_HID], A.blk[:, j, g, PAIRS // 2 * half + q, :],
                                       slots[:, half, q, :], start=(half == 0 and q == 0),
                                       stop=(half == 1 and q == PAIRS // 2 - 1))
                mm.then_inc(S.half_used, 1)
            pe.wait_ge(S.ws_copied, 1)
            pe.wait_ge(S.v_normed, 1)
            for g in range(GG):
                rhs = A.uv[:, :, D_GMLP + GGD * g:D_GMLP + GGD * (g + 1)]
                out = M.ps[:, 6 + g // 2, (g % 2) * 256:(g % 2) * 256 + 256].rearrange("p (c d) -> p c d", c=TT)
                mm = pe.matmul(out, A.wsT[:, g, :], rhs, start=True, stop=True)
            mm.then_inc(S.spatial, 1)
            for j in range(2):
                pe.wait_ge(S.hidden, j + 1)
                for m in range(2):
                    for g in range(GROUPS):
                        u = 2 * m + g
                        mm = pe.transpose(M.ps[:, 4 + j, N_CMP * u:N_CMP * (u + 1)], A.cmp_x[0:N_CMP, 2 * j + g, m * P:(m + 1) * P],
                                          M.ident[0:N_CMP, 0:N_CMP])
                mm.then_inc(S.h_turned, 1)
            pe.wait_ge(S.h_copied, 1)
            for g in range(GROUPS):
                for m in range(2):
                    mm = pe.matmul(M.ps[:, g, 0:N_CMP], A.cmp_w2[:, 0, m].rearrange("p g d -> p (g d)"),
                                   A.cmp_h[:, 0, m, g, :], start=(m == 0), stop=(m == 1))
            pe.wait_ge(S.h_copied, 2)
            for g in range(GROUPS):
                for m in range(2):
                    mm = pe.matmul(M.ps[0:N_CMP, 2 + g, 0:HD], A.cmp_h[:, 1, m, g, :], A.cmp_w2[:, 1, m, 0, :],
                                   start=(m == 0), stop=(m == 1))
            mm.then_inc(S.keys_ready, 1)

        @block.scalar
        def _(act):
            link = chain(act, S.act_chain)
            link(act.activation(A.a_neg[:], A.a_log[:], ACT.Exp))
            act.wait_ge(S.one_plus, 1)
            act.activation(A.dt_e[:], A.dt_e[:], ACT.Exp, scale=-1.0).then_inc(S.exp_ready, 1)
            act.wait_ge(S.one_plus, 2)
            act.activation(A.dt_ln[:], A.dt_u[:], ACT.Ln).then_inc(S.ln_ready, 1)
            for c in range(XT):
                act.wait_ge(S.conv_acc, SCONV * (c + 1))
                act.activation(A.xbc[:, c, :], A.xbc[:, c, :], ACT.Silu, bias=A.conv_b[:, c:c + 1]).then_inc(S.conv_done, 1)
            act.wait_ge(S.var_ready, 1)
            act.activation(A.root[:, 0:TT], A.root[:, 0:TT], ACT.Sqrt).then_inc(S.root_ready, 1)
            for j in range(2):
                act.wait_ge(S.pre_ready, j + 1)
                x = A.cmp_x[0:N_CMP, 2 * j:2 * j + 2, :]
                act.activation(x, x, ACT.Gelu_apprx_tanh).then_inc(S.hidden, 1)

        @block.vector
        def _(dve):
            for j in range(2):
                for g in range(GROUPS):
                    ins = dve.tensor_tensor(A.blk[:, j, g], A.blk[:, j, g], A.cmp_pos[:, j].unsqueeze(2)
                                            .to_broadcast([P, PAIRS, N_CMP]), ALU.add)
                ins.then_inc(S.pos_added, 1)
            dve.memset(A.raw[:, :, 0:SCONV - 1], 0.0).then_inc(S.taps_padded, 1)
            dve.wait_ge(S.taps_padded, 1)
            link = chain(dve, S.dve_chain)
            link(dve.tensor_tensor(A.dt[:], A.dt[:], A.dt_bias[:].unsqueeze(1).to_broadcast([P, TT, SH]), ALU.add))
            dve.scalar_tensor_tensor(out=A.dt_e[:], in0=A.dt[:], scalar=-1.0, in1=A.dt[:], op0=ALU.mult,
                                     op1=ALU.max).then_inc(S.one_plus, 1)
            dve.wait_ge(S.exp_ready, 1)
            dve.tensor_scalar(A.dt_u[:], A.dt_e[:], 1.0, None, ALU.add).then_inc(S.one_plus, 1)
            dve.wait_ge(S.one_plus, 2)
            link(dve.scalar_tensor_tensor(out=A.dt_r[:], in0=A.dt_u[:], scalar=-1.0, in1=A.dt_e[:], op0=ALU.add,
                                          op1=ALU.subtract))
            link(dve.tensor_scalar(A.dt[:], A.dt[:], 0.0, None, ALU.max))
            link(dve.tensor_tensor(A.dt[:], A.dt[:], A.dt_r[:], ALU.subtract))
            dve.wait_ge(S.ln_ready, 1)
            link(dve.tensor_tensor(A.dt[:], A.dt[:], A.dt_ln[:], ALU.add))
            dve.wait_ge(S.act_chain, 1)
            link(dve.scalar_tensor_tensor(out=A.a[:], in0=A.dt[:], scalar=-1.0,
                                          in1=A.a_neg[:].unsqueeze(1).to_broadcast([P, TT, SH]),
                                          op0=ALU.mult, op1=ALU.mult))
            for c in range(XT):
                dve.tensor_scalar(A.xbc[:, c, :], A.raw[:, c, 0:T], A.conv_w[:, 0, c:c + 1], None,
                                  ALU.mult).then_inc(S.conv_acc, 1)
                for j in range(1, SCONV):
                    dve.wait_ge(S.conv_acc, SCONV * c + j)
                    dve.scalar_tensor_tensor(out=A.xbc[:, c, :], in0=A.raw[:, c, j:j + T],
                                             scalar=A.conv_w[:, j, c:c + 1], in1=A.xbc[:, c, :],
                                             op0=ALU.mult, op1=ALU.add).then_inc(S.conv_acc, 1)
            for i in range(TT):
                link(dve.bn_stats(A.stats[:, i, :], A.uv[:, i, D_GMLP:]))
            for i in range(TT):
                link(dve.bn_aggr(A.mv[:, i, :], A.stats[:, i, :]))
            dve.tensor_scalar(A.root[:, 0:TT], A.mv[:, :, 1], LN_EPS, None, ALU.add).then_inc(S.var_ready, 1)
            dve.wait_ge(S.root_ready, 1)
            link(dve.reciprocal(A.root[:, 0:TT], A.root[:, 0:TT]))
            for i in range(TT):
                v = A.uv[:, i, D_GMLP:]
                link(dve.tensor_scalar(v, v, A.mv[:, i, 0:1], A.root[:, i:i + 1], ALU.subtract, ALU.mult))
                link(dve.tensor_tensor(v, v, A.ln_g[:], ALU.mult))
                ins = dve.tensor_tensor(v, v, A.ln_b[:], ALU.add)
            ins.then_inc(S.v_normed, 1)
            dve.wait_ge(S.ws_turned, 1)
            dve.tensor_tensor(A.wsT[:], M.ps[:, 6, :].rearrange("p (g t) -> p g t", g=GG),
                              M.tri[:, 3 * P:4 * P].unsqueeze(1).to_broadcast([P, GG, P]),
                              ALU.mult).then_inc(S.ws_copied, 1)
            for j in range(2):
                dve.wait_ge(S.half_used, 2 * (j + 1))
                bias = A.cmp_b[0:N_CMP, CMP_HID * j:CMP_HID * (j + 1)]
                for g in range(GROUPS):
                    ins = dve.tensor_tensor(A.cmp_x[0:N_CMP, 2 * j + g, :], M.ps[0:N_CMP, 2 * j + g, 0:CMP_HID], bias, ALU.add)
                ins.then_inc(S.pre_ready, 1)
            for j in range(2):
                dve.wait_ge(S.h_turned, j + 1)
                dve.tensor_copy(A.cmp_h[:, j].rearrange("p m g n -> p (m g n)"), M.ps[:, 4 + j, 0:4 * N_CMP]).then_inc(S.h_copied, 1)
            dve.wait_ge(S.keys_ready, 1)
            for g in range(GROUPS):
                dve.tensor_copy(A.kcT[HD * g:HD * (g + 1), :], M.ps[HD * g:HD * (g + 1), g, 0:N_CMP])
                dve.tensor_copy(A.vc[0:N_CMP, g, :], M.ps[0:N_CMP, 2 + g, 0:HD])
            dve.wait_ge(S.spatial, 1)
            for g in range(GG):
                ps = M.ps[:, 6 + g // 2, (g % 2) * 256:(g % 2) * 256 + 256].rearrange("p (c d) -> p c d", c=TT)
                dve.scalar_tensor_tensor(out=A.mix[:, :, HEADS * HD + GGD * g:HEADS * HD + GGD * (g + 1)], in0=ps,
                                         scalar=A.ws_b[:, g:g + 1], in1=A.uv[:, :, GGD * g:GGD * (g + 1)],
                                         op0=ALU.add, op1=ALU.mult)


def mixer1_compressed(nc, M, A):
    with stage(nc, "cmp", "bias_init bias_c scores chain shifted probs normed turned turned_copied pv mixed") as (block, S):

        @block.tensor
        def _(pe):
            def outputs(i):
                pe.wait_ge(S.normed, i + 1)
                if i >= 2:
                    pe.wait_ge(S.turned_copied, i - 1)
                for h in range(HEADS):
                    mm = pe.transpose(M.ps[0:N_CMP, 4 * (i % 2) + 1 + h // 4, (h % 4) * P:(h % 4 + 1) * P], A.score_c[:, i, h, :],
                                      M.ident[:])
                mm.then_inc(S.turned, 1)
                pe.wait_ge(S.turned_copied, i + 1)
                for h in range(HEADS):
                    mm = pe.matmul(M.ps[:, 4 * (i % 2) + 3, HD * h:HD * (h + 1)], A.turned_c[0:N_CMP, i % 2, h * P:(h + 1) * P],
                                   A.vc[0:N_CMP, h // HPG, :], start=True, stop=True)
                mm.then_inc(S.pv, 1)

            for i in range(TT):
                if i >= 2:
                    pe.wait_ge(S.mixed, i - 1)
                for h in range(HEADS):
                    rows = slice(HD * (h // HPG), HD * (h // HPG + 1))
                    mm = pe.matmul(M.ps[:, 4 * (i % 2) + 3 * (h // HPG), N_CMP * (h % HPG):N_CMP * (h % HPG + 1)], A.qT[rows, h % HPG, i * P:(i + 1) * P],
                                   A.kcT[rows, :], start=True, stop=True)
                mm.then_inc(S.scores, 1)
                if i >= 1:
                    outputs(i - 1)
            outputs(TT - 1)

        @block.scalar
        def _(act):
            for i in range(TT):
                act.wait_ge(S.shifted, i + 1)
                act.activation(A.score_c[:, i], A.score_c[:, i], ACT.Exp).then_inc(S.probs, 1)

        @block.vector
        def _(dve):
            dve.memset(A.bias_c[:], MASKED).then_inc(S.bias_init, 1)
            dve.wait_ge(S.bias_init, 1)
            for i in range(TT):
                start = (TT - 1 - i) * P + CMP_LEN - 1
                n = min(N_CMP, -(-(T - start) // CMP_STRIDE))
                ins = dve.tensor_copy(A.bias_c[:, i, :, 0:n], A.bias_all[:, :, start:start + CMP_STRIDE * (n - 1) + 1:CMP_STRIDE])
            ins.then_inc(S.bias_c, 1)
            dve.wait_ge(S.bias_c, 1)
            link = chain(dve, S.chain)
            spread = lambda ap: ap.unsqueeze(2).to_broadcast([P, HEADS, N_CMP])

            def probabilities(i):
                s, d = A.score_c[:, i], A.denom_c[:, i, :]
                dve.wait_ge(S.scores, i + 1)
                for g in range(GROUPS):
                    heads = slice(HPG * g, HPG * (g + 1))
                    link(dve.tensor_tensor(s[:, heads], M.ps[:, 4 * (i % 2) + 3 * g, 0:HPG * N_CMP]
                                           .rearrange("p (h n) -> p h n", h=HPG), A.bias_c[:, i, heads], ALU.add))
                link(dve.tensor_reduce(d, s, AX.X, ALU.max))
                link(dve.tensor_scalar(d, d, FLOOR, None, ALU.max))
                dve.tensor_tensor(s, s, spread(d), ALU.subtract).then_inc(S.shifted, 1)

            def normalise(i):
                s, d = A.score_c[:, i], A.denom_c[:, i, :]
                dve.wait_ge(S.probs, i + 1)
                link(dve.tensor_reduce(d, s, AX.X, ALU.add))
                link(dve.tensor_scalar(d, d, 1e-30, None, ALU.max))
                link(dve.reciprocal(d, d))
                gates = A.gates[:, i, :].rearrange("p (h b) -> p h b", b=N_BRANCH)[:, :, 0]
                link(dve.tensor_tensor(d, d, gates, ALU.mult))
                dve.tensor_tensor(s, s, spread(d), ALU.mult).then_inc(S.normed, 1)

            def turn(i):
                if i >= 2:
                    dve.wait_ge(S.pv, i - 1)
                dve.wait_ge(S.turned, i + 1)
                dve.tensor_copy(A.turned_c[0:N_CMP, i % 2, 0:4 * P], M.ps[0:N_CMP, 4 * (i % 2) + 1, :])
                dve.tensor_copy(A.turned_c[0:N_CMP, i % 2, 4 * P:], M.ps[0:N_CMP, 4 * (i % 2) + 2, :]).then_inc(S.turned_copied, 1)

            def outputs(i):
                dve.wait_ge(S.pv, i + 1)
                dve.tensor_copy(A.mix[:, i, 0:HEADS * HD], M.ps[:, 4 * (i % 2) + 3, :]).then_inc(S.mixed, 1)

            probabilities(0)
            for i in range(TT):
                normalise(i)
                if i:
                    outputs(i - 1)
                if i + 1 < TT:
                    probabilities(i + 1)
                turn(i)
            outputs(TT - 1)


def mixer1_attention(nc, M, A):
    units = [(i, h) for i in range(TT) for h in range(HEADS)]
    N = len(units)
    with stage(nc, "attn", "scores score_biased shifted probs turned slc_copied "
               "win_copied pv mixed norm_chain") as (block, S):

        def branch_bias(i, h):
            start = (TT - 1 - i) * P
            return A.bias_all[:, h, start:start + (i + 1) * P]

        @block.tensor
        def _(pe):
            def scores(u):
                i, h = units[u]
                g, a = h // HPG, h % HPG
                rows, keys = slice(HD * g, HD * (g + 1)), (i + 1) * P
                q = A.qT[rows, a, i * P:(i + 1) * P]
                if u >= 2:
                    pe.wait_ge(S.score_biased, u - 1)
                pe.matmul(M.ps[:, 2 * (u % 2), 0:keys], q, A.ksT[rows, 0:keys], start=True, stop=True)
                pe.matmul(M.ps[:, 2 * (u % 2) + 1, 0:keys], q, A.kwT[rows, 0:keys], start=True, stop=True
                          ).then_inc(S.scores, 1)

            def turn(u):
                i, h = units[u]
                pe.wait_ge(S.probs, u + 1)
                if u >= 1:
                    pe.wait_ge(S.slc_copied, u)
                    pe.wait_ge(S.win_copied, u)
                for j in range(i + 1):
                    pe.transpose(M.ps[:, 6, j * P:(j + 1) * P], A.probs[:, u % 2, 0, j * P:(j + 1) * P], M.ident[:])
                for j in range(i + 1):
                    mm = pe.transpose(M.ps[:, 7, j * P:(j + 1) * P], A.probs[:, u % 2, 1, j * P:(j + 1) * P], M.ident[:])
                mm.then_inc(S.turned, 1)

            def values(u):
                i, h = units[u]
                cols = slice(HD * (h // HPG), HD * (h // HPG + 1))
                bank = M.ps[:, 4 + u % 2, :]
                pe.wait_ge(S.slc_copied, u + 1)
                pe.wait_ge(S.win_copied, u + 1)
                if u >= 2:
                    pe.wait_ge(S.mixed, u - 1)
                for j in range(i + 1):
                    pe.matmul(bank[:, 0:HD], A.turned[:, u % 2, 0, j * P:(j + 1) * P], A.vs[:, j, cols],
                              start=(j == 0), stop=(j == i))
                for j in range(i + 1):
                    mm = pe.matmul(bank[:, HD:2 * HD], A.turned[:, u % 2, 1, j * P:(j + 1) * P], A.vw[:, j, cols],
                                   start=(j == 0), stop=(j == i))
                mm.then_inc(S.pv, 1)

            for step in range(N + 2):
                if step < N:
                    scores(step)
                if step >= 2:
                    values(step - 2)
                if 1 <= step <= N:
                    turn(step - 1)

        @block.scalar
        def _(act):
            def exps(u):
                i, h = units[u]
                keys = (i + 1) * P
                act.wait_ge(S.shifted, u + 1)
                if u >= 2:
                    act.wait_ge(S.turned, u - 1)
                for b in range(2):
                    ins = act.activation(A.probs[:, u % 2, b, 0:keys], A.score[:, u % 2, b, 0:keys], ACT.Exp,
                                         bias=A.shift[:, u % 2, b:b + 1], accum_out=A.sums[:, u % 4, b:b + 1])
                ins.then_inc(S.probs, 1)

            def copy(u):
                i, h = units[u]
                act.wait_ge(S.turned, u + 1)
                if u >= 2:
                    act.wait_ge(S.pv, u - 1)
                act.copy(A.turned[:, u % 2, 0, 0:(i + 1) * P], M.ps[:, 6, 0:(i + 1) * P]).then_inc(S.slc_copied, 1)

            for step in range(N + 1):
                if step < N:
                    exps(step)
                if step >= 1:
                    copy(step - 1)

        @block.vector
        def _(dve):
            def biased(u):
                i, h = units[u]
                keys = (i + 1) * P
                dve.wait_ge(S.scores, u + 1)
                if u >= 2:
                    dve.wait_ge(S.probs, u - 1)
                for b in range(2):
                    ins = dve.tensor_tensor_reduce(A.score[:, u % 2, b, 0:keys], M.ps[:, 2 * (u % 2) + b, 0:keys],
                                                   branch_bias(i, h), 1.0, FLOOR, ALU.add, ALU.max,
                                                   A.top[:, u % 2, b:b + 1])
                ins.then_inc(S.score_biased, 1)
                dve.wait_ge(S.score_biased, u + 1)
                dve.tensor_scalar(A.shift[:, u % 2, :], A.top[:, u % 2, :], FLOOR, -1.0, ALU.max, ALU.mult
                                  ).then_inc(S.shifted, 1)

            def copy(u):
                i, h = units[u]
                dve.wait_ge(S.turned, u + 1)
                if u >= 2:
                    dve.wait_ge(S.pv, u - 1)
                dve.tensor_copy(A.turned[:, u % 2, 1, 0:(i + 1) * P], M.ps[:, 7, 0:(i + 1) * P]).then_inc(S.win_copied, 1)

            def combine(u):
                i, h = units[u]
                n = 4 * u
                d, out = A.denom[:, u % 4, :], A.mix[:, i, HD * h:HD * (h + 1)]
                dve.tensor_scalar(d, A.sums[:, u % 4, :], 1e-30, None, ALU.max).then_inc(S.norm_chain, 1)
                dve.wait_ge(S.norm_chain, n + 1)
                dve.reciprocal(d, d).then_inc(S.norm_chain, 1)
                dve.wait_ge(S.norm_chain, n + 2)
                dve.tensor_tensor(d, d, A.gates[:, i, N_BRANCH * h + 1:N_BRANCH * (h + 1)],
                                  ALU.mult).then_inc(S.norm_chain, 1)
                dve.wait_ge(S.norm_chain, n + 3)
                dve.wait_ge(S.pv, u + 1)
                bank = M.ps[:, 4 + u % 2, :]
                dve.scalar_tensor_tensor(out=out, in0=bank[:, 0:HD], scalar=d[:, 0:1], in1=out, op0=ALU.mult,
                                         op1=ALU.add).then_inc(S.norm_chain, 1)
                dve.wait_ge(S.norm_chain, n + 4)
                dve.scalar_tensor_tensor(out=out, in0=bank[:, HD:2 * HD], scalar=d[:, 1:2], in1=out, op0=ALU.mult,
                                         op1=ALU.add).then_inc(S.mixed, 1)

            for step in range(N + 3):
                if step < N:
                    biased(step)
                if 1 <= step <= N:
                    copy(step - 1)
                if step >= 3:
                    combine(step - 3)


def mixer1_ssd(nc, M, A):
    hpg = SH // SG
    with stage(nc, "ssd", "x_turned x_copied sums_col col_copied sums_row cb diff decay weighted "
               "y_ready chain squares_done root_ready") as (block, S):
        tri = lambda k, n0, n1: M.tri[:, 3 * P - k * P + n0:3 * P - k * P + n1]
        steps = [(g, k) for g in range(SG) for k in range(TT)]

        @block.tensor
        def _(pe):
            for c in range(2):
                for i in range(TT):
                    mm = pe.transpose(M.ps[:, c, i * P:(i + 1) * P], A.xbc[:, c, i * P:(i + 1) * P], M.ident[:])
                mm.then_inc(S.x_turned, 1)
            for k in range(TT):
                for j in range(k + 1):
                    mm = pe.matmul(M.ps[:, 2, SH * k:SH * (k + 1)], tri(j, k * P, (k + 1) * P), A.a[:, j, :],
                                   start=(j == 0), stop=(j == k))
            mm.then_inc(S.sums_col, 1)
            for h in range(SH):
                for j in range(TT):
                    mm = pe.matmul(M.ps[:, 4 + h, :], A.a[:, j, h:h + 1].to_broadcast([P, P]), tri(j, 0, T),
                                   start=(j == 0), stop=(j == TT - 1))
                mm.then_inc(S.sums_row, 1)
            pe.wait_ge(S.x_copied, 2)

            def product_cb(n):
                g, k = steps[n]
                if n >= 2:
                    pe.wait_ge(S.weighted, hpg * (n - 1))
                if n < 2:
                    pe.wait_ge(S.col_copied, 1)
                pe.matmul(M.ps[:, n % 2, k * P:T], A.xbc[:, 2 + g, k * P:(k + 1) * P], A.xbc[:, 2 + SG + g, k * P:T],
                          start=True, stop=True).then_inc(S.cb, 1)

            def outputs(g, tiles):
                pe.wait_ge(S.weighted, hpg * TT * (g + 1))
                for i in tiles:
                    for h in range(hpg * g, hpg * (g + 1)):
                        for k in range(i + 1):
                            mm = pe.matmul(M.ps[:, 2 + i // 2, (i % 2) * 256 + HD * h:(i % 2) * 256 + HD * (h + 1)],
                                           A.decay[:, h, k, i * P:(i + 1) * P], A.xdt[:, k, h * HD:(h + 1) * HD],
                                           start=(k == 0), stop=(k == i))
                return mm

            for n in range(TT + 2):
                product_cb(n)
            outputs(0, range(3))
            product_cb(TT + 2)
            outputs(0, [3])
            product_cb(TT + 3)
            mm = outputs(1, range(TT))
            mm.then_inc(S.y_ready, 1)

        @block.scalar
        def _(act):
            n = 0
            for g, k in steps:
                for h in range(hpg * g, hpg * (g + 1)):
                    n += 1
                    act.wait_ge(S.diff, n)
                    act.activation(A.decay[:, h, k, k * P:T], A.decay[:, h, k, k * P:T], ACT.Exp).then_inc(S.decay, 1)
            act.wait_ge(S.squares_done, 1)
            act.activation(A.root[:], A.root[:], ACT.Sqrt).then_inc(S.root_ready, 1)

        @block.vector
        def _(dve):
            link = chain(dve, S.chain)
            for c in range(2):
                dve.wait_ge(S.x_turned, c + 1)
                dve.tensor_copy(A.xs[:, :, c * P:(c + 1) * P], M.ps[:, c, :].rearrange("p (i d) -> p i d", i=TT)
                                ).then_inc(S.x_copied, 1)
            dve.wait_ge(S.x_copied, 2)
            link(dve.tensor_tensor(A.xdt[:].rearrange("p i (h d) -> p (i h) d", h=SH),
                                   A.xs[:].rearrange("p i (h d) -> p (i h) d", h=SH),
                                   A.dt[:].rearrange("p i h -> p (i h)").unsqueeze(2).to_broadcast([P, TT * SH, HD]), ALU.mult))
            dve.wait_ge(S.sums_col, 1)
            dve.tensor_copy(A.cs[:], M.ps[:, 2, 0:SH * TT]).then_inc(S.col_copied, 1)
            dve.wait_ge(S.col_copied, 1)
            units = [(g, k, h) for g, k in steps for h in range(hpg * g, hpg * (g + 1))]

            def difference(n):
                g, k, h = units[n]
                dve.wait_ge(S.sums_row, h + 1)
                dve.tensor_scalar(A.decay[:, h, k, k * P:T], M.ps[:, 4 + h, k * P:T], A.cs[:, SH * k + h:SH * k + h + 1],
                                  0.0, ALU.subtract, ALU.min).then_inc(S.diff, 1)

            def weigh(n):
                g, k, h = units[n]
                dve.wait_ge(S.decay, n + 1)
                dve.wait_ge(S.cb, n // hpg + 1)
                link(dve.tensor_tensor(A.decay[:, h, k, k * P:T], A.decay[:, h, k, k * P:T], tri(0, 0, T - k * P), ALU.mult))
                dve.tensor_tensor(A.decay[:, h, k, k * P:T], A.decay[:, h, k, k * P:T], M.ps[:, (n // hpg) % 2, k * P:T],
                                  ALU.mult).then_inc(S.weighted, 1)

            difference(0)
            difference(1)
            for n in range(len(units)):
                if n + 2 < len(units):
                    difference(n + 2)
                weigh(n)
            out = A.mix[:, :, HEADS * HD + D_GMLP:]
            heads = lambda ap: ap.rearrange("p i (h d) -> p i h d", h=SH)
            for i in range(TT):
                link(dve.tensor_tensor(out[:, i, :].rearrange("p (h d) -> p h d", h=SH),
                                       A.xs[:, i, :].rearrange("p (h d) -> p h d", h=SH),
                                       A.d_skip[:].unsqueeze(2).to_broadcast([P, SH, HD]), ALU.mult))
            dve.wait_ge(S.y_ready, 1)
            for i in range(2):
                pair = out[:, 2 * i:2 * i + 2, :]
                link(dve.tensor_tensor(pair, pair, M.ps[:, 2 + i, :].rearrange("p (i d) -> p i d", i=2), ALU.add))
            link(dve.tensor_tensor(out, out, A.silz[:], ALU.mult))
            link(dve.tensor_tensor(A.xdt[:], out, out, ALU.mult))
            link(dve.tensor_reduce(A.root[:], A.xdt[:].rearrange("p i (g d) -> p (i g) d", g=SG), AX.X, ALU.add))
            dve.tensor_scalar(A.root[:], A.root[:], SG / D_SSM, LN_EPS, ALU.mult, ALU.add).then_inc(S.squares_done, 1)
            dve.wait_ge(S.root_ready, 1)
            link(dve.reciprocal(A.root[:], A.root[:]))
            for i in range(TT):
                o = out[:, i, :]
                og = o.rearrange("p (g d) -> p g d", g=SG)
                link(dve.tensor_tensor(og, og, A.root[:, SG * i:SG * (i + 1)].unsqueeze(2).to_broadcast([P, SG, D_SSM // SG]),
                                       ALU.mult))
                link(dve.tensor_tensor(o, o, A.norm_g[:], ALU.mult))


def out_chunks(w_out):
    w = w_out.rearrange("(k p) n -> p k n", p=P)
    return [[(slice(0, 256), w[:, :, a:a + 256])] for a in range(0, D, 256)]


def mix_out(nc, M, tag, mix, turned, w_out, sub, mine, ahead):
    n_turned = 0 if turned is None else turned.shape[1]
    signals = "mix_turned mix_high mix_ready y_ready" + SPLIT_SIGNALS + (NORM_SIGNALS if sub is not None else ROOT_SIGNALS)
    with ExitStack() as memory, stage(nc, tag, signals, mine) as (block, S):
        chunks = D // Chunks.WIDTH
        W = Chunks(nc, memory, tag, M, out_chunks(w_out), mine.landed)
        mix_high, mix_low = (rounded(nc, memory, tag + "_")(name, DT, T) for name in ("mix_high", "mix_low"))
        source = [M.ps[:, k, :] for k in range(DT - n_turned)] + [turned[:, k, :] for k in range(n_turned)]

        @block.sync
        def _(sp):
            W.load_all(sp, S, 2, ahead)

        @block.tensor
        def _(pe):
            for k in range(DT - n_turned):
                for i in range(TT):
                    mm = pe.transpose(M.ps[:, k, i * P:(i + 1) * P], mix[:, i, k * P:(k + 1) * P], M.ident[:])
                mm.then_inc(S.mix_turned, 1)
            for d in range(DT):
                pe.wait_ge(S.w_split, d // 2 + 1)
                for k in range(DT):
                    if d == 0:
                        pe.wait_ge(S.mix_ready, k + 1)
                    mm = product(pe, M.ps[:, d, :], W.parts(d // 2, k, slice(P * (d % 2), P * (d % 2 + 1))),
                                 (mix_high[:, k, :], mix_low[:, k, :]), k == 0, k == DT - 1)
                mm.then_inc(S.y_ready, 1)
            if sub is not None:
                post_norm_pe(pe, M, S)
            else:
                rms_pe(pe, M, S)

        @block.scalar
        def _(act):
            W.round_high(act, S, 0)
            for k in range(DT):
                if k < DT - n_turned:
                    act.wait_ge(S.mix_turned, k + 1)
                act.copy(mix_high[:, k, :], source[k]).then_inc(S.mix_high, 1)
            W.round_high(act, S, 1)
            for c in range(2, chunks):
                act.wait_ge(S.y_ready, 2 * c - 2)
                W.round_high(act, S, c)
            if sub is not None:
                post_norm_act(act, M, S, sub)
            else:
                rms_act(act, M, S, True)

        @block.vector
        def _(dve):
            W.round_low(dve, S, 0)
            for k in range(DT):
                dve.wait_ge(S.mix_high, k + 1)
                low_part(dve, mix_low[:, k, :], source[k], mix_high[:, k, :]).then_inc(S.mix_ready, 1)
            W.round_low(dve, S, 1)

            def split(d):
                if d in (2, 4):
                    W.round_low(dve, S, d // 2 + 1)

            if sub is not None:
                post_norm_dve(dve, M, S, sub, split)
            else:
                add_y_dve(dve, M, S, split)


def mixer1(nc, M, I, l, mine, ahead):
    with ExitStack() as memory:
        sb = tensors(nc, memory, "a_")
        A = Memory()
        M.bias = sb("bias", HEADS, T)
        A.bias_all = M.bias
        A.mix = sb("mix", TT, D)
        A.qT = sb("qT", HPG, T)
        A.ksT, A.kwT = sb("ksT", T), sb("kwT", T)
        A.vs, A.vw = sb("vs", TT, KV), sb("vw", TT, KV)
        A.gates = sb("gates", TT, HEADS * N_BRANCH)
        A.kcT, A.vc = sb("kcT", N_CMP), sb("vc", GROUPS, HD)
        A.silz, A.dt, A.a = sb("silz", TT, D_SSM), sb("dt", TT, SH), sb("a", TT, SH)
        A.xbc = sb("xbc", XT, T)
        A.d_skip, A.norm_g = sb("d_skip", SH), sb("norm_g", D_SSM)
        A.root = sb("root", TT * SG)
        with ExitStack() as inner:
            sb = tensors(nc, inner, "a_")
            A.uv = sb("uv", TT, 2 * D_GMLP)
            A.raw = sb("raw", XT, T + SCONV - 1)
            flat = A.mix[:].rearrange("p i n -> p (i n)")
            n_blk = 2 * CMP_LEN * N_CMP
            A.blk = flat[:, 0:n_blk].rearrange("p (j g m n) -> p j g m n", j=2, g=GROUPS, m=PAIRS)
            A.cmp_b = flat[:, n_blk:n_blk + 2 * CMP_HID]
            A.cmp_pos, A.cmp_w2, A.ws = sb("cmp_pos", 2, PAIRS), sb("cmp_w2", 2, 2, GROUPS, HD), sb("ws", GG, P)
            A.conv_w, A.conv_b, A.ws_b = sb("conv_w", SCONV, XT), sb("conv_b", XT), sb("ws_b", GG)
            A.ln_g, A.ln_b = sb("ln_g", D_GMLP), sb("ln_b", D_GMLP)
            A.dt_bias, A.a_log = sb("dt_bias", SH), sb("a_log", SH)
            local_ahead = compression_ahead(nc, M, "local", I.cmp_w1[l])
            mixer1_project(nc, M, A, I, l, mine, local_ahead)
            A.cmp_x = sb("cmp_x", 4, CMP_HID)
            A.cmp_h = sb("cmp_h", 2, 2, GROUPS, N_CMP)
            A.wsT, A.a_neg = sb("wsT", GG, P), sb("a_neg", SH)
            A.dt_e, A.dt_u, A.dt_r, A.dt_ln = (sb(f"dt_{x}", TT, SH) for x in "eurl")
            A.stats, A.mv = sb("stats", TT, 6), sb("mv", TT, 2)
            out_ahead = chunks_ahead(nc, M, "out1", out_chunks(I.w_out[l]))
            mixer1_local(nc, M, A, I, l, local_ahead, out_ahead)
        with ExitStack() as inner:
            sb = tensors(nc, inner, "a_")
            A.bias_c, A.score_c = sb("bias_c", TT, HEADS, N_CMP), sb("score_c", TT, HEADS, N_CMP)
            A.turned_c, A.denom_c = sb("turned_c", 2, HEADS * P), sb("denom_c", TT, HEADS)
            mixer1_compressed(nc, M, A)
        with ExitStack() as inner:
            sb = tensors(nc, inner, "a_")
            A.score, A.probs, A.turned = sb("score", 2, 2, T), sb("probs", 2, 2, T), sb("turned", 2, 2, T)
            A.top, A.shift, A.sums, A.denom = (sb(x, n, 2) for x, n in (("top", 2), ("shift", 2), ("sums", 4), ("denom", 4)))
            mixer1_attention(nc, M, A)
        with ExitStack() as inner:
            sb = tensors(nc, inner, "a_")
            A.xs, A.xdt = sb("xs", TT, D_SSM), sb("xdt", TT, D_SSM)
            A.cs = sb("cs", TT * SH)
            A.decay = sb("decay", SH, TT, T)
            mixer1_ssd(nc, M, A)
        mix_out(nc, M, "out1", A.mix, None, I.w_out[l], 1, out_ahead, ahead)


def sum_selectors():
    out = np.zeros((P, 7 * 32), np.float32)
    out[:, 96:128] = 1
    return out


def spread_selectors():
    out = np.zeros((P, 4, P), np.float32)
    for u in range(4):
        out[32 * u, u] = 1
    return out


def mixer2_chunks(w_in):
    w = w_in.rearrange("(k p) n -> p k n", p=P)
    ba = 4 * DW
    sc = ba + 2 * DH
    starts = [*range(sc, W2_COLS, 256), *range(0, ba, 256)]
    return [[(slice(0, 256), w[:, :, a:a + 256])] for a in starts] + [[(slice(0, 2 * DH), w[:, :, ba:sc])]]


def mixer2_project(nc, M, A, I, l, ahead):
    cols = lambda a, n: slice(a, a + n)

    def copy(engine, dst):
        return lambda e, ps, i: (e.copy if engine == "act" else e.tensor_copy)(dst, ps)

    def rows(first, tile_dst):
        return [(first + c // 2, cols(P * (c % 2), P), None, ("act", "dve")[c % 2], copy(("act", "dve")[c % 2], tile_dst(c)))
                for c in range(4)]

    def silu(half):
        return lambda act, ps, i: act.activation(A.silz[:, i, 256 * half:256 * (half + 1)], ps[:, 0:256], ACT.Silu)

    tiles = rows(0, lambda c: A.gate_b[:, c, :]) + rows(2, lambda c: A.gate_c[:, c, :])
    tiles += rows(4, lambda c: A.prod[:, c, SCCONV - 1:])
    for n in range(3):
        tiles += rows(6 + 2 * n, lambda h: A.raw[:, DH * n + h, DCONV - 1:])
    tiles += [(12 + half, cols(0, 256), i, "act", silu(half)) for half in range(2) for i in range(TT)]
    tiles += [(14, cols(0, 2 * DH), i, "dve", lambda dve, ps, i: dve.tensor_copy(A.ba[:, i, :], ps[:, 0:2 * DH]))
              for i in range(TT)]
    others = [(A.conv_w[:, j, :], I.dn_conv_w_2[l, j].rearrange("(c p) -> p c", p=P)) for j in range(DCONV)]
    others += [(A.sc_w[:, j, :], I.sc_conv_w_2[l, j].rearrange("(c p) -> p c", p=P)) for j in range(SCCONV)]
    others += [(A.sc_g[:], I.sc_norm_g_2[l].rearrange("(c p) -> p c", p=P))]
    others += [(dst[:], vector[l].partition_broadcast(P))
               for dst, vector in ((A.dt_bias, I.dn_dt_bias_2), (A.a_log, I.dn_a_log_2), (A.norm_g, I.dn_norm_g_2))]

    def gated_convolution(c):
        def step(dve, S, link):
            if c == 0:
                dve.wait_ge(S.others_landed, 16 * len(others))
                link(dve.memset(A.raw[:, :, 0:DCONV - 1], 0.0))
                link(dve.memset(A.prod[:, :, 0:SCCONV - 1], 0.0))
            x, y = A.prod[:, c, :], A.gate_c[:, c, :]
            link(dve.tensor_tensor(x[:, SCCONV - 1:], x[:, SCCONV - 1:], y, ALU.mult))
            link(dve.tensor_scalar(y, x[:, 0:T], A.sc_w[:, 0, c:c + 1], None, ALU.mult))
            for j in range(1, SCCONV):
                link(dve.scalar_tensor_tensor(out=y, in0=x[:, j:j + T], scalar=A.sc_w[:, j, c:c + 1], in1=y,
                                              op0=ALU.mult, op1=ALU.add))
            dve.tensor_tensor(y, y, A.gate_b[:, c, :], ALU.mult)
        return step

    def convolution(u):
        def step(dve, S, link):
            link(dve.tensor_scalar(A.qkv[:, u, :], A.raw[:, u, 0:T], A.conv_w[:, 0, u:u + 1], None, ALU.mult))
            for j in range(1, DCONV):
                ins = dve.scalar_tensor_tensor(out=A.qkv[:, u, :], in0=A.raw[:, u, j:j + T], scalar=A.conv_w[:, j, u:u + 1],
                                               in1=A.qkv[:, u, :], op0=ALU.mult, op1=ALU.add)
                if j < DCONV - 1:
                    link(ins)
            ins.then_inc(S.conv_done, 1)
        return step

    def conv_silu(u):
        def step(act, S):
            act.wait_ge(S.conv_done, u + 1)
            act.activation(A.qkv[:, u, :], A.qkv[:, u, :], ACT.Silu)
        return step

    dve_steps = {8 + c: gated_convolution(c) for c in range(SCT)}
    dve_steps.update({12 + u: convolution(u) for u in range(3 * DH)})
    act_steps = {14 + u: conv_silu(u) for u in range(3 * DH)}
    project(nc, M, "proj2", mixer2_chunks(I.w_in_2[l]), tiles, None, gain=I.norm1_g_2[l], others=others, ahead=ahead,
            dve_steps=dve_steps, act_steps=act_steps)


def mixer2_norms(nc, M, A):
    with stage(nc, "norms2", "square_ready square_used summed root_ready inverse_ready spread scaled act_chain dve_chain "
               "exp_ready one_plus ln_ready") as (block, S):
        normed = [A.gate_c[:, c, :] for c in range(SCT)] + [A.qkv[:, u, :] for u in range(2 * DH)]

        @block.tensor
        def _(pe):
            def spread(g):
                pe.wait_ge(S.inverse_ready, g + 1)
                for u in range(4):
                    n = 4 * g + u
                    if n >= 4:
                        pe.wait_ge(S.scaled, n - 3)
                    pe.matmul(M.ps[:, 4 + u, :], M.spread_sel[:, u, :], A.inverse[:, g, :], start=True,
                              stop=True).then_inc(S.spread, 1)

            for g in range(3):
                for u in range(4):
                    pe.wait_ge(S.square_ready, 4 * g + u + 1)
                    pe.matmul(M.ps[:, g, :], M.sum_sel[:, 96 - 32 * u:224 - 32 * u], M.sq[:, u % 2, :], start=(u == 0),
                              stop=(u == 3)).then_inc(S.square_used, 1)
                if g >= 1:
                    spread(g - 1)
            spread(2)

        @block.scalar
        def _(act):
            def square(n):
                if n >= 2:
                    act.wait_ge(S.square_used, n - 1)
                act.activation(M.sq[:, n % 2, :], normed[n], ACT.Square).then_inc(S.square_ready, 1)

            for g in range(3):
                for u in range(4):
                    square(4 * g + u)
                if g == 2:
                    act.wait_ge(S.summed, 2)
                    act.activation(A.inverse[:, 1, :], A.inverse[:, 1, :], ACT.Sqrt).then_inc(S.root_ready, 1)
                if g != 1:
                    act.wait_ge(S.summed, g + 1)
                    act.activation(A.inverse[:, g, :], A.inverse[:, g, :], ACT.Sqrt).then_inc(S.root_ready, 1)
            link = chain(act, S.act_chain)
            act.wait_ge(S.one_plus, 1)
            act.activation(A.dt_e[:], A.dt_e[:], ACT.Exp, scale=-1.0).then_inc(S.exp_ready, 1)
            link(act.activation(A.a_neg[:], A.a_log[:], ACT.Exp))
            act.wait_ge(S.one_plus, 2)
            act.activation(A.dt_ln[:], A.dt_u[:], ACT.Ln).then_inc(S.ln_ready, 1)
            act.activation(A.beta[:], A.ba[:, :, 0:DH], ACT.Sigmoid)

        @block.vector
        def _(dve):
            link = chain(dve, S.dve_chain)
            link(dve.tensor_tensor(A.g[:], A.ba[:, :, DH:], A.dt_bias[:].unsqueeze(1).to_broadcast([P, TT, DH]), ALU.add))
            dve.scalar_tensor_tensor(out=A.dt_e[:], in0=A.g[:], scalar=-1.0, in1=A.g[:], op0=ALU.mult,
                                     op1=ALU.max).then_inc(S.one_plus, 1)

            affine = [(P * RMS_EPS, 1.0 / P), (RMS_EPS, float(DHD)), (RMS_EPS, 1.0)]

            def root(g):
                dve.wait_ge(S.square_used, 4 * (g + 1))
                dve.tensor_scalar(A.inverse[:, g, :], M.ps[:, g, :], affine[g][0], affine[g][1], ALU.add,
                                  ALU.mult).then_inc(S.summed, 1)

            def inverse(g):
                dve.wait_ge(S.root_ready, g + 1)
                dve.reciprocal(A.inverse[:, g, :], A.inverse[:, g, :]).then_inc(S.inverse_ready, 1)

            def scale(g):
                for u in range(4):
                    n = 4 * g + u
                    dve.wait_ge(S.spread, n + 1)
                    if g:
                        dve.tensor_tensor(normed[n], normed[n], M.ps[:, 4 + u, :], ALU.mult).then_inc(S.scaled, 1)
                    else:
                        dve.scalar_tensor_tensor(out=A.scT[:, u, :], in0=normed[n], scalar=A.sc_g[:, u:u + 1],
                                                 in1=M.ps[:, 4 + u, :], op0=ALU.mult, op1=ALU.mult).then_inc(S.scaled, 1)

            root(0)
            inverse(0)
            root(1)
            scale(0)
            root(2)
            inverse(1)
            inverse(2)
            scale(1)
            dve.wait_ge(S.exp_ready, 1)
            dve.tensor_scalar(A.dt_u[:], A.dt_e[:], 1.0, None, ALU.add).then_inc(S.one_plus, 1)
            dve.wait_ge(S.one_plus, 2)
            link(dve.scalar_tensor_tensor(out=A.dt_r[:], in0=A.dt_u[:], scalar=-1.0, in1=A.dt_e[:], op0=ALU.add,
                                          op1=ALU.subtract))
            link(dve.tensor_scalar(A.g[:], A.g[:], 0.0, None, ALU.max))
            link(dve.tensor_tensor(A.g[:], A.g[:], A.dt_r[:], ALU.subtract))
            scale(2)
            dve.wait_ge(S.ln_ready, 1)
            link(dve.tensor_tensor(A.g[:], A.g[:], A.dt_ln[:], ALU.add))
            dve.wait_ge(S.act_chain, 1)
            link(dve.scalar_tensor_tensor(out=A.g[:], in0=A.g[:], scalar=-1.0,
                                          in1=A.a_neg[:].unsqueeze(1).to_broadcast([P, TT, DH]),
                                          op0=ALU.mult, op1=ALU.mult))


def mixer2_delta(nc, M, A):
    with stage(nc, "delta", "sums chain gains gain_exp g_rows diff decay rows_exp q_scaled kk qk "
               "lt_ready qk_ready k_turned v_turned nat_ready masked t1 t1_copied x_up xy_ready u_ready w_ready u_copied w_copied "
               "ws v_new o o_copied s_add s_ready root_in root_ready prep_free") as (block, S):
        tri = M.tri[:, 3 * P:4 * P]
        head = lambda ap, h: ap[:, h * P:(h + 1) * P]
        heads = lambda ap: ap.rearrange("p (h c) -> p h c", h=DH)
        cols = lambda ap, i: ap[:, DH * i:DH * (i + 1)].unsqueeze(2).to_broadcast([P, DH, P])
        g_all = A.g[:].rearrange("p i h -> p (i h)")
        beta_all = A.beta[:].rearrange("p i h -> p (i h)")
        q, k, v = (A.qkv[:, DH * n:DH * (n + 1), :] for n in range(3))
        tok = lambda ap, h, i: ap[:, h, i * P:(i + 1) * P]
        X = k.rearrange("p h t -> p (h t)").rearrange("p (i n) -> p i n", i=TT)
        Y = v.rearrange("p h t -> p (h t)").rearrange("p (i n) -> p i n", i=TT)

        @block.tensor
        def _(pe):
            pe.matmul(M.ps[:, 7, 0:16], tri, g_all, start=True, stop=True)
            pe.matmul(M.ps[:, 7, 16:32], M.ones[:], g_all, start=True, stop=True).then_inc(S.sums, 1)
            for i in range(TT):
                if i >= 1:
                    pe.wait_ge(S.diff, i)
                for h in range(DH):
                    mm = pe.matmul(head(M.ps[:, 0], h), g_all[:, DH * i + h:DH * i + h + 1].to_broadcast([P, P]), tri,
                                   start=True, stop=True)
                mm.then_inc(S.g_rows, 1)
                if i >= 1:
                    pe.wait_ge(S.lt_ready, i)
                for h in range(DH):
                    pe.matmul(head(M.ps[:, 1], h), beta_all[:, DH * i + h:DH * i + h + 1].to_broadcast([P, P]), M.ident[:],
                              start=True, stop=True)
                for h in range(DH):
                    mm = pe.matmul(head(M.ps[:, 2], h), tok(k, h, i), tok(k, h, i), start=True, stop=True)
                mm.then_inc(S.kk, 1)
                if i >= 1:
                    pe.wait_ge(S.qk_ready, i)
                for h in range(DH):
                    mm = pe.matmul(head(M.ps[:, 3], h), tok(k, h, i), tok(q, h, i), start=True, stop=True)
                mm.then_inc(S.qk, 1)
                if i >= 1:
                    pe.wait_ge(S.nat_ready, i)
                for h in range(DH):
                    mm = pe.transpose(head(M.ps[:, 4], h), tok(k, h, i), M.ident[:])
                mm.then_inc(S.k_turned, 1)
                if i >= 1:
                    pe.wait_ge(S.prep_free, i)
                for h in range(DH):
                    mm = pe.transpose(head(M.ps[:, 5], h), tok(v, h, i), M.ident[:])
                mm.then_inc(S.v_turned, 1)
            pe.wait_ge(S.prep_free, TT)
            for n in range(LEVELS):
                for i in range(TT):
                    pe.wait_ge(S.masked, TT * n + i + 1)
                    if n:
                        pe.wait_ge(S.xy_ready, TT * (n - 1) + i + 1)
                    for h in range(DH):
                        mm = pe.matmul(head(M.ps[:, 2 * i], h), head(A.BT[:, i], h), head(X[:, i], h) if n else M.ident[:],
                                       start=True, stop=True)
                    mm.then_inc(S.t1, 1)
                for i in range(TT):
                    if n:
                        pe.wait_ge(S.t1_copied, TT * (n - 1) + i + 1)
                        if n < LEVELS - 1:
                            for h in range(DH):
                                pe.matmul(head(M.ps[:, 2 * i + 1], h), head(Y[:, i], h), head(A.T1[:, i], h), start=True,
                                          stop=True)
                        for h in range(DH):
                            mm = pe.matmul(head(M.ps[:, 2 * i], h), head(A.T1[:, i], h), head(Y[:, i], h), start=True,
                                           stop=True)
                        mm.then_inc(S.x_up, 1)
            for i in range(TT):
                pe.wait_ge(S.xy_ready, TT * (LEVELS - 1) + i + 1)
                for h in range(DH):
                    mm = pe.matmul(head(M.ps[:, 2 * i], h), head(Y[:, i], h), head(A.vb[:, i], h), start=True, stop=True)
                mm.then_inc(S.u_ready, 1)
                for h in range(DH):
                    mm = pe.matmul(head(M.ps[:, 2 * i + 1], h), head(A.kbg[:, i], h), head(Y[:, i], h), start=True, stop=True)
                mm.then_inc(S.w_ready, 1)
            pe.wait_ge(S.u_copied, TT)
            pe.wait_ge(S.w_copied, TT)
            for i in range(TT):
                if i:
                    pe.wait_ge(S.s_ready, i)
                    for h in range(DH):
                        mm = pe.matmul(head(M.ps[:, 0], h), head(A.wT[:, i], h), head(A.state, h), start=True, stop=True)
                    mm.then_inc(S.ws, 1)
                    pe.wait_ge(S.v_new, i)
                if i >= 2:
                    pe.wait_ge(S.o_copied, i - 1)
                vn = A.v_new if i else A.u[:, 0]
                for h in range(DH):
                    if i:
                        pe.matmul(head(M.ps[:, 1 + i % 2], h), tok(q, h, i), head(A.state, h), start=True, stop=False)
                    mm = pe.matmul(head(M.ps[:, 1 + i % 2], h), head(A.qk[:, i], h), head(vn, h), start=(i == 0), stop=True)
                mm.then_inc(S.o, 1)
                if i < TT - 1:
                    for h in range(DH):
                        mm = pe.matmul(head(M.ps[:, 3], h), head(A.kdec[:, i], h), head(vn, h), start=True, stop=True)
                    mm.then_inc(S.s_add, 1)

        @block.scalar
        def _(act):
            act.wait_ge(S.gains, 1)
            act.activation(A.gain[:], A.gain[:], ACT.Exp).then_inc(S.gain_exp, 1)
            for i in range(TT):
                act.wait_ge(S.g_rows, i + 1)
                act.activation(A.rows[:], M.ps[:, 0], ACT.Exp).then_inc(S.rows_exp, 1)
                act.wait_ge(S.diff, i + 1)
                act.activation(A.D[:, i], A.D[:, i], ACT.Exp).then_inc(S.decay, 1)
                act.wait_ge(S.q_scaled, i + 1)
            for n in range(1, LEVELS):
                for i in range(TT):
                    act.wait_ge(S.t1, TT * n + i + 1)
                    if n > 1:
                        act.wait_ge(S.x_up, TT * (n - 2) + i + 1)
                    act.copy(A.T1[:, i], M.ps[:, 2 * i]).then_inc(S.t1_copied, 1)
            for i in range(TT):
                act.wait_ge(S.w_ready, i + 1)
                act.copy(A.wT[:, i], M.ps[:, 2 * i + 1]).then_inc(S.w_copied, 1)
            act.wait_ge(S.root_in, 1)
            act.activation(A.root[:], A.root[:], ACT.Sqrt).then_inc(S.root_ready, 1)

        @block.vector
        def _(dve):
            link = chain(dve, S.chain)
            dve.wait_ge(S.sums, 1)
            link(dve.tensor_copy(A.G[:], M.ps[:, 7, 0:16]))
            link(dve.tensor_copy(A.gain[:, 0:16], M.ps[:, 7, 0:16]))
            link(dve.tensor_tensor(A.gain[:, 16:32], M.ps[:, 7, 16:32], A.G[:], ALU.subtract))
            dve.tensor_copy(A.gain[:, 32:48], M.ps[:, 7, 16:32]).then_inc(S.gains, 1)
            dve.wait_ge(S.gain_exp, 1)
            link(dve.tensor_tensor(A.bg[:], A.gain[:, 0:16], beta_all, ALU.mult))
            for i in range(TT):
                D, LT = A.D[:, i], A.LT[:, i]
                dve.wait_ge(S.rows_exp, i + 1)
                link(dve.tensor_tensor(heads(D), heads(M.ps[:, 0]), cols(A.G, i), ALU.subtract))
                dve.scalar_tensor_tensor(out=heads(D), in0=heads(D), scalar=0.0, in1=M.mask_neg[:].unsqueeze(1).to_broadcast(
                    [P, DH, P]), op0=ALU.min, op1=ALU.add).then_inc(S.diff, 1)
                dve.wait_ge(S.decay, i + 1)
                dve.wait_ge(S.kk, i + 1)
                link(dve.tensor_tensor(LT, M.ps[:, 2], D, ALU.mult))
                dve.tensor_tensor(LT, LT, M.ps[:, 1], ALU.mult).then_inc(S.lt_ready, 1)
                dve.wait_ge(S.qk, i + 1)
                dve.tensor_tensor(A.qk[:, i], M.ps[:, 3], D, ALU.mult).then_inc(S.qk_ready, 1)
                dve.tensor_tensor(q[:, :, i * P:(i + 1) * P], q[:, :, i * P:(i + 1) * P], heads(A.rows[:]), ALU.mult
                                  ).then_inc(S.q_scaled, 1)
                dve.wait_ge(S.k_turned, i + 1)
                dve.tensor_tensor(heads(A.kbg[:, i]), heads(M.ps[:, 4]), cols(A.bg, i), ALU.mult)
                dve.tensor_tensor(heads(A.kdec[:, i]), heads(M.ps[:, 4]), cols(A.gain[:, 16:32], i), ALU.mult
                                  ).then_inc(S.nat_ready, 1)
                dve.wait_ge(S.v_turned, i + 1)
                dve.tensor_tensor(heads(A.vb[:, i]), heads(M.ps[:, 5]), cols(beta_all, i), ALU.mult).then_inc(S.prep_free, 1)
            dve.wait_ge(S.prep_free, TT)
            dve.wait_ge(S.lt_ready, TT)
            for n in range(LEVELS):
                mask = M.levels[:, n, :].unsqueeze(1).to_broadcast([P, DH, P])
                eye = M.ident[:].unsqueeze(1).to_broadcast([P, DH, P])
                for i in range(TT):
                    if n:
                        dve.wait_ge(S.t1, TT * (n - 1) + i + 1)
                    dve.tensor_tensor(heads(A.BT[:, i]), heads(A.LT[:, i]), mask, ALU.mult).then_inc(S.masked, 1)
                    if n == 0:
                        dve.wait_ge(S.masked, i + 1)
                        link(dve.tensor_tensor(heads(Y[:, i]), eye, heads(A.BT[:, i]), ALU.subtract))
                for i in range(TT):
                    if n == 0:
                        dve.wait_ge(S.t1, i + 1)
                        dve.tensor_tensor(heads(X[:, i]), eye, heads(M.ps[:, 2 * i]), ALU.subtract).then_inc(S.xy_ready, 1)
                    else:
                        dve.wait_ge(S.xy_ready, TT * (n - 1) + i + 1)
                        dve.wait_ge(S.x_up, TT * (n - 1) + i + 1)
                        if n < LEVELS - 1:
                            dve.tensor_tensor(X[:, i], X[:, i], M.ps[:, 2 * i + 1], ALU.subtract)
                        dve.tensor_tensor(Y[:, i], Y[:, i], M.ps[:, 2 * i], ALU.subtract).then_inc(S.xy_ready, 1)
            for i in range(TT):
                dve.wait_ge(S.u_ready, i + 1)
                dve.tensor_copy(A.u[:, i], M.ps[:, 2 * i]).then_inc(S.u_copied, 1)

            def output(i):
                dve.wait_ge(S.o, i + 1)
                dve.tensor_copy(A.mix[:, i, :], M.ps[:, 1 + i % 2]).then_inc(S.o_copied, 1)

            state, vn = heads(A.state[:]), A.v_new[:]
            for i in range(TT):
                if i:
                    dve.wait_ge(S.ws, i)
                    dve.tensor_tensor(vn, A.u[:, i], M.ps[:, 0], ALU.subtract).then_inc(S.v_new, 1)
                if i < TT - 1:
                    dve.wait_ge(S.s_add, i + 1)
                    if i:
                        dve.wait_ge(S.o, i + 1)
                        dve.wait_ge(S.s_ready, i)
                        link(dve.tensor_tensor(state, state, cols(A.gain[:, 32:48], i), ALU.mult))
                        dve.tensor_tensor(A.state[:], A.state[:], M.ps[:, 3], ALU.add).then_inc(S.s_ready, 1)
                    else:
                        dve.tensor_copy(A.state[:], M.ps[:, 3]).then_inc(S.s_ready, 1)
                output(i)
            dve.wait_ge(S.o_copied, TT)
            o = A.mix[:].rearrange("p i (h d) -> p (i h) d", h=DH)
            sq = A.BT[:].rearrange("p i (h d) -> p (i h) d", h=DH)
            link(dve.tensor_tensor(sq, o, o, ALU.mult))
            link(dve.tensor_reduce(A.root[:], sq, AX.X, ALU.add))
            dve.tensor_scalar(A.root[:], A.root[:], 1.0 / DHD, RMS_EPS, ALU.mult, ALU.add).then_inc(S.root_in, 1)
            link(dve.tensor_tensor(o, o, A.silz[:].rearrange("p i (h d) -> p (i h) d", h=DH), ALU.mult))
            link(dve.tensor_tensor(o, o, A.norm_g[:].unsqueeze(1).to_broadcast([P, TT * DH, DHD]), ALU.mult))
            dve.wait_ge(S.root_ready, 1)
            link(dve.reciprocal(A.root[:], A.root[:]))
            link(dve.tensor_tensor(o, o, A.root[:].unsqueeze(2).to_broadcast([P, TT * DH, DHD]), ALU.mult))


def mixer2(nc, M, I, l, ahead):
    with ExitStack() as memory:
        sb = tensors(nc, memory, "b_")
        A = Memory()
        A.qkv, A.silz, A.mix, A.scT = sb("qkv", 3 * DH, T), sb("silz", TT, DW), sb("mix", TT, DW), sb("scT", SCT, T)
        A.g, A.beta, A.norm_g = sb("g", TT, DH), sb("beta", TT, DH), sb("norm_g", DHD)
        with ExitStack() as inner:
            sb = tensors(nc, inner, "b_")
            A.raw, A.prod, A.gate_c = sb("raw", 3 * DH, T + DCONV - 1), sb("prod", SCT, T + SCCONV - 1), sb("gate_c", SCT, T)
            A.gate_b = A.scT
            A.ba = sb("ba", TT, 2 * DH)
            A.conv_w, A.sc_w, A.sc_g = sb("conv_w", DCONV, 3 * DH), sb("sc_w", SCCONV, SCT), sb("sc_g", SCT)
            A.dt_bias, A.a_log = sb("dt_bias", DH), sb("a_log", DH)
            out_ahead = chunks_ahead(nc, M, "out2", out_chunks(I.w_out_2[l]))
            mixer2_project(nc, M, A, I, l, out_ahead)
            A.inverse, A.a_neg = sb("inverse", 3, T), sb("a_neg", DH)
            A.dt_e, A.dt_u, A.dt_r, A.dt_ln = (sb(f"dt_{x}", TT, DH) for x in "eurl")
            mixer2_norms(nc, M, A)
        with ExitStack() as inner:
            sb = tensors(nc, inner, "b_")
            A.D, A.LT, A.T1 = sb("D", TT, DW), sb("LT", TT, DW), sb("T1", TT, DW)
            A.qk, A.kdec, A.kbg, A.vb = sb("qk", TT, DW), sb("kdec", TT, DW), sb("kbg", TT, DW), sb("vb", TT, DW)
            A.rows, A.state, A.v_new = sb("rows", DW), sb("state", DW), sb("v_new", DW)
            A.G, A.gain, A.bg, A.root = sb("G", 16), sb("gain", 48), sb("bg", 16), sb("root", 16)
            A.BT, A.u, A.wT = A.D, A.D, A.LT
            mixer2_delta(nc, M, A)
        mix_out(nc, M, "out2", A.mix, A.scT, I.w_out_2[l], None, out_ahead, ahead)


def finish(nc, M, I, out):
    with ExitStack() as memory, stage(nc, "finish", "h_ready turned copied stored" + GAIN_SIGNALS) as (block, S):
        sb = tensors(nc, memory, "f_")
        h, rows = sb("h", DT, T), sb("rows", TT, D)

        @block.tensor
        def _(pe):
            pe.wait_ge(S.h_ready, DT)
            for n in range(2 * TT):
                i, half = n // 2, n % 2
                for d in range(4):
                    mm = pe.transpose(M.ps[:, n, d * P:(d + 1) * P], h[:, 4 * half + d, i * P:(i + 1) * P], M.ident[:])
                mm.then_inc(S.turned, 1)

        @block.vector
        def _(dve):
            dve.wait_ge(S.gain_landed, 16)
            for d in range(DT):
                rms_value(dve, M, d, h[:, d, :]).then_inc(S.h_ready, 1)
            for n in range(2 * TT):
                dve.wait_ge(S.turned, n + 1)
                dve.tensor_copy(rows[:, n // 2, 512 * (n % 2):512 * (n % 2 + 1)], M.ps[:, n, :]).then_inc(S.copied, 1)

        @block.sync
        def _(sp):
            rms_sp(sp, nc, M, S, I.final_norm_g_2)
            for i in range(TT):
                sp.wait_ge(S.copied, 2 * i + 2)
                sp.dma_start(out[0, i * P:(i + 1) * P, :], rows[:, i, :]).then_inc(S.stored, 16)
            sp.wait_ge(S.stored, 16 * TT)


def ada_columns(w, subs):
    return w.rearrange("(k p) n -> p k n", p=P)[:, :, 3 * D * subs[0]:3 * D * (subs[-1] + 1)]


def first_stack_layer(nc, M, I, l):
    after = 1 - l
    vectors = (M.columns[:, bass.ds(l, 1), :].rearrange("p a t -> p (a t)"),
               M.columns[:, bass.ds(after, 1), 0:3 * DT].rearrange("p a t -> p (a t)"))
    mixer_ahead = chunks_ahead(nc, M, "mixer1", mixer1_chunks(I.w_in[l]))
    ffn(nc, M, "ffn0", I.ffn_w1[l, 0], I.ffn_w3[l, 0], I.ffn_w2[l, 0], 0, vectors=vectors, ahead=mixer_ahead,
        ada=([1, 2], ada_columns(I.ada_w[l], [1, 2]), M.pcol[:, 24:72]))
    last_ahead = ffn_ahead(nc, M, "ffn2", I.ffn_w1[l, 1], I.ffn_w3[l, 1])
    mixer1(nc, M, I, l, mixer_ahead, last_ahead)
    ffn(nc, M, "ffn2", I.ffn_w1[l, 1], I.ffn_w3[l, 1], I.ffn_w2[l, 1], 2, mine=last_ahead,
        ada=([0], ada_columns(I.ada_w[after], [0]), M.bnext[:]))


def program(nc, I, out):
    with ExitStack() as memory:
        sb = tensors(nc, memory, "m_")
        M = Memory()
        M.x = sb("x", DT, T)
        M.ident, M.tri, M.ones, M.mean_d = sb("ident", P), sb("tri", T + 3 * P), sb("ones", P), sb("mean_d", P)
        M.sq, M.rstd = sb("sq", 2, T), sb("rstd", T)
        M.raw = sb("raw", 2, 2 * D)
        M.ps = memory.enter_context(nc.psum_tensor("m_ps", [P, 8, T], F32))
        with ExitStack() as inner:
            sb = tensors(nc, inner, "m_")
            M.ccol, M.columns, M.pcol, M.bnext, M.mod = sb("ccol", DT), sb("columns", DEPTH, 120), sb("pcol", 120), sb("bnext", 3 * DT), sb("mod", 72)
            M.part = sb("part", 2, 2 * P)
            M.tape_dram = nc.dram_tensor("bias_tape", [HEADS, T + P], F32, kind="Internal").ap()
            M.bias_dram = nc.dram_tensor("bias_windows", [P, HEADS, T], F32, kind="Internal").ap()
            setup(nc, M, I)
            with nc.Fori(0, DEPTH) as l:
                first_stack_layer(nc, M, I, l)
        sb = tensors(nc, memory, "m_")
        M.gain = sb("gain", DT)
        M.sum_sel, M.spread_sel = sb("sum_sel", 7 * 32), sb("spread_sel", 4, P)
        M.levels, M.mask_neg = sb("levels", LEVELS, P), sb("mask_neg", P)
        first_root(nc, M)
        with stage(nc, "consts2", "landed") as (block, S):
            @block.sync
            def _(sp):
                for dst, value in ((M.sum_sel, sum_selectors()), (M.spread_sel, spread_selectors()),
                                   (M.levels, level_masks()), (M.mask_neg, (triangle()[:, 3 * P:4 * P] - 1) * 1e30)):
                    sp.dma_start(dst[:], nc.inline_tensor(value.astype(np.float32), name="c_" + dst.name).ap()).then_inc(S.landed, 16)
                sp.wait_ge(S.landed, 64)
        with nc.Fori(0, DEPTH) as l:
            last_ahead = ffn_ahead(nc, M, "ffn3", I.ffn_w_gate_2[l], I.ffn_w_up_2[l])
            mixer2(nc, M, I, l, last_ahead)
            ffn(nc, M, "ffn3", I.ffn_w_gate_2[l], I.ffn_w_up_2[l], I.ffn_w_down_2[l], None, gain=I.norm2_g_2[l],
                mine=last_ahead)
        finish(nc, M, I, out)


_NAMES = ["x", "c", "rel_bias", "ada_w", "ada_b", "ln_g", "ln_b", "ffn_w1", "ffn_w3", "ffn_w2", "w_in", "w_out",
          "cmp_pe", "cmp_w1", "cmp_b1", "cmp_w2", "gmlp_ln_g", "gmlp_ln_b", "gmlp_ws", "gmlp_bs", "ssm_conv_w",
          "ssm_conv_b", "ssm_dt_bias", "ssm_a_log", "ssm_d", "ssm_norm_g", "norm1_g_2", "w_in_2", "dn_conv_w_2",
          "dn_a_log_2", "dn_dt_bias_2", "dn_norm_g_2", "sc_conv_w_2", "sc_norm_g_2", "w_out_2", "norm2_g_2",
          "ffn_w_gate_2", "ffn_w_up_2", "ffn_w_down_2", "final_norm_g_2"]


def kernel(**inputs):
    import concourse.bacc as bacc
    from concourse.bass_utils import run_bass_kernel_spmd

    nc = bacc.Bacc("TRN2", target_bir_lowering=False, num_devices=1)
    arrays, aps = {}, {}
    for name in _NAMES:
        a = np.ascontiguousarray(inputs[name])
        arrays[f"in_{name}"] = a
        aps[name] = nc.dram_tensor(f"in_{name}", a.shape, mybir.dt.from_np(a.dtype), kind="ExternalInput").ap()
    out = nc.dram_tensor("out", (1, T, D), F32, kind="ExternalOutput").ap()
    program(nc, namedtuple("Inputs", _NAMES)(**aps), out)
    return run_bass_kernel_spmd(nc, [arrays], core_ids=[0]).results[0]["out"]
```
